# Optimizing a Trainium2 kernel written in Bass

```python
import math
import jax, jax.numpy as jnp
from jax import lax
import numpy as np

D_MODEL = 1024
BATCH = 1
SEQ = 512
DEPTH = 2

N_A_LAYERS = DEPTH // 2
N_B_LAYERS = DEPTH - N_A_LAYERS
CONV_WIDTH = 31
FOX_HEADS = 16
FOX_HEAD_DIM = D_MODEL // FOX_HEADS
MEM_LEN = 256
MEM_HEADS = 4
MEM_HEAD_DIM = D_MODEL // MEM_HEADS
D_FF = 4 * D_MODEL
Q_BLOCK = 128
RMS_EPS = 1e-6
LN_EPS = 1e-5


def rmsnorm(x, g):
    xf = x.astype(jnp.float32)
    y = xf * lax.rsqrt(jnp.mean(xf * xf, axis=-1, keepdims=True) + RMS_EPS)
    return (y * g.astype(jnp.float32)).astype(x.dtype)

def layernorm(x, g, b):
    xf = x.astype(jnp.float32)
    mu = jnp.mean(xf, axis=-1, keepdims=True)
    var = jnp.mean(jnp.square(xf - mu), axis=-1, keepdims=True)
    y = (xf - mu) * lax.rsqrt(var + LN_EPS)
    return (y * g.astype(jnp.float32) + b.astype(jnp.float32)).astype(x.dtype)

def conformer_conv(h, w_pw1, b_pw1, w_dw, b_dw, ln_g, ln_b, w_pw2, b_pw2):
    u = h @ w_pw1 + b_pw1
    a, gate = jnp.split(u, 2, axis=-1)
    u = a * jax.nn.sigmoid(gate)
    u = lax.conv_general_dilated(
        u, w_dw[:, None, :].astype(u.dtype),
        window_strides=(1,), padding=[(CONV_WIDTH - 1, 0)],
        dimension_numbers=("NWC", "WIO", "NWC"),
        feature_group_count=D_MODEL) + b_dw
    u = jax.nn.silu(layernorm(u, ln_g, ln_b))
    return u @ w_pw2 + b_pw2

def fox_attention(h, w_q, w_o, k, v, c_bhs):
    B, S, _ = h.shape
    nb = S // Q_BLOCK
    q = (h @ w_q).reshape(B, nb, Q_BLOCK, FOX_HEADS, FOX_HEAD_DIM).transpose(1, 0, 2, 3, 4)
    c_q = c_bhs.reshape(B, FOX_HEADS, nb, Q_BLOCK).transpose(2, 0, 1, 3)
    key_pos = jnp.arange(S)
    scale = 1.0 / math.sqrt(FOX_HEAD_DIM)

    def block(args):
        qi, ci, i = args
        s = jnp.einsum("bqhd,bkhd->bhqk", qi, k).astype(jnp.float32) * scale
        s = s + (ci[..., :, None] - c_bhs[:, :, None, :])
        q_pos = i * Q_BLOCK + jnp.arange(Q_BLOCK)
        mask = key_pos[None, :] <= q_pos[:, None]
        s = jnp.where(mask[None, None], s, -jnp.inf)
        p = jax.nn.softmax(s, axis=-1)
        return jnp.einsum("bhqk,bkhd->bqhd", p.astype(v.dtype), v)

    out = lax.map(block, (q, c_q, jnp.arange(nb)))
    out = out.transpose(1, 0, 2, 3, 4).reshape(B, S, D_MODEL)
    return out @ w_o

def memory_cross_attention(h, mem_n, w_q, w_k, w_v, w_o):
    B, S, _ = h.shape
    q = (h @ w_q).reshape(B, S, MEM_HEADS, MEM_HEAD_DIM)
    k = (mem_n @ w_k).reshape(B, MEM_LEN, MEM_HEADS, MEM_HEAD_DIM)
    v = (mem_n @ w_v).reshape(B, MEM_LEN, MEM_HEADS, MEM_HEAD_DIM)
    s = jnp.einsum("bshd,bmhd->bhsm", q, k).astype(jnp.float32) / math.sqrt(MEM_HEAD_DIM)
    p = jax.nn.softmax(s, axis=-1)
    o = jnp.einsum("bhsm,bmhd->bshd", p.astype(v.dtype), v).reshape(B, S, D_MODEL)
    return o @ w_o

def sqrelu_mlp(h, w1, w2):
    return jnp.square(jax.nn.relu(h @ w1)) @ w2

def first_inputs(seed: int = 0) -> dict:
    key = jax.random.key(seed)
    ks = iter(jax.random.split(key, 40))

    def nrm(shape, scale):
        return jax.random.normal(next(ks), shape, jnp.float32) * scale

    def gain(shape):
        return 1.0 + nrm(shape, 0.05)

    D = D_MODEL
    return {
        "x": nrm((BATCH, SEQ, D), 1.0),
        "mem": nrm((BATCH, MEM_LEN, D), 1.0),
        "norm_mix_g": gain((DEPTH, D)),
        "norm_mem_g": gain((DEPTH, D)),
        "norm_memsrc_g": gain((DEPTH, D)),
        "norm_ff_g": gain((DEPTH, D)),
        "mem_wq": nrm((DEPTH, D, D), D ** -0.5),
        "mem_wk": nrm((DEPTH, D, D), D ** -0.5),
        "mem_wv": nrm((DEPTH, D, D), D ** -0.5),
        "mem_wo": nrm((DEPTH, D, D), 0.5 * D ** -0.5),
        "ff_w1": nrm((DEPTH, D, D_FF), D ** -0.5),
        "ff_w2": nrm((DEPTH, D_FF, D), 0.5 * D_FF ** -0.5),
        "conv_pw1_w": nrm((N_A_LAYERS, D, 2 * D), D ** -0.5),
        "conv_pw1_b": nrm((N_A_LAYERS, 2 * D), 0.02),
        "conv_dw_w": nrm((N_A_LAYERS, CONV_WIDTH, D), CONV_WIDTH ** -0.5),
        "conv_dw_b": nrm((N_A_LAYERS, D), 0.02),
        "conv_ln_g": gain((N_A_LAYERS, D)),
        "conv_ln_b": nrm((N_A_LAYERS, D), 0.02),
        "conv_pw2_w": nrm((N_A_LAYERS, D, D), 0.5 * D ** -0.5),
        "conv_pw2_b": nrm((N_A_LAYERS, D), 0.02),
        "kv_norm_g": gain((D,)),
        "kvf_w": nrm((D, 2 * D + FOX_HEADS), D ** -0.5),
        "fgate_b": 3.0 + nrm((FOX_HEADS,), 0.5),
        "fox_wq": nrm((N_B_LAYERS, D, D), D ** -0.5),
        "fox_wo": nrm((N_B_LAYERS, D, D), 0.5 * D ** -0.5),
        "final_norm_g": gain((D,)),
    }

def first_block(x, mem, norm_mix_g, norm_mem_g, norm_memsrc_g, norm_ff_g,
              mem_wq, mem_wk, mem_wv, mem_wo, ff_w1, ff_w2,
              conv_pw1_w, conv_pw1_b, conv_dw_w, conv_dw_b, conv_ln_g, conv_ln_b,
              conv_pw2_w, conv_pw2_b,
              kv_norm_g, kvf_w, fgate_b, fox_wq, fox_wo, final_norm_g):
    B, S, D = x.shape
    k = v = c_bhs = None
    for l in range(DEPTH):
        if l == N_A_LAYERS:
            hk = rmsnorm(x, kv_norm_g)
            kvf = hk @ kvf_w
            k = kvf[..., :D].reshape(B, S, FOX_HEADS, FOX_HEAD_DIM)
            v = kvf[..., D:2 * D].reshape(B, S, FOX_HEADS, FOX_HEAD_DIM)
            log_f = jax.nn.log_sigmoid((kvf[..., 2 * D:] + fgate_b).astype(jnp.float32))
            c_bhs = jnp.cumsum(log_f, axis=1).transpose(0, 2, 1)
        h = rmsnorm(x, norm_mix_g[l])
        if l < N_A_LAYERS:
            a = l
            x = x + conformer_conv(h, conv_pw1_w[a], conv_pw1_b[a], conv_dw_w[a], conv_dw_b[a],
                                   conv_ln_g[a], conv_ln_b[a], conv_pw2_w[a], conv_pw2_b[a])
        else:
            bl = l - N_A_LAYERS
            x = x + fox_attention(h, fox_wq[bl], fox_wo[bl], k, v, c_bhs)
        h = rmsnorm(x, norm_mem_g[l])
        mem_n = rmsnorm(mem, norm_memsrc_g[l])
        x = x + memory_cross_attention(h, mem_n, mem_wq[l], mem_wk[l], mem_wv[l], mem_wo[l])
        h = rmsnorm(x, norm_ff_g[l])
        x = x + sqrelu_mlp(h, ff_w1[l], ff_w2[l])
    return rmsnorm(x, final_norm_g)


N_MIXERS = 2
N_HEADS = 16
HEAD_DIM = D_MODEL // N_HEADS
CONV_WIDTH_2 = 3
BRANCHES = ((128, 1), (512, 4), (2048, 16))
NUM_BUCKETS = 32
MAX_DISTANCE = 2048
D_FF_2 = ((8 * D_MODEL // 3 + 255) // 256) * 256
EPS = 1e-6
NEG_INF = -1e30


def rms_norm(x, g):
    xf = x.astype(jnp.float32)
    y = xf * lax.rsqrt(jnp.mean(xf * xf, axis=-1, keepdims=True) + EPS)
    return (y * g.astype(jnp.float32)).astype(x.dtype)

def t5_bucket(dist):
    exact = NUM_BUCKETS // 2
    df = jnp.maximum(dist, 1).astype(jnp.float32)
    large = exact + (jnp.log(df / exact) / math.log(MAX_DISTANCE / exact)
                     * (NUM_BUCKETS - exact)).astype(jnp.int32)
    large = jnp.minimum(large, NUM_BUCKETS - 1)
    return jnp.where(dist < exact, dist, large)

def short_conv_mixer(h, w_in, conv_k, w_out):
    b, c, u = jnp.split(h @ w_in, 3, axis=-1)
    y = lax.conv_general_dilated(
        c * u, conv_k[:, None, :].astype(u.dtype),
        window_strides=(1,), padding=[(CONV_WIDTH_2 - 1, 0)],
        dimension_numbers=("NWC", "WIO", "NWC"),
        feature_group_count=D_MODEL)
    return (b * y) @ w_out

def dilated_branch(q, k, v, rel_bias, window, dilation):
    bsz, seq, nh, dh = q.shape
    blk = window // dilation
    L = seq // dilation
    nb = -(-L // blk)
    Lp = nb * blk

    def sub(t):
        t = t.reshape(bsz, L, dilation, nh, dh).transpose(0, 2, 1, 3, 4)
        t = jnp.pad(t, ((0, 0), (0, 0), (0, Lp - L), (0, 0), (0, 0)))
        return t.reshape(bsz, dilation, nb, blk, nh, dh)

    def with_prev(t):
        prev = jnp.pad(t, ((0, 0), (0, 0), (1, 0), (0, 0), (0, 0), (0, 0)))[:, :, :-1]
        return jnp.concatenate([prev, t], axis=3)

    qb = sub(q)
    kk = with_prev(sub(k))
    vv = with_prev(sub(v))

    s = jnp.einsum("brnqhd,brnkhd->brnhqk", qb, kk,
                   preferred_element_type=jnp.float32) * (HEAD_DIM ** -0.5)
    qi = jnp.arange(blk)[:, None]
    ki = jnp.arange(2 * blk)[None, :]
    rel = qi + blk - ki
    band = (rel >= 0) & (rel <= blk)
    valid_start = (jnp.arange(nb)[:, None, None] > 0) | (ki >= blk)[None]
    mask = band[None] & valid_start
    bias = rel_bias[t5_bucket(jnp.clip(rel, 0) * dilation)]
    s = s + bias.transpose(2, 0, 1).astype(jnp.float32)
    s = jnp.where(mask[:, None], s, NEG_INF)
    lse = jax.nn.logsumexp(s, axis=-1)
    p = jnp.exp(s - lse[..., None])
    o = jnp.einsum("brnhqk,brnkhd->brnqhd", p.astype(v.dtype), vv,
                   preferred_element_type=jnp.float32)

    o = o.reshape(bsz, dilation, Lp, nh, dh)[:, :, :L]
    o = o.transpose(0, 2, 1, 3, 4).reshape(bsz, seq, nh, dh)
    lse = lse.transpose(0, 1, 2, 4, 3).reshape(bsz, dilation, Lp, nh)[:, :, :L]
    lse = lse.transpose(0, 2, 1, 3).reshape(bsz, seq, nh)
    return o, lse

def dilated_attention_mixer(h, w_qkv, w_out, rel_bias):
    bsz, seq, _ = h.shape
    qkv = (h @ w_qkv).reshape(bsz, seq, 3, N_HEADS, HEAD_DIM)
    q, k, v = qkv[:, :, 0], qkv[:, :, 1], qkv[:, :, 2]
    outs, lses = [], []
    for window, dilation in BRANCHES:
        o, l = dilated_branch(q, k, v, rel_bias, window, dilation)
        outs.append(o)
        lses.append(l)
    alpha = jax.nn.softmax(jnp.stack(lses, axis=0), axis=0)
    o = jnp.sum(alpha[..., None] * jnp.stack(outs, axis=0), axis=0)
    return o.reshape(bsz, seq, D_MODEL).astype(h.dtype) @ w_out

def swiglu(h, w_gate, w_up, w_down):
    return (jax.nn.silu(h @ w_gate) * (h @ w_up)) @ w_down

def second_inputs(seed: int = 0) -> dict:
    key = jax.random.key(seed)
    ks = jax.random.split(key, 14)
    n_conv = (DEPTH + 1) // 2
    n_attn = DEPTH // 2
    f32 = jnp.float32
    nrm = lambda k, shape, scale: jax.random.normal(k, shape, f32) * scale
    return {
        "x": nrm(ks[0], (BATCH, SEQ, D_MODEL), 1.0),
        "mix_norm": 1.0 + nrm(ks[1], (DEPTH, D_MODEL), 0.05),
        "ffn_norm": 1.0 + nrm(ks[2], (DEPTH, D_MODEL), 0.05),
        "final_norm": 1.0 + nrm(ks[3], (D_MODEL,), 0.05),
        "conv_w_in": nrm(ks[4], (n_conv, D_MODEL, 3 * D_MODEL), D_MODEL ** -0.5),
        "conv_kernel": nrm(ks[5], (n_conv, CONV_WIDTH_2, D_MODEL), CONV_WIDTH_2 ** -0.5),
        "conv_w_out": nrm(ks[6], (n_conv, D_MODEL, D_MODEL), D_MODEL ** -0.5),
        "attn_w_qkv": nrm(ks[7], (n_attn, D_MODEL, 3 * D_MODEL), D_MODEL ** -0.5),
        "attn_w_out": nrm(ks[8], (n_attn, D_MODEL, D_MODEL), D_MODEL ** -0.5),
        "rel_bias": nrm(ks[9], (NUM_BUCKETS, N_HEADS), 0.2),
        "ffn_w_gate": nrm(ks[10], (DEPTH, D_MODEL, D_FF_2), D_MODEL ** -0.5),
        "ffn_w_up": nrm(ks[11], (DEPTH, D_MODEL, D_FF_2), D_MODEL ** -0.5),
        "ffn_w_down": nrm(ks[12], (DEPTH, D_FF_2, D_MODEL), D_FF_2 ** -0.5),
    }

def second_block(x, mix_norm, ffn_norm, final_norm, conv_w_in, conv_kernel, conv_w_out,
              attn_w_qkv, attn_w_out, rel_bias, ffn_w_gate, ffn_w_up, ffn_w_down):
    for i in range(DEPTH):
        h = rms_norm(x, mix_norm[i])
        j = i // N_MIXERS
        if i % N_MIXERS == 0:
            x = x + short_conv_mixer(h, conv_w_in[j], conv_kernel[j], conv_w_out[j])
        else:
            x = x + dilated_attention_mixer(h, attn_w_qkv[j], attn_w_out[j], rel_bias)
        h = rms_norm(x, ffn_norm[i])
        x = x + swiglu(h, ffn_w_gate[i], ffn_w_up[i], ffn_w_down[i])
    return rms_norm(x, final_norm)


def setup_inputs(seed=0):
    out = dict(first_inputs(seed))
    for name, value in second_inputs(seed + 1).items():
        if name != "x":
            out[name + "_2"] = value
    return out


def reference(
    x, mem, norm_mix_g, norm_mem_g, norm_memsrc_g, norm_ff_g, mem_wq, mem_wk, mem_wv, mem_wo,
    ff_w1, ff_w2, conv_pw1_w, conv_pw1_b, conv_dw_w, conv_dw_b, conv_ln_g, conv_ln_b,
    conv_pw2_w, conv_pw2_b, kv_norm_g, kvf_w, fgate_b, fox_wq, fox_wo, final_norm_g, mix_norm_2,
    ffn_norm_2, final_norm_2, conv_w_in_2, conv_kernel_2, conv_w_out_2, attn_w_qkv_2,
    attn_w_out_2, rel_bias_2, ffn_w_gate_2, ffn_w_up_2, ffn_w_down_2,
):
    x = first_block(
        x, mem, norm_mix_g, norm_mem_g, norm_memsrc_g, norm_ff_g, mem_wq, mem_wk, mem_wv,
        mem_wo, ff_w1, ff_w2, conv_pw1_w, conv_pw1_b, conv_dw_w, conv_dw_b, conv_ln_g,
        conv_ln_b, conv_pw2_w, conv_pw2_b, kv_norm_g, kvf_w, fgate_b, fox_wq, fox_wo,
        final_norm_g,
    )
    return second_block(
        x, mix_norm_2, ffn_norm_2, final_norm_2, conv_w_in_2, conv_kernel_2, conv_w_out_2,
        attn_w_qkv_2, attn_w_out_2, rel_bias_2, ffn_w_gate_2, ffn_w_up_2, ffn_w_down_2,
    )


_drawn_inputs = setup_inputs


def setup_inputs(seed=0):
    import zlib

    import numpy as np

    out = dict(_drawn_inputs(seed))
    spreads = {}
    factors = {'norm_mem_g': 8.0,
     'norm_memsrc_g': 6.78,
     'conv_pw1_b': 4.607,
     'conv_ln_b': 5.295,
     'kv_norm_g': 3.771,
     'rel_bias_2': 3.053}
    for name, (base, spread) in spreads.items():
        noise = np.random.default_rng([zlib.crc32(name.encode()), seed]).standard_normal(out[name].shape)
        drawn = base * np.exp(spread * noise) if base else spread * noise
        out[name] = __import__('jax').numpy.asarray(drawn.astype(out[name].dtype))
    for name, factor in factors.items():
        out[name] = (out[name] * factor).astype(out[name].dtype)
    return out
```

```python
from contextlib import ExitStack, contextmanager

import numpy as np

import concourse.bass as bass
from concourse import mybir

P = 128
F32 = mybir.dt.float32
F32R = mybir.dt.float32r
ALU = mybir.AluOpType
ACT = mybir.ActivationFunctionType
AX_X = mybir.AxisListType.X

D = 1024
S = 512
DC = D // P
TB = S // P
MEM = 256
MB = MEM // P
D_FF = 4 * D
D_FF2 = 2816
TAPS = 31
PAD = TAPS - 1
HEADS, HEAD_DIM = 16, 64
MEM_HEADS, MEM_HEAD_DIM = 4, 256
BUCKETS, MAX_DISTANCE = 32, 2048
BRANCHES = ((128, 1), (512, 4), (2048, 16))
RMS_EPS, LN_EPS = 1e-6, 1e-5
MASKED = -1e30

SLOTS = 4
COLS = 512
GCOLS = 640
SBUF_BASE = 16640

GROUP = {
    "relu2": dict(psum_read=2, t_ready=2, part_hi=2, part_lo=2),
    "gate": dict(psum_read=2, gated=1, t_ready=1, part_hi=1, part_lo=1),
    "glu": dict(psum_read=2, gated=1, t_ready=1),
    "cu": dict(psum_read=2, step=4),
    "bmul": dict(psum_read=2, t_ready=2, part_hi=2, part_lo=2),
    "proj": dict(psum_read=2, part_hi=2, part_lo=2),
    "add": dict(psum_read=2),
}
STATS = dict(pe_side=1, act_side=1, rstd_ready=1)
MEM_TURN = dict(act_side=3, step=3, pe_side=4, part_hi=4, part_lo=4)
LN_MEAN, LN_CENTRE, LN_SQUARES, LN_SCALE = 7, 1 + 4, 7, 4
LAYER_NORM = dict(pe_side=2, act_side=1, rstd_ready=1, step=LN_MEAN + LN_CENTRE + LN_SQUARES + LN_SCALE,
                  squared=4, gated=4, part_hi=4, part_lo=4)
GATES = dict(act_side=1 + 3, step=2 + 4, pe_side=1)
COLUMNS = dict(pe_side=1, step=1)
FINAL_NORM = dict(pe_side=1, act_side=1, rstd_ready=1, step=4)
PROLOGUE = dict(pe_side=2 + DC, psum_read=4, step=3)


def prep_counts(first, n, split=True, squares=True):
    c = {}
    if split:
        c.update(part_hi=n, part_lo=n)
    if squares:
        c.update(squared=n, step=sum(1 if p == 0 else 2 for p in range(first, first + n)))
    return c


VECTORS = {}


def vector_rows():
    rows, at = [], 0
    for name, n in (("norm_mix_g", 16), ("norm_mem_g", 16), ("norm_memsrc_g", 16), ("norm_ff_g", 16),
                    ("kv_norm_g", 8), ("final_norm_g", 8), ("mix_norm_2", 16), ("ffn_norm_2", 16),
                    ("final_norm_2", 8),
                    ("conv_pw1_b", 16), ("conv_dw_b", 8), ("conv_ln_g", 8), ("conv_ln_b", 8),
                    ("conv_pw2_b", 8), ("conv_kernel_2", 24), ("conv_dw_w", 8 * TAPS)):
        rows.append((name, at, n))
        VECTORS[name] = at
        at += n
    return rows, at


def distance_tables():
    d = (S - 1) - np.arange(GCOLS)
    exact = BUCKETS // 2
    df = np.maximum(d, 1).astype(np.float32)
    large = exact + (np.log(df / np.float32(exact)) / np.float32(np.log(MAX_DISTANCE / exact))
                     * np.float32(BUCKETS - exact)).astype(np.int32)
    bucket = np.where(d < exact, d, np.minimum(large, BUCKETS - 1))
    onehot = np.zeros((BUCKETS, GCOLS), np.float32)
    count = np.zeros(GCOLS)
    for window, dilation in BRANCHES:
        count += (d >= 0) & (d % dilation == 0) & (d // dilation <= window // dilation)
    for m in range(GCOLS):
        if d[m] >= 0:
            onehot[bucket[m], m] = 1.0
    logcount = np.where(count > 0, np.log(np.maximum(count, 1)), MASKED).astype(np.float32)
    return onehot, np.tile(logcount[None, :], (HEADS, 1))


class Book:

    def __init__(self, eng):
        self.eng, self.count, self.index, self.per, self.parity = eng, {}, None, {}, 0

    def at(self, name, more=0):
        v = max(self.count.get(name, 0) + more, 0)
        return v if self.index is None else v + self.index * self.per.get(name, 0)

    def add(self, **more):
        for k, v in more.items():
            self.count[k] = self.count.get(k, 0) + v

    @contextmanager
    def loop(self, n, per):
        before = dict(self.count)
        if self.eng is None:
            yield 0
        else:
            with self.eng.Fori(0, n) as i:
                self.index, self.per = i, per
                yield i
        for k in set(self.count) | set(per):
            assert self.count.get(k, 0) - before.get(k, 0) == per.get(k, 0), (k, per)
            self.count[k] = before.get(k, 0) + n * per.get(k, 0)
        self.index, self.per = None, {}


def group_counts(kind, tiles):
    return {**GROUP[kind], "tiles": tiles}


def attention_shape(kind):
    if kind == "mem":
        return [MEM * i for i in range(TB)], [MEM] * TB, (lambda i: range(MB)), [(0, 0), (S, 0)]
    return ([0, 128, 384, 768], [(i + 1) * P for i in range(TB)], (lambda i: range(i + 1)),
            [(0, 0), (512, 128), (1024, 256), (896, 384)])


def attention_counts(kind):
    n = MEM_HEADS if kind == "mem" else HEADS
    c = {k: TB * n for k in ("scored", "maxed", "expd", "summed")}
    c["normed"] = (TB - 1) * n
    c.update({k: n for k in ("normed_last", "turned", "turned_hi", "turned_lo", "weighed", "out_hi", "out_lo")})
    if kind != "mem":
        c.update(tables=n // 2, shifted=TB * n)
    if kind == "fox":
        c["masked"] = n
    return c


def schedule(b, e):

    def do(step, counts, *args, **kw):
        if step in e:
            e[step](*args, **kw)
        b.add(**counts)

    def groups(kind, src, rhs, dst=None, first=False, tiles=4, g=0, n=1, c0=None, **kw):
        for i in range(n):
            do("group", group_counts(kind, tiles), kind, src, g + i, rhs, dst, first and i == 0, tiles,
               at=(g if c0 is None else c0) + i, **kw)
            b.parity ^= 1

    def normed(kind, src, rhs, dst=None, n=1, **kw):
        do("group", {**group_counts(kind, 4), **STATS}, kind, src, 0, rhs, dst, True, 4, at=0, stats=True, **kw)
        b.parity ^= 1
        groups(kind, src, rhs, dst, n=n - 1, g=1, **kw)

    def add(src, rhs, gain=None, tiles=4, fresh=True, bias=None, row0=0, split=True):
        for g in range(2):
            do("group", group_counts("add", tiles), "add", src, g, rhs, None, fresh and g == 0, tiles,
               at=g, bias=bias, row0=row0)
            b.parity ^= 1
            if gain is not None:
                do("prep", prep_counts(2 * g, 2, split), gain, 2 * g, 2, split)

    def mem_kv_groups(layer):
        return [lambda g=g: groups("proj", f"mem_wk{layer}", "hm", "km", g=g, width=MEM)
                for g in range(2)] + \
               [lambda g=g: groups("proj", f"mem_wv{layer}", "hm", "vm", g=g, rows=MB) for g in range(2)]

    def mem_attention(layer, next_gain):
        if layer:
            do("mem_turn", MEM_TURN, layer)
            for f in mem_kv_groups(layer):
                f()
        normed("proj", f"mem_wq{layer}", "h", "q", n=2, scale=MEM_HEAD_DIM ** -0.5)
        do("attend", attention_counts("mem"), "mem")
        add(f"mem_wo{layer}", "q", gain=next_gain, fresh=False)

    def ff(layer, next_gain, split=True):
        up, down = f"ff_w1{layer}", f"ff_w2{layer}"
        rounds = D_FF // D
        per_round = {}
        for part in (group_counts("relu2", 4), group_counts("relu2", 4),
                     group_counts("add", 4), group_counts("add", 4)):
            for k, v in part.items():
                per_round[k] = per_round.get(k, 0) + v
        normed("relu2", up, "h", "mid", n=2)
        add(down, "mid")
        with b.loop(rounds - 2, per_round) as i:
            groups("relu2", up, "h", "mid", g=2 * i + 2, n=2, c0=0)
            add(down, "mid", row0=(i + 1) * D)
        groups("relu2", up, "h", "mid", g=2 * (rounds - 1), n=2, c0=0)
        add(down, "mid", gain=next_gain, row0=(rounds - 1) * D, split=split)

    def swiglu(layer, next_gain, split=True):
        src, down = f"glu2{layer}", f"down2{layer}"
        normed("gate", src, "h", "mid", n=4)
        add(down, "mid")
        groups("gate", src, "h", "mid", g=4, n=4, c0=0)
        add(down, "mid", row0=D)
        rest = (D_FF2 - 2 * D) // 256
        groups("gate", src, "h", "mid", g=8, n=rest, c0=0)
        add(down, "mid", gain=next_gain, tiles=rest, row0=2 * D, split=split)

    def gain(name, layer=0):
        return VECTORS[name] + DC * layer

    do("prologue", PROLOGUE)
    do("mem_turn", MEM_TURN, 0)
    do("prep_all", prep_counts(0, 4), gain("norm_mix_g"))
    kv = mem_kv_groups(0)
    for g in range(4):
        if g == 0:
            normed("glu", "pw1", "h")
        else:
            groups("glu", "pw1", "h", g=g)
        do("conv", dict(step=2 * TAPS), g)
        kv[g]()
    do("layer_norm", LAYER_NORM)
    add("pw2", "mid", gain=gain("norm_mem_g"), bias="conv_pw2_b")
    mem_attention(0, gain("norm_ff_g"))
    ff(0, gain("kv_norm_g"))
    do("gates_load", {})
    normed("proj", "fox_k", "h", "k", n=2)
    do("columns", COLUMNS)
    groups("proj", "fox_v", "h", "v", n=2, rows=TB)
    do("gates", GATES)
    do("prep_all", prep_counts(0, 4, squares=False), gain("norm_mix_g", 1), squares=False)
    groups("proj", "fox_wq", "h", "q", n=2, first=True, scale=HEAD_DIM ** -0.5)
    do("attend", attention_counts("fox"), "fox")
    add("fox_wo", "q", gain=gain("norm_mem_g", 1), fresh=False)
    mem_attention(1, gain("norm_ff_g", 1))
    ff(1, gain("final_norm_g"), split=False)
    do("final_norm", FINAL_NORM, gain("final_norm_g"))
    do("prep_all", prep_counts(0, 4), gain("mix_norm_2"))
    normed("cu", "conv_cu", "h", n=4)
    groups("bmul", "conv_b", "h", "mid", n=2)
    add("conv_out", "mid", gain=gain("ffn_norm_2"))
    swiglu(0, gain("mix_norm_2", 1))
    normed("proj", "dil_q", "h", "q", n=2, scale=HEAD_DIM ** -0.5)
    groups("proj", "dil_k", "h", "k", n=2)
    do("columns", COLUMNS)
    groups("proj", "dil_v", "h", "v", n=2, rows=TB)
    do("attend", attention_counts("dil"), "dil")
    add("dil_out", "q", gain=gain("ffn_norm_2", 1), fresh=False)
    swiglu(1, gain("final_norm_2"), split=False)
    do("final_norm", FINAL_NORM, gain("final_norm_2"))
    do("output", {})


def build(nc, A, out):
    with ExitStack() as ctx:
        build_in(nc, A, out, ctx)


def build_in(nc, A, out, ctx):
    def sem(name):
        return ctx.enter_context(nc.semaphore(name))

    KB = 1024
    place = [SBUF_BASE]

    def region(nbytes):
        place[0] += nbytes
        assert place[0] <= nc.sbuf_usable_end
        return place[0] - nbytes

    def at(name, shape, dt, offset):
        return nc.alloc_sbuf_tensor_at(name, shape, dt, offset=offset)

    rows, n_rows = vector_rows()
    R_X, R_H, R_MID = region(16 * KB), region(32 * KB), region(32 * KB)
    R_ST, R_W = region(16 * KB), region(32 * KB)
    R_A0, R_A1, R_T = region(32 * KB), region(32 * KB), region(8 * KB)

    x = at("x", [P, DC, S], F32, R_X)
    h_hi, h_lo = at("h_hi", [P, DC, S], F32R, R_H), at("h_lo", [P, DC, S], F32R, R_H + 16 * KB)
    mid_hi, mid_lo = at("mid_hi", [P, DC, S], F32R, R_MID), at("mid_lo", [P, DC, S], F32R, R_MID + 16 * KB)
    stage = at("stage", [P, SLOTS, 2, COLS], F32, R_ST)
    w_hi = at("w_hi", [P, SLOTS, 2, COLS], F32R, R_W)
    w_lo = at("w_lo", [P, SLOTS, 2, COLS], F32R, R_W + 16 * KB)
    q_hi, q_lo = at("q_hi", [P, DC, S], F32R, R_A0), at("q_lo", [P, DC, S], F32R, R_A0 + 16 * KB)
    k_hi, k_lo = at("k_hi", [P, DC, S], F32R, R_A1), at("k_lo", [P, DC, S], F32R, R_A1 + 16 * KB)
    t = at("t", [P, 4, S], F32, R_T)
    rstd, acc = at("rstd", [P, S], F32, region(2 * KB)), at("acc", [P, S], F32, region(2 * KB))
    ident, ones = at("ident", [P, P], F32, region(512)), at("ones", [P, P], F32, region(512))
    mask = at("mask", [P, P], F32, region(512))
    vec = at("vec", [P, n_rows], F32, region((n_rows * 4 + 31) // 32 * 32))
    small = at("small", [P, 64], F32, region(256))
    xnat = at("xnat", [P, TB, D], F32, R_MID)
    vrow = at("vrow", [P, 4, P], F32, R_A0)
    g_tab = at("g_tab", [HEADS, GCOLS], F32, R_A0 + 2 * KB)
    g_log = at("g_log", [HEADS, GCOLS], F32, R_A0 + 5 * KB)
    onehot_sb = at("onehot_sb", [BUCKETS, GCOLS], F32, R_A0 + 8 * KB)
    relb = at("relb", [BUCKETS, HEADS], F32, R_A0 + 11 * KB)
    memn, junk = at("memn", [P, MB, D], F32, R_A1), at("junk", [P, D], F32, R_A1 + 8 * KB)
    hm_hi = at("hm_hi", [P, DC, MEM], F32R, R_A0 + 16 * KB)
    hm_lo = at("hm_lo", [P, DC, MEM], F32R, R_A0 + 24 * KB)
    km_hi, km_lo = at("km_hi", [P, DC, MEM], F32R, R_A1), at("km_lo", [P, DC, MEM], F32R, R_A1 + 8 * KB)
    vm_hi, vm_lo = at("vm_hi", [P, MB, D], F32R, R_A1 + 16 * KB), at("vm_lo", [P, MB, D], F32R, R_A1 + 24 * KB)
    u_pad, conv = at("u_pad", [P, DC, PAD + S], F32, R_MID), at("conv", [P, DC, S], F32, R_A0)
    z_pad, y2 = at("z_pad", [P, 2, 2 + S], F32, R_A1), at("y2", [P, DC, S], F32, R_A0)
    v_hi, v_lo = at("v_hi", [P, TB, D], F32R, R_MID), at("v_lo", [P, TB, D], F32R, R_MID + 16 * KB)
    wf = at("wf", [P, DC, HEADS], F32, R_A0)
    wf_hi, wf_lo = at("wf_hi", [P, DC, P], F32R, R_A0 + 4 * KB), at("wf_lo", [P, DC, P], F32R, R_A0 + 8 * KB)
    f_t = at("f_t", [HEADS, 4, S], F32, R_A0 + 16 * KB)
    WID = 1280
    prob = [at(f"prob{i}", [P, WID], F32, R_H + i * 5 * KB) for i in range(2)]
    pt_hi = [at(f"pt_hi{i}", [P, WID], F32R, R_H + (10 + 10 * i) * KB) for i in range(2)]
    pt_lo = [at(f"pt_lo{i}", [P, WID], F32R, R_H + (15 + 10 * i) * KB) for i in range(2)]

    operand = {"h": (h_hi, h_lo), "mid": (mid_hi, mid_lo), "q": (q_hi, q_lo), "k": (k_hi, k_lo),
               "hm": (hm_hi, hm_lo), "km": (km_hi, km_lo), "vm": (vm_hi, vm_lo), "v": (v_hi, v_lo)}

    ps = ctx.enter_context(nc.psum_tensor("ps", [P, 8, S], F32))

    negc_dram = nc.dram_tensor("negc_dram", (HEADS, S), F32, kind="Internal").ap()
    g_dram = nc.dram_tensor("g_dram", (HEADS, GCOLS), F32, kind="Internal").ap()
    skew_dram = nc.dram_tensor("skew_dram", (HEADS, P * GCOLS), F32, kind="Internal").ap()
    onehot, logcount = distance_tables()
    onehot_c = nc.inline_tensor(onehot, "onehot_c").ap()
    logcount_c = nc.inline_tensor(logcount, "logcount_c").ap()

    tile_loaded = [sem(f"tile_loaded{i}") for i in range(SLOTS)]
    tile_hi, tile_lo = sem("tile_hi"), sem("tile_lo")
    tiles_used = sem("tiles_used")
    psum_read = sem("psum_read")
    t_ready = sem("t_ready")
    gated = sem("gated")
    part_hi, part_lo = sem("part_hi"), sem("part_lo")
    squared = sem("squared")
    step = sem("step")
    pe_side, act_side = sem("pe_side"), sem("act_side")
    rstd_ready = sem("rstd_ready")
    consts = sem("consts")
    rows_in, x_in, mem_in = sem("rows_in"), sem("x_in"), sem("mem_in")
    g_out, skewed, gates_in, negc_out, stored = (sem(n) for n in ("g_out", "skewed", "gates_in", "negc_out", "stored"))
    table_in = [sem("table_in0"), sem("table_in1")]
    scored, shifted, maxed, expd = (sem(n) for n in ("scored", "shifted", "maxed", "expd"))
    masked, summed, turned = sem("masked"), sem("summed"), sem("turned")
    normed_p, normed_last = sem("normed"), sem("normed_last")
    turned_hi, turned_lo, weighed = sem("turned_hi"), sem("turned_lo"), sem("weighed")
    out_hi, out_lo = sem("out_hi"), sem("out_lo")

    def column(j):
        return vec[:, j:j + 1]

    def head_rows(h):
        return h * HEAD_DIM // P, slice(h * HEAD_DIM % P, h * HEAD_DIM % P + HEAD_DIM)

    dry = Book(None)
    schedule(dry, {})
    TILES = dry.count["tiles"]

    def loaded_at(b, ahead):
        n = b.count.get("tiles", 0) + ahead
        v = 32 * (n // SLOTS + 1)
        if b.index is not None:
            v = v + b.index * (32 // SLOTS * b.per["tiles"])
        return n % SLOTS, v

    def flat(banks, n):
        return banks.rearrange("p b s -> p (b s)")[:, 0:n]

    def proj_parts(dst, lo, at, width):
        to = operand[dst][lo]
        c = slice(S * at, S * at + S)
        if dst == "vm":
            return [(to[:, a, c], t[:, a, :]) for a in range(2)]
        if dst == "v":
            return [(to[:, 2 * a:2 * a + 2, c], t[:, 2 * a:2 * a + 2, :]) for a in range(2)]
        return [(to[:, 4 * at + 2 * a:4 * at + 2 * a + 2, :], t[:, 2 * a:2 * a + 2, 0:width]) for a in range(2)]

    def out_of(kind, h, q):
        if kind == "mem":
            return q[:, 2 * h:2 * h + 2, :], ps[:, 6:8, :]
        c, r = head_rows(h)
        return q[r, c, :], ps[r, 7, :]

    row_loads = []
    for name, first, n in rows:
        flat_ap = A[name].rearrange("(a b) -> a b", b=P) if len(A[name].shape) == 1 else \
            A[name].rearrange("a (b c) -> (a b) c", c=P) if len(A[name].shape) == 2 else \
            A[name][0].rearrange("a (b c) -> (a b) c", c=P)
        done = 0
        while done < n:
            r = first + done
            m = min(n - done, P - r % P)
            row_loads.append((vrow[r % P:r % P + m, r // P, :], (flat_ap[done:done + m, :], m)))
            done += m
    row_loads += [(relb[:, :], (A["rel_bias_2"], 0)), (onehot_sb[:, :], (onehot_c, 0)), (g_log[:, :], (logcount_c, 0))]
    ROWS_IN = 16 * len(row_loads)

    block = ctx.enter_context(nc.Block())

    @block.sync
    def _(sp):
        b = Book(sp)

        def plain(w):
            def src(g, j, row0):
                return [(stage_at[:, a, :], w[bass.ds(row0 + (2 * j + a) * P, P), bass.ds(g * COLS, COLS)])
                        for a in (0, 1)]
            return src

        def pair(wa, wb, off_a=0, off_b=0):
            def src(g, j, row0):
                return [(stage_at[:, :, 256 * n:256 * n + 256],
                         w[2 * j * P:2 * (j + 1) * P, off + g * 256:off + (g + 1) * 256]
                         .rearrange("(a p) n -> p a n", p=P))
                        for n, (w, off) in enumerate(((wa, off_a), (wb, off_b)))]
            return src

        src_of = {"pw1": pair(A["conv_pw1_w"][0], A["conv_pw1_w"][0], D, 0), "pw2": plain(A["conv_pw2_w"][0]),
                  "fox_k": plain(A["kvf_w"][:, 0:D]), "fox_v": plain(A["kvf_w"][:, D:2 * D]),
                  "fox_wq": plain(A["fox_wq"][0]), "fox_wo": plain(A["fox_wo"][0]),
                  "conv_cu": pair(A["conv_w_in_2"][0], A["conv_w_in_2"][0], D, 2 * D),
                  "conv_b": plain(A["conv_w_in_2"][0][:, 0:D]), "conv_out": plain(A["conv_w_out_2"][0]),
                  "dil_q": plain(A["attn_w_qkv_2"][0][:, 0:D]), "dil_k": plain(A["attn_w_qkv_2"][0][:, D:2 * D]),
                  "dil_v": plain(A["attn_w_qkv_2"][0][:, 2 * D:3 * D]), "dil_out": plain(A["attn_w_out_2"][0])}
        for layer in range(2):
            for n in ("mem_wq", "mem_wk", "mem_wv", "mem_wo", "ff_w1", "ff_w2"):
                src_of[f"{n}{layer}"] = plain(A[n][layer])
            src_of[f"glu2{layer}"] = pair(A["ffn_w_gate_2"][layer], A["ffn_w_up_2"][layer])
            src_of[f"down2{layer}"] = plain(A["ffn_w_down_2"][layer])

        def group(kind, src, g, rhs, dst, fresh, tiles, row0=0, **_):
            nonlocal stage_at
            for j in range(tiles):
                slot, _v = loaded_at(b, j)
                stage_at = stage[:, slot]
                sp.wait_ge(tile_lo, b.at("tiles", j - SLOTS + 1))
                for to, frm in src_of[src](g, j, row0):
                    sp.dma_start(to, frm).then_inc(tile_loaded[slot], 16)

        stage_at = None
        schedule(b, dict(group=group))
        sp.wait_ge(stored, 16)

    @block.gpsimd
    def _(pool):
        b = Book(pool)
        pool.memset(ones[:, :], 1.0)
        pool.memset(ident[:, :], 0.0)
        pool.memset(mask[:, :], 0.0).then_inc(consts, 1)
        pool.wait_ge(consts, 1)
        pool.affine_select(out=ident[:, :], in_=ident[:, :], compare_op=ALU.not_equal, fill=1.0,
                           base=0, pattern=[[-1, P]], channel_multiplier=1)
        pool.affine_select(out=mask[:, :], in_=mask[:, :], compare_op=ALU.is_ge, fill=MASKED,
                           base=0, pattern=[[-1, P]], channel_multiplier=1).then_inc(consts, 1)

        def group(kind, src, g, rhs, dst, fresh, tiles, **_):
            for j in range(tiles):
                slot, _v = loaded_at(b, j)
                pool.wait_ge(tile_hi, b.at("tiles", j + 1))
                pool.tensor_tensor(w_lo[:, slot], stage[:, slot], w_hi[:, slot].bitcast(F32),
                                   ALU.subtract).then_inc(tile_lo, 1)

        def attend(kind):
            offs, widths, _keys, _pt = attention_shape(kind)
            heads = MEM_HEADS if kind == "mem" else HEADS

            def diagonals(h):
                if kind != "fox" or h >= heads:
                    return
                pool.wait_ge(table_in[h % 2], 16 * (b.count.get("tables", 0) + h // 2 + 1))
                if h >= 2:
                    pool.wait_ge(shifted, b.at("shifted", TB * (h - 1)))
                pool.tensor_tensor(t[:, 2 + h % 2, :].rearrange("p (i k) -> p i k", i=TB),
                                   t[:, h % 2, :].rearrange("p (i k) -> p i k", i=TB),
                                   mask[:, :].unsqueeze(1).broadcast_to([P, TB, P]), ALU.add).then_inc(masked, 1)

            pool.wait_ge(part_lo, b.at("part_lo"))
            diagonals(0)
            for h in range(heads):
                diagonals(h + 1)
                for i in range(TB - 1):
                    pool.wait_ge(summed, b.at("summed", TB * h + i + 1))
                    row, n = prob[h % 2][:, offs[i]:offs[i] + widths[i]], 4 * (h % 2) + i
                    pool.tensor_scalar(row, row, small[:, 24 + n:25 + n], None, ALU.mult).then_inc(normed_p, 1)

        schedule(b, dict(group=group, attend=attend))

    @block.tensor
    def _(pe):
        b = Book(pe)

        def sums(bank):
            pe.matmul(ps[:, bank, :], ones[:, :], acc[:, :], start=True, stop=True).then_inc(pe_side, 1)

        def group(kind, src, g, rhs, dst, fresh, tiles, stats=False, rows=None, width=S, **_):
            r_hi, r_lo = operand[rhs]
            base = 4 * b.parity
            pe.wait_ge(psum_read, b.at("psum_read", -2))
            for j in range(tiles):
                if stats and j == tiles - 1:
                    pe.wait_ge(step, b.at("step"))
                    pe.wait_ge(psum_read, b.at("psum_read"))
                    sums(4 - base)
                if fresh:
                    pe.wait_ge(part_lo, b.at("part_lo", j + 1 - tiles))
                slot, _v = loaded_at(b, j)
                pe.wait_ge(tile_lo, b.at("tiles", j + 1))
                for a in range(2):
                    k = 2 * j + a
                    for n in range(rows or 4):
                        c = slice(n * P, (n + 1) * P)
                        if rows:
                            passes = ((r_hi[:, k, c], w_hi[:, slot, a, :]), (r_hi[:, k, c], w_lo[:, slot, a, :]),
                                      (r_lo[:, k, c], w_hi[:, slot, a, :]))
                        else:
                            passes = ((w_hi[:, slot, a, c], r_hi[:, k, :]), (w_hi[:, slot, a, c], r_lo[:, k, :]),
                                      (w_lo[:, slot, a, c], r_hi[:, k, :]))
                        for m, (lhs, mov) in enumerate(passes):
                            last = pe.matmul(ps[:, base + n, 0:width], lhs, mov, start=k == 0 and m == 0,
                                             stop=k == 2 * tiles - 1 and m == 2)
                last.then_inc(tiles_used, 1)
            if stats:
                pe.wait_ge(act_side, b.at("act_side", 1))

        def prologue():
            pe.wait_ge(consts, 2)
            pe.wait_ge(rows_in, ROWS_IN)
            for r in range(4):
                n = min(P, n_rows - r * P)
                last = pe.transpose(ps[:, 0, r * P:r * P + n], vrow[0:n, r, :], ident[0:n, 0:n])
            last.then_inc(pe_side, 1)
            for c, n in ((0, S), (S, GCOLS - S)):
                last = pe.matmul(ps[0:HEADS, 1 + c // S, 0:n], relb[:, :], onehot_sb[:, c:c + n],
                                 start=True, stop=True)
            last.then_inc(pe_side, 1)
            pe.wait_ge(x_in, 16)
            for c in range(DC):
                if c < 2:
                    pe.wait_ge(step, c + 1)
                for i in range(TB):
                    last = pe.transpose(ps[:, c, i * P:(i + 1) * P], xnat[:, i, c * P:(c + 1) * P], ident[:, :])
                last.then_inc(pe_side, 1)

        def mem_turn(layer):
            pe.wait_ge(psum_read, b.at("psum_read"))
            pe.wait_ge(step, b.at("step", 3))
            for c in range(DC):
                for i in range(MB):
                    o = (c % 2) * MEM + i * P
                    last = pe.transpose(ps[:, c // 2, o:o + P], memn[:, i, c * P:(c + 1) * P], ident[:, :])
                if c % 2:
                    last.then_inc(pe_side, 1)
            pe.wait_ge(part_lo, b.at("part_lo", 4))

        def layer_norm():
            pe.wait_ge(psum_read, b.at("psum_read"))
            pe.wait_ge(step, b.at("step", LN_MEAN))
            sums(0)
            pe.wait_ge(step, b.at("step", LN_MEAN + LN_CENTRE + LN_SQUARES))
            sums(0)
            pe.wait_ge(act_side, b.at("act_side", 1))

        def columns():
            bank = 4 * b.parity
            pe.wait_ge(psum_read, b.at("psum_read", -2))
            pe.wait_ge(rstd_ready, b.at("rstd_ready"))
            for i in range(TB):
                last = pe.transpose(ps[:, bank, i * P:(i + 1) * P], rstd[:, i * P:(i + 1) * P], ident[:, :])
            last.then_inc(pe_side, 1)
            pe.wait_ge(step, b.at("step", 1))

        def gates():
            bank = 4 * b.parity
            pe.wait_ge(psum_read, b.at("psum_read", -2))
            pe.wait_ge(act_side, b.at("act_side", 1))
            pe.wait_ge(step, b.at("step", 2))
            n = 0
            for k in range(DC):
                for lhs, mov in ((wf_hi, h_hi), (wf_hi, h_lo), (wf_lo, h_hi)):
                    last = pe.matmul(ps[:, bank, :], lhs[:, k, :], mov[:, k, :], start=n == 0, stop=n == 3 * DC - 1)
                    n += 1
            last.then_inc(pe_side, 1)
            pe.wait_ge(step, b.at("step", 3))

        def final_norm(gain):
            pe.wait_ge(step, b.at("step"))
            pe.wait_ge(psum_read, b.at("psum_read"))
            sums(4 * b.parity)
            pe.wait_ge(act_side, b.at("act_side", 1))

        def attend(kind):
            offs, widths, keys, pt = attention_shape(kind)
            mem = kind == "mem"
            heads, dch = (MEM_HEADS, MEM_HEAD_DIM // P) if mem else (HEADS, 1)
            (K_hi, K_lo), (V_hi, V_lo) = operand["km" if mem else "k"], operand["vm" if mem else "v"]
            pe.wait_ge(psum_read, b.at("psum_read"))
            pe.wait_ge(part_lo, b.at("part_lo"))

            def scores(h):
                for i in range(TB):
                    if h and mem:
                        pe.wait_ge(expd, b.at("expd", TB * (h - 1) + i + 1))
                    elif h:
                        pe.wait_ge(shifted, b.at("shifted", TB * (h - 1) + i + 1))
                    n = 0
                    for dc in range(dch):
                        c, r = (h * dch + dc, slice(0, P)) if mem else head_rows(h)
                        for lhs, mov in ((q_hi, K_hi), (q_hi, K_lo), (q_lo, K_hi)):
                            last = pe.matmul(ps[:, i, 0:widths[i]], lhs[r, c, i * P:(i + 1) * P],
                                             mov[r, c, 0:widths[i]], start=n == 0, stop=n == 3 * dch - 1)
                            n += 1
                    last.then_inc(scored, 1)

            def turn(h):
                if h:
                    pe.wait_ge(turned_lo, b.at("turned_lo", h))
                for i in range(TB):
                    if i < TB - 1:
                        pe.wait_ge(normed_p, b.at("normed", (TB - 1) * h + i + 1))
                    else:
                        pe.wait_ge(normed_last, b.at("normed_last", h + 1))
                    for j in keys(i):
                        c = pt[j][0] + i * P - pt[j][1]
                        last = pe.transpose(ps[:, 4 + c // S, c % S:c % S + P],
                                            prob[h % 2][:, offs[i] + j * P:offs[i] + (j + 1) * P], ident[:, :])
                last.then_inc(turned, 1)

            def weigh(h):
                pe.wait_ge(turned_lo, b.at("turned_lo", h + 1))
                if h:
                    pe.wait_ge(out_lo, b.at("out_lo", h))
                for dc in range(dch):
                    bank, c = (6 + dc, h * dch + dc) if mem else (7, head_rows(h)[0])
                    n = 0
                    for j, (col, tok) in enumerate(pt):
                        for lhs, mov in ((V_hi, pt_hi), (V_hi, pt_lo), (V_lo, pt_hi)):
                            last = pe.matmul(ps[:, bank, tok:S], lhs[:, j, c * P:(c + 1) * P],
                                             mov[h % 2][:, col:col + S - tok], start=n == 0, stop=n == 3 * len(pt) - 1)
                            n += 1
                last.then_inc(weighed, 1)

            scores(0)
            for h in range(heads + 2):
                if 1 <= h <= heads:
                    turn(h - 1)
                if h >= 2:
                    weigh(h - 2)
                if h + 1 < heads:
                    scores(h + 1)
            pe.wait_ge(out_lo, b.at("out_lo", heads))

        def output():
            pe.wait_ge(step, b.at("step"))
            for n in range(2 * TB):
                for a in range(4):
                    last = pe.transpose(ps[:, n, a * P:(a + 1) * P],
                                        x[:, 4 * (n % 2) + a, n // 2 * P:(n // 2 + 1) * P], ident[:, :])
                last.then_inc(pe_side, 1)

        schedule(b, dict(prologue=prologue, group=group, mem_turn=mem_turn, layer_norm=layer_norm,
                         columns=columns, gates=gates, final_norm=final_norm, attend=attend, output=output))

    @block.scalar
    def _(act):
        b = Book(act)

        def split_tiles(first, n):
            for m in range(first, first + n):
                if b.index is None and b.count.get("tiles", 0) + m >= TILES:
                    return
                slot, v = loaded_at(b, m)
                act.wait_ge(tile_loaded[slot], v)
                act.wait_ge(tiles_used, b.at("tiles", m - SLOTS + 1))
                act.activation(w_hi[:, slot], stage[:, slot], ACT.Copy).then_inc(tile_hi, 1)

        def root(bank, eps):
            act.activation(rstd[:, :], ps[:, bank, :], ACT.Sqrt, scale=1.0 / D, bias=eps_col(eps)).then_inc(act_side, 1)

        def eps_col(eps):
            return small[:, 40:41] if eps == RMS_EPS else small[:, 41:42]

        def group(kind, src, g, rhs, dst, fresh, tiles, at=0, stats=False, rows=None, width=S, **_):
            split_tiles(SLOTS, tiles - 1)
            if stats:
                act.wait_ge(pe_side, b.at("pe_side", 1))
                root(4 - 4 * b.parity, RMS_EPS)
            if kind == "glu":
                act.wait_ge(psum_read, b.at("psum_read", 1))
                for a in range(2):
                    last = act.activation(t[:, a, :], t[:, a, :], ACT.Sigmoid,
                                          bias=column(VECTORS["conv_pw1_b"] + DC + 2 * at + a))
                last.then_inc(gated, 1)
            if kind == "gate":
                act.wait_ge(psum_read, b.at("psum_read", 1))
                act.activation(t[:, 0:2, :], t[:, 0:2, :], ACT.Silu).then_inc(gated, 1)
                act.wait_ge(t_ready, b.at("t_ready", 1))
                act.activation(mid_hi[:, 2 * at:2 * at + 2, :], t[:, 2:4, :], ACT.Copy).then_inc(part_hi, 1)
            if kind in ("relu2", "bmul"):
                for a in range(2):
                    act.wait_ge(t_ready, b.at("t_ready", a + 1))
                    act.activation(mid_hi[:, 4 * at + 2 * a:4 * at + 2 * a + 2, :], t[:, 2 * a:2 * a + 2, :],
                                   ACT.Copy).then_inc(part_hi, 1)
            if kind == "proj":
                for a, (to, frm) in enumerate(proj_parts(dst, 0, at, width)):
                    act.wait_ge(psum_read, b.at("psum_read", a + 1))
                    act.activation(to, frm, ACT.Copy).then_inc(part_hi, 1)
            split_tiles(SLOTS + tiles - 1, 1)

        def prologue():
            for r, (frm, n) in row_loads:
                act.dma_start(r, frm).then_inc(rows_in, 16)
            act.dma_start(xnat[:, :, :], A["x"][0].rearrange("(i p) d -> p i d", p=P)).then_inc(x_in, 16)
            act.wait_ge(step, 2)
            act.dma_start(g_dram, g_tab[:, :]).then_inc(g_out, 16)
            act.wait_ge(g_out, 16)
            act.dma_start(skew_dram.rearrange("h (p n) -> h p n", p=P),
                          bass.AP(g_dram.tensor, 0, [[GCOLS, HEADS], [0, P], [1, GCOLS]])).then_inc(skewed, 16)
            split_tiles(0, SLOTS)

        def mem_turn(layer):
            if layer:
                act.wait_ge(psum_read, b.at("psum_read"))
            act.dma_start(memn[:, :, :], A["mem"][0].rearrange("(i p) d -> p i d", p=P)).then_inc(mem_in, 16)
            act.wait_ge(mem_in, 16 * (layer + 1))
            for i in range(MB):
                act.activation(junk[:, :], memn[:, i, :], ACT.Square, accum_out=small[:, i:i + 1]).then_inc(act_side, 1)
                act.wait_ge(act_side, b.at("act_side", i + 1))
            act.activation(small[:, 2:4], small[:, 0:2], ACT.Sqrt, scale=1.0 / D, bias=eps_col(RMS_EPS)).then_inc(act_side, 1)
            for m in range(4):
                act.wait_ge(pe_side, b.at("pe_side", m + 1))
                for a in range(2):
                    last = act.activation(hm_hi[:, 2 * m + a, :], ps[:, m, a * MEM:(a + 1) * MEM], ACT.Copy,
                                          scale=column(VECTORS["norm_memsrc_g"] + DC * layer + 2 * m + a))
                last.then_inc(part_hi, 1)

        def prep(gain, first, n, split, squares=True, whole=False):
            for m in range(n):
                p = first + m
                if not whole:
                    act.wait_ge(psum_read, b.at("psum_read", m + 1 - n))
                if split:
                    for c in (2 * p, 2 * p + 1):
                        last = act.activation(h_hi[:, c, :], x[:, c, :], ACT.Copy, scale=column(gain + c))
                    last.then_inc(part_hi, 1)
                if squares:
                    if m >= 2:
                        act.wait_ge(step, b.at("step", steps_after(first, m - 1)))
                    a = 2 * (p % 2)
                    act.activation(t[:, a:a + 2, :], x[:, 2 * p:2 * p + 2, :], ACT.Square).then_inc(squared, 1)

        def steps_after(first, m):
            return sum(1 if p == 0 else 2 for p in range(first, first + m))

        def prep_all(gain, squares=True):
            act.wait_ge(psum_read, b.at("psum_read"))
            act.wait_ge(step, b.at("step"))
            act.wait_ge(pe_side, b.at("pe_side"))
            prep(gain, 0, 4, True, squares, whole=True)

        def layer_norm():
            for p in range(4):
                act.wait_ge(step, b.at("step", LN_MEAN + (2 if p == 0 else LN_CENTRE + 2 * p - 1)))
                act.activation(t[:, 2:4, :], conv[:, 2 * p:2 * p + 2, :], ACT.Square).then_inc(squared, 1)
            act.wait_ge(pe_side, b.at("pe_side", 2))
            root(0, LN_EPS)
            for p in range(4):
                act.wait_ge(step, b.at("step", LN_MEAN + LN_CENTRE + LN_SQUARES + p + 1))
                for c in (2 * p, 2 * p + 1):
                    last = act.activation(conv[:, c, :], conv[:, c, :], ACT.Silu,
                                          scale=column(VECTORS["conv_ln_g"] + c), bias=column(VECTORS["conv_ln_b"] + c))
                last.then_inc(gated, 1)
                act.wait_ge(gated, b.at("gated", p + 1))
                act.activation(mid_hi[:, 2 * p:2 * p + 2, :], conv[:, 2 * p:2 * p + 2, :], ACT.Copy).then_inc(part_hi, 1)

        def gates():
            act.wait_ge(gates_in, 32)
            act.wait_ge(psum_read, b.at("psum_read"))
            act.wait_ge(step, b.at("step", 1))
            act.activation(wf_hi[:, :, 0:HEADS], wf[:, :, :], ACT.Copy).then_inc(act_side, 1)
            act.wait_ge(step, b.at("step", 4))
            act.activation(f_t[:, 1, :], f_t[:, 0, :], ACT.Abs).then_inc(act_side, 1)
            act.wait_ge(act_side, b.at("act_side", 2))
            act.activation(f_t[:, 1, :], f_t[:, 1, :], ACT.Exp, scale=-1.0).then_inc(act_side, 1)
            act.wait_ge(act_side, b.at("act_side", 3))
            act.activation(f_t[:, 1, :], f_t[:, 1, :], ACT.Ln, bias=1.0).then_inc(act_side, 1)
            act.wait_ge(step, b.at("step", 6))
            act.dma_start(negc_dram, f_t[:, 3, :]).then_inc(negc_out, 16)
            act.wait_ge(negc_out, 16)

        def final_norm(gain):
            act.wait_ge(pe_side, b.at("pe_side", 1))
            root(4 * b.parity, RMS_EPS)

        def gates_load():
            act.wait_ge(psum_read, b.at("psum_read"))
            act.dma_start(wf[:, :, :], A["kvf_w"][:, 2 * D:2 * D + HEADS].rearrange("(k p) n -> p k n", p=P)).then_inc(gates_in, 16)
            act.dma_start(small[0:HEADS, 50:51], A["fgate_b"].rearrange("(h a) -> h a", a=1)).then_inc(gates_in, 16)

        def attend(kind):
            offs, widths, keys, pt = attention_shape(kind)
            mem = kind == "mem"
            heads = MEM_HEADS if mem else HEADS
            wid = 2 * S if mem else WID

            def load_table(h):
                if mem or h >= heads:
                    return
                if kind == "fox":
                    src = bass.AP(negc_dram.tensor, h * S, [[0, P], [1, S]])
                else:
                    src = bass.AP(skew_dram.tensor, h * P * GCOLS + P - 1, [[GCOLS - 1, P], [1, S]])
                act.dma_start(t[:, h % 2, :], src).then_inc(table_in[h % 2], 16)

            def exps(h, i):
                act.wait_ge(maxed, b.at("maxed", TB * h + i + 1))
                n = 4 * (h % 2) + i
                row = prob[h % 2][:, offs[i]:offs[i] + widths[i]]
                if mem and i == 0 and h >= 2:
                    act.wait_ge(turned, b.at("turned", h - 1))
                act.activation(row, ps[:, i, 0:widths[i]] if mem else row, ACT.Exp, bias=small[:, 8 + n:9 + n],
                               accum_out=small[:, 16 + n:17 + n]).then_inc(expd, 1)

            def turned_parts(h):
                act.wait_ge(turned, b.at("turned", h + 1))
                if h >= 2:
                    act.wait_ge(weighed, b.at("weighed", h - 1))
                act.activation(pt_hi[h % 2][:, 0:wid], flat(ps[:, 4:7, :], wid), ACT.Copy).then_inc(turned_hi, 1)

            def out_parts(h):
                act.wait_ge(weighed, b.at("weighed", h + 1))
                to, frm = out_of(kind, h, q_hi)
                act.activation(to, frm, ACT.Copy).then_inc(out_hi, 1)

            act.wait_ge(part_lo, b.at("part_lo"))
            if kind == "dil":
                act.wait_ge(skewed, 16)
            load_table(0)
            load_table(1)
            for h in range(heads + 2):
                if h < heads:
                    exps(h, 0)
                    exps(h, 1)
                if 1 <= h <= heads:
                    turned_parts(h - 1)
                if h < heads:
                    exps(h, 2)
                    exps(h, 3)
                    load_table(h + 2)
                if h >= 2:
                    out_parts(h - 2)

        def output():
            act.wait_ge(t_ready, b.at("t_ready", 2 * TB))
            act.dma_start(out[0].rearrange("(i p) d -> p i d", p=P), xnat[:, :, :]).then_inc(stored, 16)

        schedule(b, dict(prologue=prologue, group=group, mem_turn=mem_turn, prep=prep, prep_all=prep_all,
                         layer_norm=layer_norm, gates=gates, gates_load=gates_load, final_norm=final_norm,
                         attend=attend, output=output))

    @block.vector
    def _(dve):
        b = Book(dve)
        rstd2 = rstd[:, :].unsqueeze(1).broadcast_to([P, 2, S])

        def lo_of(to, value, hi):
            return dve.tensor_tensor(to, value, hi.bitcast(F32), ALU.subtract)

        def settle():
            dve.wait_ge(psum_read, b.at("psum_read"))
            dve.wait_ge(t_ready, b.at("t_ready"))
            dve.wait_ge(part_lo, b.at("part_lo"))
            dve.wait_ge(step, b.at("step"))

        def group(kind, src, g, rhs, dst, fresh, tiles, at=0, stats=False, rows=None, width=S, scale=None,
                  bias=None, **_):
            base = 4 * b.parity
            if stats:
                dve.wait_ge(act_side, b.at("act_side", 1))
                dve.reciprocal(rstd[:, :], rstd[:, :]).then_inc(rstd_ready, 1)
            dve.wait_ge(rstd_ready, b.at("rstd_ready", 1 if stats else 0))
            settle()
            dve.wait_ge(tiles_used, b.at("tiles", tiles))
            for a in range(2):
                bank, here = ps[:, base + 2 * a:base + 2 * a + 2, :], t[:, 2 * a:2 * a + 2, :]
                if kind == "add":
                    cs = range(4 * at + 2 * a, 4 * at + 2 * a + 2)
                    if bias:
                        for c in cs:
                            last = dve.scalar_tensor_tensor(out=x[:, c, :], in0=ps[:, base + c - 4 * at, :],
                                                            scalar=column(VECTORS[bias] + c), in1=x[:, c, :],
                                                            op0=ALU.add, op1=ALU.add)
                    else:
                        last = dve.tensor_tensor(x[:, cs[0]:cs[1] + 1, :], bank, x[:, cs[0]:cs[1] + 1, :], ALU.add)
                elif dst in ("km", "vm"):
                    if dst == "km":
                        last = dve.tensor_copy(t[:, 2 * a:2 * a + 2, 0:width], ps[:, base + 2 * a:base + 2 * a + 2, 0:width])
                    else:
                        last = dve.tensor_copy(t[:, a, :], ps[:, base + a, :])
                elif rows:
                    for i in (2 * a, 2 * a + 1):
                        last = dve.tensor_scalar(t[:, i, :], ps[:, base + i, :], small[:, 4 + i:5 + i], None, ALU.mult)
                elif scale:
                    last = dve.scalar_tensor_tensor(out=here, in0=bank, scalar=scale, in1=rstd2, op0=ALU.mult,
                                                    op1=ALU.mult)
                else:
                    last = dve.tensor_tensor(here, bank, rstd2, ALU.mult)
                last.then_inc(psum_read, 1)
            if kind == "glu":
                dve.wait_ge(psum_read, b.at("psum_read", 2))
                dve.wait_ge(gated, b.at("gated", 1))
                for a in range(2):
                    c = 2 * at + a
                    last = dve.scalar_tensor_tensor(out=u_pad[:, c, PAD:PAD + S], in0=t[:, 2 + a, :],
                                                    scalar=column(VECTORS["conv_pw1_b"] + c), in1=t[:, a, :],
                                                    op0=ALU.add, op1=ALU.mult)
                last.then_inc(t_ready, 1)
            if kind == "gate":
                dve.wait_ge(psum_read, b.at("psum_read", 2))
                dve.wait_ge(gated, b.at("gated", 1))
                dve.tensor_tensor(t[:, 2:4, :], t[:, 0:2, :], t[:, 2:4, :], ALU.mult).then_inc(t_ready, 1)
                dve.wait_ge(part_hi, b.at("part_hi", 1))
                cs = slice(2 * at, 2 * at + 2)
                lo_of(mid_lo[:, cs, :], t[:, 2:4, :], mid_hi[:, cs, :]).then_inc(part_lo, 1)
            if kind in ("relu2", "bmul"):
                for a in range(2):
                    here, cs = t[:, 2 * a:2 * a + 2, :], slice(4 * at + 2 * a, 4 * at + 2 * a + 2)
                    dve.wait_ge(psum_read, b.at("psum_read", a + 1))
                    if kind == "relu2":
                        last = dve.scalar_tensor_tensor(out=here, in0=here, scalar=0.0, in1=here, op0=ALU.max,
                                                        op1=ALU.mult)
                    else:
                        last = dve.tensor_tensor(here, here, y2[:, cs, :], ALU.mult)
                    last.then_inc(t_ready, 1)
                for a in range(2):
                    here, cs = t[:, 2 * a:2 * a + 2, :], slice(4 * at + 2 * a, 4 * at + 2 * a + 2)
                    dve.wait_ge(part_hi, b.at("part_hi", a + 1))
                    lo_of(mid_lo[:, cs, :], here, mid_hi[:, cs, :]).then_inc(part_lo, 1)
            if kind == "proj":
                for a, ((to, frm), (hi, _f)) in enumerate(zip(proj_parts(dst, 1, at, width), proj_parts(dst, 0, at, width))):
                    dve.wait_ge(part_hi, b.at("part_hi", a + 1))
                    lo_of(to, frm, hi).then_inc(part_lo, 1)
            if kind == "cu":
                dve.wait_ge(psum_read, b.at("psum_read", 2))
                if at == 0:
                    dve.memset(z_pad[:, :, 0:2], 0.0)
                dve.tensor_tensor(z_pad[:, :, 2:2 + S], t[:, 0:2, :], t[:, 2:4, :], ALU.mult).then_inc(step, 1)
                for k in range(3):
                    dve.wait_ge(step, b.at("step", k + 1))
                    for a in range(2):
                        c = 2 * at + a
                        w = column(VECTORS["conv_kernel_2"] + DC * k + c)
                        if k == 0:
                            last = dve.tensor_scalar(y2[:, c, :], z_pad[:, a, 0:S], w, None, ALU.mult)
                        else:
                            last = dve.scalar_tensor_tensor(out=y2[:, c, :], in0=z_pad[:, a, k:k + S], scalar=w,
                                                            in1=y2[:, c, :], op0=ALU.mult, op1=ALU.add)
                    last.then_inc(step, 1)

        def prologue():
            dve.memset(small[:, 40:41], RMS_EPS)
            dve.memset(small[:, 41:42], LN_EPS)
            dve.wait_ge(pe_side, 1)
            dve.tensor_copy(vec[:, :], ps[:, 0, 0:n_rows]).then_inc(step, 1)
            dve.wait_ge(pe_side, 2)
            dve.wait_ge(rows_in, ROWS_IN)
            dve.tensor_tensor(g_tab[:, :], flat(ps[0:HEADS, 1:3, :], GCOLS), g_log[:, :], ALU.add).then_inc(step, 1)
            for p in range(4):
                dve.wait_ge(pe_side, 2 + 2 * p + 2)
                dve.tensor_copy(x[:, 2 * p:2 * p + 2, :], ps[:, 2 * p:2 * p + 2, :]).then_inc(psum_read, 1)
            dve.memset(u_pad[:, :, 0:PAD], 0.0).then_inc(step, 1)

        def mem_turn(layer):
            dve.wait_ge(act_side, b.at("act_side", 3))
            dve.reciprocal(small[:, 2:4], small[:, 2:4]).then_inc(step, 1)
            dve.wait_ge(step, b.at("step", 1))
            for i in range(MB):
                dve.tensor_scalar(memn[:, i, :], memn[:, i, :], small[:, 2 + i:3 + i], None, ALU.mult).then_inc(step, 1)
            for m in range(4):
                dve.wait_ge(part_hi, b.at("part_hi", m + 1))
                for a in range(2):
                    c = 2 * m + a
                    last = dve.scalar_tensor_tensor(
                        out=hm_lo[:, c, :], in0=ps[:, m, a * MEM:(a + 1) * MEM],
                        scalar=column(VECTORS["norm_memsrc_g"] + DC * layer + c), in1=hm_hi[:, c, :].bitcast(F32),
                        op0=ALU.mult, op1=ALU.subtract)
                last.then_inc(part_lo, 1)

        def take(p, a, done):
            if p == 0:
                dve.tensor_tensor(acc[:, :], t[:, a, :], t[:, a + 1, :], ALU.add).then_inc(step, 1)
                return done + 1
            dve.tensor_tensor(t[:, a, :], t[:, a, :], t[:, a + 1, :], ALU.add).then_inc(step, 1)
            dve.wait_ge(step, b.at("step", done + 1))
            dve.tensor_tensor(acc[:, :], acc[:, :], t[:, a, :], ALU.add).then_inc(step, 1)
            return done + 2

        def prep(gain, first, n, split, squares=True, whole=False):
            done = 0
            for m in range(n):
                p = first + m
                if not whole:
                    dve.wait_ge(psum_read, b.at("psum_read", m + 1 - n))
                if split:
                    dve.wait_ge(part_hi, b.at("part_hi", m + 1))
                    for c in (2 * p, 2 * p + 1):
                        last = dve.scalar_tensor_tensor(out=h_lo[:, c, :], in0=x[:, c, :], scalar=column(gain + c),
                                                        in1=h_hi[:, c, :].bitcast(F32), op0=ALU.mult, op1=ALU.subtract)
                    last.then_inc(part_lo, 1)
                if squares:
                    dve.wait_ge(squared, b.at("squared", m + 1))
                    done = take(p, 2 * (p % 2), done)

        def prep_all(gain, squares=True):
            dve.wait_ge(psum_read, b.at("psum_read"))
            dve.wait_ge(step, b.at("step"))
            prep(gain, 0, 4, True, squares, whole=True)

        def conv_taps(g):
            cs = (2 * g, 2 * g + 1)
            w = VECTORS["conv_dw_w"]
            dve.wait_ge(t_ready, b.at("t_ready"))
            for c in cs:
                dve.tensor_scalar(conv[:, c, :], u_pad[:, c, 0:S], column(w + c), column(VECTORS["conv_dw_b"] + c),
                                  ALU.mult, ALU.add).then_inc(step, 1)
            now = b.at("step")
            with dve.Fori(1, TAPS) as k:
                for a, c in enumerate(cs):
                    dve.wait_ge(step, k * 2 + (now + a - 1))
                    dve.scalar_tensor_tensor(out=conv[:, c, :], in0=u_pad[:, c, bass.ds(k, S)],
                                             scalar=vec[:, bass.ds(k * DC + (w + c), 1)], in1=conv[:, c, :],
                                             op0=ALU.mult, op1=ALU.add).then_inc(step, 1)

        def layer_norm():
            dve.wait_ge(step, b.at("step"))
            for m in range(LN_MEAN):
                dve.tensor_tensor(acc[:, :], conv[:, 0, :] if m == 0 else acc[:, :], conv[:, m + 1, :],
                                  ALU.add).then_inc(step, 1)
                dve.wait_ge(step, b.at("step", m + 1))
            done = LN_MEAN
            dve.wait_ge(pe_side, b.at("pe_side", 1))
            dve.tensor_scalar(t[:, 0, :], ps[:, 0, :], 1.0 / D, None, ALU.mult).then_inc(step, 1)
            done += 1
            dve.wait_ge(step, b.at("step", done))
            mean2 = t[:, 0, :].unsqueeze(1).broadcast_to([P, 2, S])
            for p in range(4):
                c = conv[:, 2 * p:2 * p + 2, :]
                dve.tensor_tensor(c, c, mean2, ALU.subtract).then_inc(step, 1)
                done += 1
            for p in range(4):
                dve.wait_ge(squared, b.at("squared", p + 1))
                done = take(p, 2, done)
            dve.wait_ge(act_side, b.at("act_side", 1))
            dve.reciprocal(rstd[:, :], rstd[:, :]).then_inc(rstd_ready, 1)
            dve.wait_ge(rstd_ready, b.at("rstd_ready", 1))
            for p in range(4):
                c = conv[:, 2 * p:2 * p + 2, :]
                dve.tensor_tensor(c, c, rstd2, ALU.mult).then_inc(step, 1)
            for p in range(4):
                cs = slice(2 * p, 2 * p + 2)
                dve.wait_ge(part_hi, b.at("part_hi", p + 1))
                lo_of(mid_lo[:, cs, :], conv[:, cs, :], mid_hi[:, cs, :]).then_inc(part_lo, 1)

        def columns():
            dve.wait_ge(pe_side, b.at("pe_side", 1))
            dve.tensor_copy(small[:, 4:8], ps[:, 4 * b.parity, :].rearrange("p (i s) -> p i s", i=TB)[:, :, 0]
                            ).then_inc(step, 1)
            dve.wait_ge(step, b.at("step", 1))

        def gates():
            dve.wait_ge(psum_read, b.at("psum_read"))
            dve.memset(wf_hi[:, :, :].bitcast(F32), 0.0)
            dve.memset(wf_lo[:, :, :].bitcast(F32), 0.0).then_inc(step, 1)
            dve.wait_ge(act_side, b.at("act_side", 1))
            lo_of(wf_lo[:, :, 0:HEADS], wf[:, :, :], wf_hi[:, :, 0:HEADS]).then_inc(step, 1)
            dve.wait_ge(pe_side, b.at("pe_side", 1))
            dve.tensor_tensor(f_t[:, 0, :], ps[0:HEADS, 4 * b.parity, :], rstd[0:HEADS, :], ALU.mult).then_inc(step, 1)
            dve.wait_ge(step, b.at("step", 3))
            dve.wait_ge(gates_in, 32)
            dve.tensor_scalar(f_t[:, 0, :], f_t[:, 0, :], small[0:HEADS, 50:51], None, ALU.add).then_inc(step, 1)
            dve.wait_ge(step, b.at("step", 4))
            dve.tensor_scalar(f_t[:, 2, :], f_t[:, 0, :], -1.0, 0.0, ALU.mult, ALU.max).then_inc(step, 1)
            dve.wait_ge(act_side, b.at("act_side", 4))
            dve.wait_ge(step, b.at("step", 5))
            dve.tensor_tensor_scan(f_t[:, 3, :], f_t[:, 1, :], f_t[:, 2, :], initial=0.0, op0=ALU.add,
                                   op1=ALU.add).then_inc(step, 1)

        def final_norm(gain):
            dve.wait_ge(act_side, b.at("act_side", 1))
            dve.reciprocal(rstd[:, :], rstd[:, :]).then_inc(rstd_ready, 1)
            dve.wait_ge(rstd_ready, b.at("rstd_ready", 1))
            dve.wait_ge(psum_read, b.at("psum_read"))
            for c in range(DC):
                last = dve.scalar_tensor_tensor(out=x[:, c, :], in0=x[:, c, :], scalar=column(gain + c),
                                                in1=rstd[:, :], op0=ALU.mult, op1=ALU.mult)
                if c % 2:
                    last.then_inc(step, 1)

        def attend(kind):
            offs, widths, keys, pt = attention_shape(kind)
            mem = kind == "mem"
            heads = MEM_HEADS if mem else HEADS
            wid = 2 * S if mem else WID

            def shift(h, i):
                row, w, n = prob[h % 2][:, offs[i]:offs[i] + widths[i]], widths[i], 4 * (h % 2) + i
                if i == 0 and not mem:
                    if h >= 2:
                        dve.wait_ge(turned, b.at("turned", h - 1))
                    dve.wait_ge(table_in[h % 2], 16 * (b.count.get("tables", 0) + h // 2 + 1))
                if i == 0 and kind == "fox":
                    dve.wait_ge(masked, b.at("masked", h + 1))
                dve.wait_ge(scored, b.at("scored", TB * h + i + 1))
                if not mem:
                    if kind == "dil":
                        last = dve.tensor_tensor(row, ps[:, i, 0:w], t[:, h % 2, S - w:S], ALU.add)
                    else:
                        if i:
                            dve.tensor_tensor(row[:, 0:w - P], ps[:, i, 0:w - P], t[:, h % 2, 0:w - P], ALU.add)
                        last = dve.tensor_tensor(row[:, w - P:w], ps[:, i, w - P:w],
                                                 t[:, 2 + h % 2, i * P:(i + 1) * P], ALU.add)
                    last.then_inc(shifted, 1)
                    dve.wait_ge(shifted, b.at("shifted", TB * h + i + 1))
                dve.reduce_max(small[:, 8 + n:9 + n], ps[:, i, 0:w] if mem else row, AX_X, negate=True).then_inc(maxed, 1)

            def over_sum(h, i):
                n = 4 * (h % 2) + i
                dve.wait_ge(expd, b.at("expd", TB * h + i + 1))
                dve.reciprocal(small[:, 24 + n:25 + n], small[:, 16 + n:17 + n]).then_inc(summed, 1)
                if i == TB - 1:
                    row = prob[h % 2][:, offs[i]:offs[i] + widths[i]]
                    dve.wait_ge(summed, b.at("summed", TB * h + i + 1))
                    dve.tensor_scalar(row, row, small[:, 24 + n:25 + n], None, ALU.mult).then_inc(normed_last, 1)

            def turned_parts(h):
                dve.wait_ge(turned_hi, b.at("turned_hi", h + 1))
                lo_of(pt_lo[h % 2][:, 0:wid], flat(ps[:, 4:7, :], wid), pt_hi[h % 2][:, 0:wid]).then_inc(turned_lo, 1)

            def out_parts(h):
                dve.wait_ge(out_hi, b.at("out_hi", h + 1))
                to, frm = out_of(kind, h, q_lo)
                lo_of(to, frm, out_of(kind, h, q_hi)[0]).then_inc(out_lo, 1)

            for h in range(heads + 2):
                if h < heads:
                    shift(h, 0)
                    shift(h, 1)
                    over_sum(h, 0)
                    shift(h, 2)
                    over_sum(h, 1)
                    shift(h, 3)
                    over_sum(h, 2)
                if 1 <= h <= heads:
                    turned_parts(h - 1)
                if h < heads:
                    over_sum(h, 3)
                if h >= 2:
                    out_parts(h - 2)

        def output():
            for n in range(2 * TB):
                dve.wait_ge(pe_side, b.at("pe_side", n + 1))
                dve.tensor_copy(xnat[:, n // 2, S * (n % 2):S * (n % 2) + S], ps[:, n, :]).then_inc(t_ready, 1)

        schedule(b, dict(prologue=prologue, group=group, mem_turn=mem_turn, prep=prep, prep_all=prep_all,
                         conv=conv_taps, layer_norm=layer_norm, gates=gates, columns=columns,
                         final_norm=final_norm, attend=attend, output=output))


INPUTS = ["x", "mem", "norm_mix_g", "norm_mem_g", "norm_memsrc_g", "norm_ff_g", "mem_wq", "mem_wk", "mem_wv",
          "mem_wo", "ff_w1", "ff_w2", "conv_pw1_w", "conv_pw1_b", "conv_dw_w", "conv_dw_b", "conv_ln_g",
          "conv_ln_b", "conv_pw2_w", "conv_pw2_b", "kv_norm_g", "kvf_w", "fgate_b", "fox_wq", "fox_wo",
          "final_norm_g", "mix_norm_2", "ffn_norm_2", "final_norm_2", "conv_w_in_2", "conv_kernel_2",
          "conv_w_out_2", "attn_w_qkv_2", "attn_w_out_2", "rel_bias_2", "ffn_w_gate_2", "ffn_w_up_2",
          "ffn_w_down_2"]


def kernel(**inputs):
    import concourse.bacc as bacc
    from concourse.bass_utils import run_bass_kernel_spmd

    nc = bacc.Bacc("TRN2", target_bir_lowering=False, num_devices=1)
    arrays, aps = {}, {}
    for name in INPUTS:
        a = np.ascontiguousarray(inputs[name])
        arrays[f"in_{name}"] = a
        aps[name] = nc.dram_tensor(f"in_{name}", a.shape, mybir.dt.from_np(a.dtype), kind="ExternalInput").ap()
    out = nc.dram_tensor("out", (1, S, D), F32, kind="ExternalOutput").ap()
    build(nc, aps, out)
    r = run_bass_kernel_spmd(nc, [arrays], core_ids=[0])
    return r.results[0]["out"]
```

```python
from contextlib import ExitStack, contextmanager

import numpy as np

import concourse.bass as bass
from concourse import mybir

P = 128
F32 = mybir.dt.float32
F32R = mybir.dt.float32r
ALU = mybir.AluOpType
ACT = mybir.ActivationFunctionType
AX_X = mybir.AxisListType.X

D = 1024
S = 512
DC = D // P
TB = S // P
MEM = 256
MB = MEM // P
D_FF = 4 * D
D_FF2 = 2816
TAPS = 31
PAD = TAPS - 1
DVE_PAIRS = 3
ROUNDS = [(0, 5), (5, 5), (10, 5), (15, 4), (19, 4), (23, 4), (27, 4)]
HEADS, HEAD_DIM = 16, 64
MEM_HEADS, MEM_HEAD_DIM = 4, 256
BUCKETS, MAX_DISTANCE = 32, 2048
BRANCHES = ((128, 1), (512, 4), (2048, 16))
RMS_EPS, LN_EPS = 1e-6, 1e-5
MASKED = -2.0 ** 100

SLOTS = 4
COLS = 512
GCOLS = 640
SBUF_BASE = 16640

GROUP = {
    "relu2": dict(psum_read=2, t_ready=2, part_hi=2, part_lo=2),
    "gate": dict(psum_read=2, gated=1, t_ready=1, part_hi=1, part_lo=1),
    "glu": dict(psum_read=2, gated=1, t_ready=1),
    "glu_split": dict(psum_read=2, gated=1, t_ready=1, part_hi=1, part_lo=1),
    "cu": dict(psum_read=2, step=4),
    "bmul": dict(psum_read=2, t_ready=2, part_hi=2, part_lo=2),
    "proj": dict(psum_read=2, part_hi=2, part_lo=2),
    "add": dict(psum_read=2),
}
STATS = dict(pe_side=1, act_side=1, rstd_ready=1)
MEM_ROWS = dict(act_side=3, step=3)
MEM_TURN = dict(pe_side=4, part_hi=4, part_lo=4)
LN_CENTRE, LN_SQUARES = 1 + 4, 7
LN_CENTRED = dict(pe_side=1, step=LN_CENTRE + LN_SQUARES, squared=4)
LN_SUM = dict(pe_side=1, act_side=1)
LN_SCALED = dict(rstd_ready=1, step=4, gated=4, part_hi=4, part_lo=4)
GATES_SPLIT = dict(act_side=1, step=2)
GATES = dict(pe_side=1, psum_read=2)
GATES_SUM = dict(act_side=3, step=3)
COLUMNS = dict(pe_side=1, step=1)
FINAL_NORM = dict(pe_side=1, act_side=1, rstd_ready=1, step=4)
PROLOGUE = dict(pe_side=2 + DC, psum_read=4, step=3)


def prep_counts(first, n, split=True, squares=True, last=False):
    c = {}
    if split:
        c.update(part_hi=n, part_lo=n)
    if last:
        c.update(part_hi=n)
    if squares:
        c.update(squared=n, step=sum(1 if p == 0 else 2 for p in range(first, first + n)))
    return c


VECTORS = {}


def vector_rows():
    rows, at = [], 0
    for name, n in (("norm_mix_g", 16), ("norm_mem_g", 16), ("norm_memsrc_g", 16), ("norm_ff_g", 16),
                    ("kv_norm_g", 8), ("final_norm_g", 8), ("mix_norm_2", 16), ("ffn_norm_2", 16),
                    ("final_norm_2", 8),
                    ("conv_pw1_b", 16), ("conv_dw_b", 8), ("conv_ln_g", 8), ("conv_ln_b", 8),
                    ("conv_pw2_b", 8), ("conv_kernel_2", 24), ("conv_dw_w", 8 * TAPS)):
        rows.append((name, at, n))
        VECTORS[name] = at
        at += n
    return rows, at


def distance_tables():
    d = (S - 1) - np.arange(GCOLS)
    exact = BUCKETS // 2
    df = np.maximum(d, 1).astype(np.float32)
    large = exact + (np.log(df / np.float32(exact)) / np.float32(np.log(MAX_DISTANCE / exact))
                     * np.float32(BUCKETS - exact)).astype(np.int32)
    bucket = np.where(d < exact, d, np.minimum(large, BUCKETS - 1))
    onehot = np.zeros((BUCKETS, GCOLS), np.float32)
    count = np.zeros(GCOLS)
    for window, dilation in BRANCHES:
        count += (d >= 0) & (d % dilation == 0) & (d // dilation <= window // dilation)
    for m in range(GCOLS):
        if d[m] >= 0:
            onehot[bucket[m], m] = 1.0
    logcount = np.where(count > 0, np.log(np.maximum(count, 1)), MASKED).astype(np.float32)
    return onehot, np.tile(logcount[None, :], (HEADS, 1))


class Book:

    def __init__(self, eng):
        self.eng, self.count, self.index, self.per, self.parity = eng, {}, None, {}, 0

    def at(self, name, more=0):
        v = max(self.count.get(name, 0) + more, 0)
        return v if self.index is None else v + self.index * self.per.get(name, 0)

    def add(self, **more):
        for k, v in more.items():
            self.count[k] = self.count.get(k, 0) + v

    @contextmanager
    def loop(self, n, per):
        before = dict(self.count)
        if self.eng is None:
            yield 0
        else:
            with self.eng.Fori(0, n) as i:
                self.index, self.per = i, per
                yield i
        for k in set(self.count) | set(per):
            assert self.count.get(k, 0) - before.get(k, 0) == per.get(k, 0), (k, per)
            self.count[k] = before.get(k, 0) + n * per.get(k, 0)
        self.index, self.per = None, {}


def group_counts(kind, tiles, columns=False, reprep=None, **_):
    c = {**GROUP[kind], "tiles": tiles}
    if columns:
        c.update(COLUMNS)
    if reprep is not None:
        c.update({k: c[k] + 4 for k in ("part_hi", "part_lo")})
    return c


def attention_shape(kind):
    if kind == "mem":
        return [MEM * i for i in range(TB)], [MEM] * TB, (lambda i: range(MB)), [(0, 0), (S, 0)]
    return ([0, 128, 384, 768], [(i + 1) * P for i in range(TB)], (lambda i: range(i + 1)),
            [(0, 0), (512, 128), (1024, 256), (896, 384)])


def attention_counts(kind):
    n = MEM_HEADS if kind == "mem" else HEADS
    c = {k: TB * n for k in ("scored", "maxed", "expd", "summed")}
    c["normed"] = (TB - 1) * n
    c.update({k: n for k in ("normed_last", "turned", "turned_hi", "turned_lo", "weighed", "out_hi", "out_lo")})
    if kind != "mem":
        c.update(tables=n // 2, shifted=TB * n)
    return c


def schedule(b, e):

    def do(step, counts, *args, **kw):
        if step in e:
            e[step](*args, **kw)
        b.add(**counts)

    def groups(kind, src, rhs, dst=None, first=False, tiles=4, g=0, n=1, c0=None, **kw):
        for i in range(n):
            do("group", group_counts(kind, tiles, **kw), kind, src, g + i, rhs, dst, first and i == 0, tiles,
               at=(g if c0 is None else c0) + i, **kw)
            b.parity ^= 1

    def normed(kind, src, rhs, dst=None, n=1, **kw):
        do("group", {**group_counts(kind, 4), **STATS}, kind, src, 0, rhs, dst, True, 4, at=0, stats=True, **kw)
        b.parity ^= 1
        groups(kind, src, rhs, dst, n=n - 1, g=1, **kw)

    def add(src, rhs, gain=None, tiles=4, fresh=True, bias=None, row0=0, split=True,
            last=False):
        for g in range(2):
            do("group", group_counts("add", tiles), "add", src, g, rhs, None, fresh and g == 0, tiles,
               at=g, bias=bias, row0=row0)
            b.parity ^= 1
            if gain is not None:
                do("prep", prep_counts(2 * g, 2, split, last=last), gain, 2 * g, 2, split, last=last)

    def mem_kv_groups(layer):
        return [lambda g=g: groups("proj", f"mem_wk{layer}", "hm", "km", g=g, width=MEM, settled=layer == 1)
                for g in range(2)] + \
               [lambda g=g, **kw: groups("proj", f"mem_wv{layer}", "hm", "vm", g=g, rows=MB, **kw)
                for g in range(2)]

    def mem_attention(layer, next_gain):
        normed("proj", f"mem_wq{layer}", "h", "q", n=2, scale=MEM_HEAD_DIM ** -0.5)
        do("attend", attention_counts("mem"), "mem", layer)
        add(f"mem_wo{layer}", "q", gain=next_gain, fresh=False)

    def ff(layer, next_gain, split=True):
        up, down = f"ff_w1{layer}", f"ff_w2{layer}"
        rounds = D_FF // D
        per_round = {}
        for part in (group_counts("relu2", 4), group_counts("relu2", 4),
                     group_counts("add", 4), group_counts("add", 4)):
            for k, v in part.items():
                per_round[k] = per_round.get(k, 0) + v
        normed("relu2", up, "h", "mid", n=2)
        add(down, "mid")
        with b.loop(rounds - 2, per_round) as i:
            groups("relu2", up, "h", "mid", g=2 * i + 2, n=2, c0=0)
            add(down, "mid", row0=(i + 1) * D)
        groups("relu2", up, "h", "mid", g=2 * (rounds - 1), n=2, c0=0)
        add(down, "mid", gain=next_gain, row0=(rounds - 1) * D, split=split)

    def swiglu(layer, next_gain, last=False):
        src, down = f"glu2{layer}", f"down2{layer}"
        normed("gate", src, "h", "mid", n=4)
        add(down, "mid")
        groups("gate", src, "h", "mid", g=4, n=4, c0=0)
        add(down, "mid", row0=D)
        rest = (D_FF2 - 2 * D) // 256
        groups("gate", src, "h", "mid", g=8, n=rest, c0=0)
        add(down, "mid", gain=next_gain, tiles=rest, row0=2 * D, split=not last, last=last)

    def gain(name, layer=0):
        return VECTORS[name] + DC * layer

    def mem_turn(layer):
        do("mem_turn", MEM_TURN, layer)
        b.parity ^= 1

    pair_taps = [(p, k) for p in range(DVE_PAIRS) for k in range(TAPS)]

    def taps(n):
        while n and pair_taps:
            p, k = pair_taps[0]
            m = min(n, TAPS - k)
            del pair_taps[:m]
            n -= m
            do("conv", dict(step=2 * m), p, k, m)

    do("prologue", PROLOGUE)
    do("prep", prep_counts(0, 4), gain("norm_mix_g"), 0, 4, True)
    do("mem_rows", MEM_ROWS)
    normed("glu", "pw1", "h")
    mem_turn(1)
    taps(10)
    groups("glu", "pw1", "h", g=1, after_turn=True)
    do("skew", {})
    for n, group in zip((4, 6, 6, 6), mem_kv_groups(1)):
        taps(n)
        group()
    mem_turn(0)
    taps(12)
    groups("glu", "pw1", "h", g=2, after_turn=True)
    do("keys_out", {})
    do("diag_hi_first", {})
    taps(13)
    groups("glu_split", "pw1", "h", g=3, settled=True)
    do("diag_lo_first", {})
    keys0, keys1, values0, values1 = mem_kv_groups(0)
    taps(4)
    keys0()
    taps(6)
    keys1()
    taps(DVE_PAIRS * TAPS)
    do("conv_pe", dict(psum_read=2))
    b.parity ^= 1
    do("ln_centred", LN_CENTRED)
    values0()
    do("ln_sum", LN_SUM)
    do("ln_scaled", LN_SCALED)
    values1(ahead=False)
    add("pw2", "mid", gain=gain("norm_mem_g"), bias="conv_pw2_b")
    mem_attention(0, gain("norm_ff_g"))
    ff(0, gain("kv_norm_g"))
    do("gates_load", {})
    normed("proj", "fox_k", "h", "k")
    do("gates_split", GATES_SPLIT)
    groups("proj", "fox_k", "h", "k", g=1, columns=True)
    do("gates", GATES)
    b.parity ^= 1
    do("gates_sum", GATES_SUM)
    groups("proj", "fox_v", "h", "v", rows=TB)
    groups("proj", "fox_v", "h", "v", g=1, rows=TB, reprep=gain("norm_mix_g", 1))
    do("gates_out", {})
    groups("proj", "fox_wq", "h", "q", n=2, first=True, since=2, scale=HEAD_DIM ** -0.5)
    do("attend", attention_counts("fox"), "fox")
    do("keys_back", {})
    add("fox_wo", "q", gain=gain("norm_mem_g", 1), fresh=False)
    mem_attention(1, gain("norm_ff_g", 1))
    ff(1, gain("final_norm_g"), split=False)
    do("final_norm", FINAL_NORM, gain("final_norm_g"))
    do("prep_all", prep_counts(0, 4), gain("mix_norm_2"))
    normed("cu", "conv_cu", "h", n=4)
    groups("bmul", "conv_b", "h", "mid", n=2)
    add("conv_out", "mid", gain=gain("ffn_norm_2"))
    swiglu(0, gain("mix_norm_2", 1))
    normed("proj", "dil_q", "h", "q", n=2, scale=HEAD_DIM ** -0.5)
    groups("proj", "dil_k", "h", "k")
    groups("proj", "dil_k", "h", "k", g=1, columns=True)
    groups("proj", "dil_v", "h", "v", n=2, rows=TB)
    do("attend", attention_counts("dil"), "dil")
    add("dil_out", "q", gain=gain("ffn_norm_2", 1), fresh=False)
    swiglu(1, gain("final_norm_2"), last=True)
    do("output", {})


def build(nc, A, out):
    with ExitStack() as ctx:
        build_in(nc, A, out, ctx)


def build_in(nc, A, out, ctx):
    def sem(name):
        return ctx.enter_context(nc.semaphore(name))

    KB = 1024
    place = [SBUF_BASE]

    def region(nbytes):
        place[0] += nbytes
        assert place[0] <= nc.sbuf_usable_end
        return place[0] - nbytes

    def at(name, shape, dt, offset):
        return nc.alloc_sbuf_tensor_at(name, shape, dt, offset=offset)

    rows, n_rows = vector_rows()
    R_X, R_H, R_MID = region(16 * KB), region(32 * KB), region(32 * KB)
    R_ST, R_W = region(16 * KB), region(32 * KB)
    R_A0, R_A1, R_T = region(32 * KB), region(32 * KB), region(8 * KB)

    x = at("x", [P, DC, S], F32, R_X)
    h_hi, h_lo = at("h_hi", [P, DC, S], F32R, R_H), at("h_lo", [P, DC, S], F32R, R_H + 16 * KB)
    mid_hi, mid_lo = at("mid_hi", [P, DC, S], F32R, R_MID), at("mid_lo", [P, DC, S], F32R, R_MID + 16 * KB)
    stage = at("stage", [P, SLOTS, 2, COLS], F32, R_ST)
    w_hi = at("w_hi", [P, SLOTS, 2, COLS], F32R, R_W)
    w_lo = at("w_lo", [P, SLOTS, 2, COLS], F32R, R_W + 16 * KB)
    q_hi, q_lo = at("q_hi", [P, DC, S], F32R, R_A0), at("q_lo", [P, DC, S], F32R, R_A0 + 16 * KB)
    k_hi, k_lo = at("k_hi", [P, DC, S], F32R, R_A1), at("k_lo", [P, DC, S], F32R, R_A1 + 16 * KB)
    t = at("t", [P, 4, S], F32, R_T)
    rstd, acc = at("rstd", [P, S], F32, region(2 * KB)), at("acc", [P, S], F32, region(2 * KB))
    ident, ones = at("ident", [P, P], F32, region(512)), at("ones", [P, P], F32, region(512))
    mask = at("mask", [P, P], F32, region(512))
    vec = at("vec", [P, n_rows], F32, region((n_rows * 4 + 31) // 32 * 32))
    small = at("small", [P, 64], F32, region(256))
    xnat = at("xnat", [P, TB, D], F32, R_MID)
    vrow = at("vrow", [P, 4, P], F32, R_A0)
    g_tab = at("g_tab", [HEADS, GCOLS], F32, R_A1)
    g_log = at("g_log", [HEADS, GCOLS], F32, R_A1 + 3 * KB)
    onehot_sb = at("onehot_sb", [BUCKETS, GCOLS], F32, R_A1 + 6 * KB)
    relb = at("relb", [BUCKETS, HEADS], F32, R_A1 + 9 * KB)
    memn = at("memn", [P, MB, D], F32, R_A0 + 8 * KB)
    junk = at("junk", [P, D], F32, R_MID + 28 * KB)
    hm_hi = at("hm_hi", [P, DC, MEM], F32R, R_A0 + 16 * KB)
    hm_lo = at("hm_lo", [P, DC, MEM], F32R, R_A0 + 24 * KB)
    km_hi, km_lo = at("km_hi", [P, DC, MEM], F32R, R_A1), at("km_lo", [P, DC, MEM], F32R, R_A1 + 8 * KB)
    vm_hi, vm_lo = at("vm_hi", [P, MB, D], F32R, R_A1 + 16 * KB), at("vm_lo", [P, MB, D], F32R, R_A1 + 24 * KB)
    u_pad = at("u_pad", [P, 2 * DVE_PAIRS, PAD + S], F32, R_MID)
    u_hi = at("u_hi", [P, 2, PAD + S], F32R, R_MID + 13056)
    u_lo = at("u_lo", [P, 2, PAD + S], F32R, R_MID + 17408)
    diag = at("diag", [P, 2, 2, 5, P], F32R, R_MID + 21760)
    tap_hi, tap_lo = at("tap_hi", [P, 2, TAPS], F32R, R_MID + 32000), at("tap_lo", [P, 2, TAPS], F32, R_MID + 32256)
    conv = at("conv", [P, DC, S], F32, R_A0)
    z_pad, y2 = at("z_pad", [P, 2, 2 + S], F32, R_A1), at("y2", [P, DC, S], F32, R_A0)
    v_hi, v_lo = at("v_hi", [P, TB, D], F32R, R_MID), at("v_lo", [P, TB, D], F32R, R_MID + 16 * KB)
    wf = at("wf", [P, DC, HEADS], F32, R_A0)
    wf_hi, wf_lo = at("wf_hi", [P, DC, P], F32R, R_A0 + 4 * KB), at("wf_lo", [P, DC, P], F32R, R_A0 + 8 * KB)
    f_t = at("f_t", [HEADS, 4, S], F32, R_A0 + 16 * KB)
    WID = 1280
    prob = [at(f"prob{i}", [P, WID], F32, R_H + i * 5 * KB) for i in range(2)]
    ident_r, mask_r = at("ident_r", [P, P], F32R, R_H + 30 * KB), at("mask_r", [P, P], F32R, R_H + 30 * KB + 512)
    pt_hi = [at(f"pt_hi{i}", [P, WID], F32R, R_H + (10 + 10 * i) * KB) for i in range(2)]
    pt_lo = [at(f"pt_lo{i}", [P, WID], F32R, R_H + (15 + 10 * i) * KB) for i in range(2)]

    kv_parts = [part[:, :, :].bitcast(F32).rearrange("p a n -> p (a n)") for part in (km_hi, km_lo, vm_hi, vm_lo)]
    operand = {"h": (h_hi, h_lo), "mid": (mid_hi, mid_lo), "q": (q_hi, q_lo), "k": (k_hi, k_lo),
               "hm": (hm_hi, hm_lo), "km": (km_hi, km_lo), "vm": (vm_hi, vm_lo), "v": (v_hi, v_lo)}

    ps = ctx.enter_context(nc.psum_tensor("ps", [P, 8, S], F32))

    negc_dram = nc.dram_tensor("negc_dram", (HEADS, S), F32, kind="Internal").ap()
    g_dram = nc.dram_tensor("g_dram", (HEADS, GCOLS), F32, kind="Internal").ap()
    skew_dram = nc.dram_tensor("skew_dram", (HEADS, P * GCOLS), F32, kind="Internal").ap()
    keys_dram = nc.dram_tensor("keys_dram", (P, 8 * D), F32, kind="Internal").ap()
    onehot, logcount = distance_tables()
    onehot_c = nc.inline_tensor(onehot, "onehot_c").ap()
    logcount_c = nc.inline_tensor(logcount, "logcount_c").ap()

    tile_loaded = [sem(f"tile_loaded{i}") for i in range(SLOTS)]
    tile_hi, tile_lo = sem("tile_hi"), sem("tile_lo")
    tiles_used = sem("tiles_used")
    psum_read = sem("psum_read")
    t_ready = sem("t_ready")
    gated = sem("gated")
    part_hi, part_lo = sem("part_hi"), sem("part_lo")
    squared = sem("squared")
    step = sem("step")
    pe_side, act_side = sem("pe_side"), sem("act_side")
    rstd_ready = sem("rstd_ready")
    consts = sem("consts")
    tap_parts, diag_hi, diag_lo = sem("tap_parts"), sem("diag_hi"), sem("diag_lo")
    diag_used = sem("diag_used")
    keys_out, keys_back = sem("keys_out"), sem("keys_back")
    rows_in, x_in, mem_in = sem("rows_in"), sem("x_in"), sem("mem_in")
    g_out, skewed, gates_in, negc_out, stored = (sem(n) for n in ("g_out", "skewed", "gates_in", "negc_out", "stored"))
    table_in = [sem("table_in0"), sem("table_in1")]
    scored, shifted, maxed, expd = (sem(n) for n in ("scored", "shifted", "maxed", "expd"))
    summed, turned = sem("summed"), sem("turned")
    normed_p, normed_last = sem("normed"), sem("normed_last")
    turned_hi, turned_lo, weighed = sem("turned_hi"), sem("turned_lo"), sem("weighed")
    out_hi, out_lo = sem("out_hi"), sem("out_lo")

    def column(j):
        return vec[:, j:j + 1]

    def head_rows(h):
        return h * HEAD_DIM // P, slice(h * HEAD_DIM % P, h * HEAD_DIM % P + HEAD_DIM)

    dry = Book(None)
    schedule(dry, {})
    TILES = dry.count["tiles"]

    def loaded_at(b, ahead):
        n = b.count.get("tiles", 0) + ahead
        v = 32 * (n // SLOTS + 1)
        if b.index is not None:
            v = v + b.index * (32 // SLOTS * b.per["tiles"])
        return n % SLOTS, v

    def flat(banks, n):
        return banks.rearrange("p b s -> p (b s)")[:, 0:n]

    def proj_parts(dst, lo, at, width):
        to = operand[dst][lo]
        c = slice(S * at, S * at + S)
        if dst == "vm":
            return [(to[:, a, c], t[:, a, :]) for a in range(2)]
        if dst == "v":
            return [(to[:, 2 * a:2 * a + 2, c], t[:, 2 * a:2 * a + 2, :]) for a in range(2)]
        return [(to[:, 4 * at + 2 * a:4 * at + 2 * a + 2, :], t[:, 2 * a:2 * a + 2, 0:width]) for a in range(2)]

    def out_of(kind, h, q):
        if kind == "mem":
            return q[:, 2 * h:2 * h + 2, :], ps[:, 6:8, :]
        c, r = head_rows(h)
        return q[r, c, :], ps[r, 7, :]

    row_loads = []
    for name, first, n in rows:
        flat_ap = A[name].rearrange("(a b) -> a b", b=P) if len(A[name].shape) == 1 else \
            A[name].rearrange("a (b c) -> (a b) c", c=P) if len(A[name].shape) == 2 else \
            A[name][0].rearrange("a (b c) -> (a b) c", c=P)
        done = 0
        while done < n:
            r = first + done
            m = min(n - done, P - r % P)
            row_loads.append((vrow[r % P:r % P + m, r // P, :], (flat_ap[done:done + m, :], m)))
            done += m
    row_loads += [(relb[:, :], (A["rel_bias_2"], 0)), (onehot_sb[:, :], (onehot_c, 0)), (g_log[:, :], (logcount_c, 0))]
    ROWS_IN = 16 * len(row_loads)
    HALF = len(row_loads) // 2

    block = ctx.enter_context(nc.Block())

    @block.sync
    def _(sp):
        b = Book(sp)

        def plain(w):
            def src(g, j, row0):
                return [(stage_at[:, a, :], w[bass.ds(row0 + (2 * j + a) * P, P), bass.ds(g * COLS, COLS)])
                        for a in (0, 1)]
            return src

        def pair(wa, wb, off_a=0, off_b=0):
            def src(g, j, row0):
                return [(stage_at[:, :, 256 * n:256 * n + 256],
                         w[2 * j * P:2 * (j + 1) * P, off + g * 256:off + (g + 1) * 256]
                         .rearrange("(a p) n -> p a n", p=P))
                        for n, (w, off) in enumerate(((wa, off_a), (wb, off_b)))]
            return src

        src_of = {"pw1": pair(A["conv_pw1_w"][0], A["conv_pw1_w"][0], D, 0), "pw2": plain(A["conv_pw2_w"][0]),
                  "fox_k": plain(A["kvf_w"][:, 0:D]), "fox_v": plain(A["kvf_w"][:, D:2 * D]),
                  "fox_wq": plain(A["fox_wq"][0]), "fox_wo": plain(A["fox_wo"][0]),
                  "conv_cu": pair(A["conv_w_in_2"][0], A["conv_w_in_2"][0], D, 2 * D),
                  "conv_b": plain(A["conv_w_in_2"][0][:, 0:D]), "conv_out": plain(A["conv_w_out_2"][0]),
                  "dil_q": plain(A["attn_w_qkv_2"][0][:, 0:D]), "dil_k": plain(A["attn_w_qkv_2"][0][:, D:2 * D]),
                  "dil_v": plain(A["attn_w_qkv_2"][0][:, 2 * D:3 * D]), "dil_out": plain(A["attn_w_out_2"][0])}
        for layer in range(2):
            for n in ("mem_wq", "mem_wk", "mem_wv", "mem_wo", "ff_w1", "ff_w2"):
                src_of[f"{n}{layer}"] = plain(A[n][layer])
            src_of[f"glu2{layer}"] = pair(A["ffn_w_gate_2"][layer], A["ffn_w_up_2"][layer])
            src_of[f"down2{layer}"] = plain(A["ffn_w_down_2"][layer])

        def group(kind, src, g, rhs, dst, fresh, tiles, row0=0, **_):
            nonlocal stage_at
            for j in range(tiles):
                slot, _v = loaded_at(b, j)
                stage_at = stage[:, slot]
                sp.wait_ge(tile_lo, b.at("tiles", j - SLOTS + 1))
                for to, frm in src_of[src](g, j, row0):
                    sp.dma_start(to, frm).then_inc(tile_loaded[slot], 16)

        def prologue():
            for r, (frm, n) in row_loads[HALF:]:
                sp.dma_start(r, frm).then_inc(rows_in, 16)

        stage_at = None
        def output():
            for i in range(TB):
                sp.wait_ge(t_ready, b.at("t_ready", i + 1))
                sp.wait_ge(gated, b.at("gated", i + 1))
                sp.dma_start(out[0, i * P:(i + 1) * P, :], xnat[:, i, :]).then_inc(stored, 16)

        schedule(b, dict(prologue=prologue, group=group, output=output))
        sp.wait_ge(stored, 16 * TB)

    @block.gpsimd
    def _(pool):
        b = Book(pool)
        pool.memset(ones[:, :], 1.0)
        pool.memset(ident[:, :], 0.0)
        pool.memset(mask[:, :], 0.0).then_inc(consts, 1)
        pool.wait_ge(consts, 1)
        pool.affine_select(out=ident[:, :], in_=ident[:, :], compare_op=ALU.not_equal, fill=1.0,
                           base=0, pattern=[[-1, P]], channel_multiplier=1)
        pool.affine_select(out=mask[:, :], in_=mask[:, :], compare_op=ALU.is_ge, fill=MASKED,
                           base=0, pattern=[[-1, P]], channel_multiplier=1).then_inc(consts, 1)

        def group(kind, src, g, rhs, dst, fresh, tiles, **_):
            for j in range(tiles):
                slot, _v = loaded_at(b, j)
                pool.wait_ge(tile_hi, b.at("tiles", j + 1))
                pool.tensor_tensor(w_lo[:, slot], stage[:, slot], w_hi[:, slot].bitcast(F32),
                                   ALU.subtract).then_inc(tile_lo, 1)

        def diag_lo_first():
            pool.wait_ge(tap_parts, 1)
            taps = vec[:, VECTORS["conv_dw_w"]:VECTORS["conv_dw_w"] + TAPS * DC].rearrange("p (k c) -> p c k", c=DC)
            pool.tensor_tensor(tap_lo[:, :, :], taps[:, 2 * DVE_PAIRS:, :], tap_hi[:, :, :].bitcast(F32),
                               ALU.subtract).then_inc(tap_parts, 1)
            pool.wait_ge(tap_parts, 2)
            diagonal_rounds(0, 2)

        def conv_pe():
            diagonal_rounds(2, 2 * len(ROUNDS))

        def diagonal_rounds(first, last):
            for r in range(first, last):
                c, (k, n) = r // len(ROUNDS), ROUNDS[r % len(ROUNDS)]
                if r >= 2:
                    pool.wait_ge(diag_used, r - 1)
                pool.tensor_tensor(diag[:, r % 2, 1, 0:n, :], ident[:, :].unsqueeze(1).broadcast_to([P, n, P]),
                                   tap_lo[:, c, k:k + n].unsqueeze(2).broadcast_to([P, n, P]),
                                   ALU.mult).then_inc(diag_lo, 1)

        def attend(kind, layer=0):
            offs, widths, _keys, _pt = attention_shape(kind)
            heads = MEM_HEADS if kind == "mem" else HEADS
            pool.wait_ge(part_lo, b.at("part_lo"))
            if kind == "fox":
                pool.tensor_copy(ident_r[:, :], ident[:, :])
                pool.tensor_copy(mask_r[:, :], mask[:, :]).then_inc(consts, 1)
            for h in range(heads):
                for i in range(TB - 1):
                    pool.wait_ge(summed, b.at("summed", TB * h + i + 1))
                    row, n = prob[h % 2][:, offs[i]:offs[i] + widths[i]], 4 * (h % 2) + i
                    pool.tensor_scalar(row, row, small[:, 24 + n:25 + n], None, ALU.mult).then_inc(normed_p, 1)

        schedule(b, dict(group=group, diag_lo_first=diag_lo_first, conv_pe=conv_pe, attend=attend))

    @block.tensor
    def _(pe):
        b = Book(pe)

        def sums(bank):
            pe.matmul(ps[:, bank, :], ones[:, :], acc[:, :], start=True, stop=True).then_inc(pe_side, 1)

        def group(kind, src, g, rhs, dst, fresh, tiles, stats=False, rows=None, width=S, settled=False,
                  after_turn=False, columns=False, since=0, **_):
            r_hi, r_lo = operand[rhs]
            base = 4 * b.parity
            pe.wait_ge(psum_read, b.at("psum_read", 0 if after_turn else -2))
            if settled:
                pe.wait_ge(part_lo, b.at("part_lo"))
            for j in range(tiles):
                if stats and j == tiles - 1:
                    pe.wait_ge(step, b.at("step"))
                    pe.wait_ge(psum_read, b.at("psum_read"))
                    sums(4 - base)
                if columns and j == tiles - 1:
                    pe.wait_ge(rstd_ready, b.at("rstd_ready"))
                    pe.wait_ge(psum_read, b.at("psum_read"))
                    for i in range(TB):
                        last = pe.transpose(ps[:, 4 - base, i * P:(i + 1) * P], rstd[:, i * P:(i + 1) * P], ident[:, :])
                    last.then_inc(pe_side, 1)
                if fresh:
                    pe.wait_ge(part_lo, b.at("part_lo", j + 1 - tiles - since))
                slot, _v = loaded_at(b, j)
                pe.wait_ge(tile_lo, b.at("tiles", j + 1))
                for a in range(2):
                    k = 2 * j + a
                    for n in range(rows or 4):
                        c = slice(n * P, (n + 1) * P)
                        if rows:
                            passes = ((r_hi[:, k, c], w_hi[:, slot, a, :]), (r_hi[:, k, c], w_lo[:, slot, a, :]),
                                      (r_lo[:, k, c], w_hi[:, slot, a, :]))
                        else:
                            passes = ((w_hi[:, slot, a, c], r_hi[:, k, :]), (w_hi[:, slot, a, c], r_lo[:, k, :]),
                                      (w_lo[:, slot, a, c], r_hi[:, k, :]))
                        for m, (lhs, mov) in enumerate(passes):
                            last = pe.matmul(ps[:, base + n, 0:width], lhs, mov, start=k == 0 and m == 0,
                                             stop=k == 2 * tiles - 1 and m == 2)
                last.then_inc(tiles_used, 1)
            if stats:
                pe.wait_ge(act_side, b.at("act_side", 1))
            if columns:
                pe.wait_ge(step, b.at("step", 1))

        def prologue():
            pe.wait_ge(consts, 2)
            pe.wait_ge(rows_in, ROWS_IN)
            for r in range(4):
                n = min(P, n_rows - r * P)
                last = pe.transpose(ps[:, 0, r * P:r * P + n], vrow[0:n, r, :], ident[0:n, 0:n])
            last.then_inc(pe_side, 1)
            for c, n in ((0, S), (S, GCOLS - S)):
                last = pe.matmul(ps[0:HEADS, 1 + c // S, 0:n], relb[:, :], onehot_sb[:, c:c + n],
                                 start=True, stop=True)
            last.then_inc(pe_side, 1)
            pe.wait_ge(x_in, 16)
            for c in range(DC):
                if c < 2:
                    pe.wait_ge(step, c + 1)
                for i in range(TB):
                    last = pe.transpose(ps[:, c, i * P:(i + 1) * P], xnat[:, i, c * P:(c + 1) * P], ident[:, :])
                last.then_inc(pe_side, 1)

        def mem_turn(layer):
            pe.wait_ge(psum_read, b.at("psum_read", -2))
            pe.wait_ge(step, b.at("step"))
            for c in range(DC):
                for i in range(MB):
                    o = (c % 2) * MEM + i * P
                    last = pe.transpose(ps[:, 4 * b.parity + c // 2, o:o + P], memn[:, i, c * P:(c + 1) * P], ident[:, :])
                if c % 2:
                    last.then_inc(pe_side, 1)

        def conv_pe():
            pe.wait_ge(psum_read, b.at("psum_read", -2))
            pe.wait_ge(part_lo, b.at("part_lo", -2 * GROUP["proj"]["part_lo"]))
            for r in range(2 * len(ROUNDS)):
                c, (k0, n) = r // len(ROUNDS), ROUNDS[r % len(ROUNDS)]
                pe.wait_ge(diag_hi, r + 1)
                pe.wait_ge(diag_lo, r + 1)
                for m in range(n):
                    k = k0 + m
                    for p, (part, u) in enumerate(((0, u_hi), (0, u_lo), (1, u_hi))):
                        last = pe.matmul(ps[:, 4 * b.parity + c, :], diag[:, r % 2, part, m, :], u[:, c, k:k + S],
                                         start=k == 0 and p == 0, stop=k == TAPS - 1 and p == 2)
                last.then_inc(diag_used, 1)

        def ln_centred():
            pe.wait_ge(psum_read, b.at("psum_read", -2))
            pe.wait_ge(step, b.at("step"))
            for c in range(DC):
                if c == 2 * DVE_PAIRS:
                    pe.wait_ge(psum_read, b.at("psum_read"))
                last = pe.matmul(ps[:, 4 * b.parity + 3, :], ones[:, :], conv[:, c, :], start=c == 0, stop=c == DC - 1)
            last.then_inc(pe_side, 1)

        def ln_sum():
            pe.wait_ge(psum_read, b.at("psum_read", -2))
            pe.wait_ge(step, b.at("step"))
            sums(4 * b.parity + 3)

        def gates():
            bank = 4 * b.parity
            pe.wait_ge(psum_read, b.at("psum_read", -2))
            pe.wait_ge(step, b.at("step"))
            n = 0
            for k in range(DC):
                for lhs, mov in ((wf_hi, h_hi), (wf_hi, h_lo), (wf_lo, h_hi)):
                    last = pe.matmul(ps[:, bank, :], lhs[:, k, :], mov[:, k, :], start=n == 0, stop=n == 3 * DC - 1)
                    n += 1
            last.then_inc(pe_side, 1)

        def final_norm(gain):
            pe.wait_ge(step, b.at("step"))
            pe.wait_ge(psum_read, b.at("psum_read"))
            sums(4 * b.parity)
            pe.wait_ge(act_side, b.at("act_side", 1))

        def attend(kind, layer=0):
            offs, widths, keys, pt = attention_shape(kind)
            mem = kind == "mem"
            heads, dch = (MEM_HEADS, MEM_HEAD_DIM // P) if mem else (HEADS, 1)
            (K_hi, K_lo), (V_hi, V_lo) = operand["km" if mem else "k"], operand["vm" if mem else "v"]
            if layer:
                pe.wait_ge(keys_back, 64)
            pe.wait_ge(psum_read, b.at("psum_read"))
            pe.wait_ge(part_lo, b.at("part_lo"))

            if kind == "fox":
                pe.wait_ge(consts, 3)

            def scores(h):
                for i in range(TB):
                    if h and mem:
                        pe.wait_ge(expd, b.at("expd", TB * (h - 1) + i + 1))
                    elif h:
                        pe.wait_ge(shifted, b.at("shifted", TB * (h - 1) + i + 1))
                    n = 0
                    for dc in range(dch):
                        c, r = (h * dch + dc, slice(0, P)) if mem else head_rows(h)
                        for lhs, mov in ((q_hi, K_hi), (q_hi, K_lo), (q_lo, K_hi)):
                            last = pe.matmul(ps[:, i, 0:widths[i]], lhs[r, c, i * P:(i + 1) * P],
                                             mov[r, c, 0:widths[i]], start=n == 0, stop=n == 3 * dch - 1)
                            if kind == "fox" and n == 0:
                                pe.matmul(ps[:, i, i * P:(i + 1) * P], ident_r[:, :], mask_r[:, :], start=False, stop=False)
                            n += 1
                    last.then_inc(scored, 1)

            def turn(h):
                if h:
                    pe.wait_ge(turned_lo, b.at("turned_lo", h))
                for i in range(TB):
                    if i < TB - 1:
                        pe.wait_ge(normed_p, b.at("normed", (TB - 1) * h + i + 1))
                    else:
                        pe.wait_ge(normed_last, b.at("normed_last", h + 1))
                    for j in keys(i):
                        c = pt[j][0] + i * P - pt[j][1]
                        last = pe.transpose(ps[:, 4 + c // S, c % S:c % S + P],
                                            prob[h % 2][:, offs[i] + j * P:offs[i] + (j + 1) * P], ident[:, :])
                last.then_inc(turned, 1)

            def weigh(h):
                pe.wait_ge(turned_lo, b.at("turned_lo", h + 1))
                if h:
                    pe.wait_ge(out_lo, b.at("out_lo", h))
                for dc in range(dch):
                    bank, c = (6 + dc, h * dch + dc) if mem else (7, head_rows(h)[0])
                    n = 0
                    for j, (col, tok) in enumerate(pt):
                        for lhs, mov in ((V_hi, pt_hi), (V_hi, pt_lo), (V_lo, pt_hi)):
                            last = pe.matmul(ps[:, bank, tok:S], lhs[:, j, c * P:(c + 1) * P],
                                             mov[h % 2][:, col:col + S - tok], start=n == 0, stop=n == 3 * len(pt) - 1)
                            n += 1
                last.then_inc(weighed, 1)

            scores(0)
            for h in range(heads + 2):
                if 1 <= h <= heads:
                    turn(h - 1)
                if h >= 2:
                    weigh(h - 2)
                if h + 1 < heads:
                    scores(h + 1)
            pe.wait_ge(out_lo, b.at("out_lo", heads))

        def output():
            def turn(i, half):
                for a in range(4):
                    last = pe.transpose(ps[:, 2 * i + half, a * P:(a + 1) * P],
                                        x[:, 4 * half + a, i * P:(i + 1) * P], ident[:, :])
                last.then_inc(pe_side, 1)

            pe.wait_ge(psum_read, b.at("psum_read"))
            pe.wait_ge(part_hi, b.at("part_hi", -2))
            for i in range(TB):
                turn(i, 0)
            pe.wait_ge(part_hi, b.at("part_hi"))
            for i in range(TB - 1):
                turn(i, 1)
            pe.wait_ge(step, b.at("step"))
            for i in range(TB):
                last = pe.matmul(ps[:, 2 * TB - 1, i:i + 1], acc[:, i * P:(i + 1) * P], ones[:, 0:1], start=True, stop=True)
            last.then_inc(pe_side, 1)
            pe.wait_ge(act_side, b.at("act_side", 1))
            turn(TB - 1, 1)

        schedule(b, dict(prologue=prologue, group=group, mem_turn=mem_turn, conv_pe=conv_pe,
                         ln_centred=ln_centred, ln_sum=ln_sum, gates=gates, final_norm=final_norm, attend=attend, output=output))

    @block.scalar
    def _(act):
        b = Book(act)

        def split_tiles(first, n):
            for m in range(first, first + n):
                if b.index is None and b.count.get("tiles", 0) + m >= TILES:
                    return
                slot, v = loaded_at(b, m)
                act.wait_ge(tile_loaded[slot], v)
                act.wait_ge(tiles_used, b.at("tiles", m - SLOTS + 1))
                act.activation(w_hi[:, slot], stage[:, slot], ACT.Copy).then_inc(tile_hi, 1)

        def root(bank, eps):
            act.activation(rstd[:, :], ps[:, bank, :], ACT.Sqrt, scale=1.0 / D, bias=eps_col(eps)).then_inc(act_side, 1)

        def eps_col(eps):
            return small[:, 40:41] if eps == RMS_EPS else small[:, 41:42]

        def group(kind, src, g, rhs, dst, fresh, tiles, at=0, stats=False, rows=None, width=S, ahead=True,
                  reprep=None, **_):
            if ahead and reprep is None:
                split_tiles(SLOTS, tiles - 1)
            if reprep is not None:
                for m in range(tiles):
                    if m < tiles - 1:
                        split_tiles(SLOTS + m, 1)
                    act.wait_ge(tiles_used, b.at("tiles", m + 1))
                    for c in (2 * m, 2 * m + 1):
                        last = act.activation(h_hi[:, c, :], x[:, c, :], ACT.Copy, scale=column(reprep + c))
                    last.then_inc(part_hi, 1)
            if stats:
                act.wait_ge(pe_side, b.at("pe_side", 1))
                root(4 - 4 * b.parity, RMS_EPS)
            if kind in ("glu", "glu_split"):
                act.wait_ge(psum_read, b.at("psum_read", 1))
                for a in range(2):
                    last = act.activation(t[:, a, :], t[:, a, :], ACT.Sigmoid,
                                          bias=column(VECTORS["conv_pw1_b"] + DC + 2 * at + a))
                last.then_inc(gated, 1)
            if kind == "glu_split":
                act.wait_ge(t_ready, b.at("t_ready", 1))
                act.activation(u_hi[:, :, PAD:PAD + S], t[:, 0:2, :], ACT.Copy).then_inc(part_hi, 1)
            if kind == "gate":
                act.wait_ge(psum_read, b.at("psum_read", 1))
                act.activation(t[:, 0:2, :], t[:, 0:2, :], ACT.Silu).then_inc(gated, 1)
                act.wait_ge(t_ready, b.at("t_ready", 1))
                act.activation(mid_hi[:, 2 * at:2 * at + 2, :], t[:, 2:4, :], ACT.Copy).then_inc(part_hi, 1)
            if kind in ("relu2", "bmul"):
                for a in range(2):
                    act.wait_ge(t_ready, b.at("t_ready", a + 1))
                    act.activation(mid_hi[:, 4 * at + 2 * a:4 * at + 2 * a + 2, :], t[:, 2 * a:2 * a + 2, :],
                                   ACT.Copy).then_inc(part_hi, 1)
            if kind == "proj":
                if src == "mem_wk0":
                    act.wait_ge(keys_out, 64)
                for a, (to, frm) in enumerate(proj_parts(dst, 0, at, width)):
                    act.wait_ge(psum_read, b.at("psum_read", a + 1))
                    act.activation(to, frm, ACT.Copy).then_inc(part_hi, 1)
            if ahead:
                split_tiles(SLOTS + tiles - 1, 1)

        def prologue():
            act.dma_start(xnat[:, :, :], A["x"][0].rearrange("(i p) d -> p i d", p=P)).then_inc(x_in, 16)
            for r, (frm, n) in row_loads[:HALF]:
                act.dma_start(r, frm).then_inc(rows_in, 16)
            act.dma_start(memn[:, :, :], A["mem"][0].rearrange("(i p) d -> p i d", p=P)).then_inc(mem_in, 16)
            split_tiles(0, SLOTS)

        def skew():
            act.wait_ge(g_out, 16)
            act.dma_start(skew_dram.rearrange("h (p n) -> h p n", p=P),
                          bass.AP(g_dram.tensor, 0, [[GCOLS, HEADS], [0, P], [1, GCOLS]])).then_inc(skewed, 16)

        def mem_rows():
            act.wait_ge(step, b.at("step"))
            act.dma_start(g_dram, g_tab[:, :]).then_inc(g_out, 16)
            act.wait_ge(mem_in, 16)
            for i in range(MB):
                act.activation(junk[:, :], memn[:, i, :], ACT.Square, accum_out=small[:, i:i + 1]).then_inc(act_side, 1)
                act.wait_ge(act_side, b.at("act_side", i + 1))
            act.activation(small[:, 2:4], small[:, 0:2], ACT.Sqrt, scale=1.0 / D, bias=eps_col(RMS_EPS)).then_inc(act_side, 1)

        def mem_turn(layer):
            for m in range(4):
                act.wait_ge(pe_side, b.at("pe_side", m + 1))
                for a in range(2):
                    last = act.activation(hm_hi[:, 2 * m + a, :], ps[:, 4 * b.parity + m, a * MEM:(a + 1) * MEM],
                                          ACT.Copy, scale=column(VECTORS["norm_memsrc_g"] + DC * layer + 2 * m + a))
                last.then_inc(part_hi, 1)

        def keys_out_dma():
            act.wait_ge(part_lo, b.at("part_lo"))
            for n, part in enumerate(kv_parts):
                act.dma_start(keys_dram[:, 2 * D * n:2 * D * n + 2 * D], part).then_inc(keys_out, 16)

        def keys_back_dma():
            act.wait_ge(weighed, b.at("weighed"))
            act.wait_ge(keys_out, 64)
            for n, part in enumerate(kv_parts):
                act.dma_start(part, keys_dram[:, 2 * D * n:2 * D * n + 2 * D]).then_inc(keys_back, 16)

        def diag_hi_first():
            taps = vec[:, VECTORS["conv_dw_w"]:VECTORS["conv_dw_w"] + TAPS * DC].rearrange("p (k c) -> p c k", c=DC)
            act.activation(tap_hi[:, :, :], taps[:, 2 * DVE_PAIRS:, :], ACT.Copy).then_inc(tap_parts, 1)
            diagonal_rounds(0, 2)

        def conv_pe():
            diagonal_rounds(2, 2 * len(ROUNDS))

        def diagonal_rounds(first, end):
            w = VECTORS["conv_dw_w"] + 2 * DVE_PAIRS
            for r in range(first, end):
                c, (k, n) = r // len(ROUNDS), ROUNDS[r % len(ROUNDS)]
                if r >= 2:
                    act.wait_ge(diag_used, r - 1)
                for m in range(n):
                    last = act.activation(diag[:, r % 2, 0, m, :], ident[:, :], ACT.Copy,
                                          scale=column(w + DC * (k + m) + c))
                last.then_inc(diag_hi, 1)

        def prep(gain, first, n, split, squares=True, whole=False, last=False):
            scale_x = last
            for m in range(n):
                p = first + m
                if not whole:
                    act.wait_ge(psum_read, b.at("psum_read", m + 1 - n))
                if split:
                    for c in (2 * p, 2 * p + 1):
                        last = act.activation(h_hi[:, c, :], x[:, c, :], ACT.Copy, scale=column(gain + c))
                    last.then_inc(part_hi, 1)
                if squares:
                    if m >= 2:
                        act.wait_ge(step, b.at("step", steps_after(first, m - 1)))
                    a = 2 * (p % 2)
                    act.activation(t[:, a:a + 2, :], x[:, 2 * p:2 * p + 2, :], ACT.Square).then_inc(squared, 1)
                if scale_x:
                    act.wait_ge(squared, b.at("squared", m + 1))
                    for c in (2 * p, 2 * p + 1):
                        last = act.activation(x[:, c, :], x[:, c, :], ACT.Copy, scale=column(gain + c))
                    last.then_inc(part_hi, 1)

        def steps_after(first, m):
            return sum(1 if p == 0 else 2 for p in range(first, first + m))

        def prep_all(gain, squares=True):
            act.wait_ge(psum_read, b.at("psum_read"))
            act.wait_ge(step, b.at("step"))
            act.wait_ge(pe_side, b.at("pe_side"))
            prep(gain, 0, 4, True, squares, whole=True)

        def ln_centred():
            for p in range(4):
                act.wait_ge(step, b.at("step", p + 2 if p == 0 else LN_CENTRE + 2 * p - 1))
                act.activation(t[:, 2:4, :], conv[:, 2 * p:2 * p + 2, :], ACT.Square).then_inc(squared, 1)

        def ln_sum():
            act.wait_ge(pe_side, b.at("pe_side", 1))
            root(4 * b.parity + 3, LN_EPS)

        def ln_scaled():
            for p in range(4):
                act.wait_ge(step, b.at("step", p + 1))
                for c in (2 * p, 2 * p + 1):
                    last = act.activation(conv[:, c, :], conv[:, c, :], ACT.Silu,
                                          scale=column(VECTORS["conv_ln_g"] + c), bias=column(VECTORS["conv_ln_b"] + c))
                last.then_inc(gated, 1)
                act.wait_ge(gated, b.at("gated", p + 1))
                act.activation(mid_hi[:, 2 * p:2 * p + 2, :], conv[:, 2 * p:2 * p + 2, :], ACT.Copy).then_inc(part_hi, 1)
                split_tiles(SLOTS + p, 1)

        def gates_split():
            act.wait_ge(gates_in, 32)
            act.wait_ge(step, b.at("step", 1))
            act.activation(wf_hi[:, :, 0:HEADS], wf[:, :, :], ACT.Copy).then_inc(act_side, 1)

        def gates_sum():
            act.wait_ge(step, b.at("step", 1))
            act.activation(f_t[:, 1, :], f_t[:, 0, :], ACT.Abs).then_inc(act_side, 1)
            act.wait_ge(act_side, b.at("act_side", 1))
            act.activation(f_t[:, 1, :], f_t[:, 1, :], ACT.Exp, scale=-1.0).then_inc(act_side, 1)
            act.wait_ge(act_side, b.at("act_side", 2))
            act.activation(f_t[:, 1, :], f_t[:, 1, :], ACT.Ln, bias=1.0).then_inc(act_side, 1)

        def gates_out():
            act.wait_ge(step, b.at("step"))
            act.dma_start(negc_dram, f_t[:, 3, :]).then_inc(negc_out, 16)
            act.wait_ge(negc_out, 16)

        def final_norm(gain):
            act.wait_ge(pe_side, b.at("pe_side", 1))
            root(4 * b.parity, RMS_EPS)

        def gates_load():
            act.wait_ge(psum_read, b.at("psum_read"))
            act.dma_start(wf[:, :, :], A["kvf_w"][:, 2 * D:2 * D + HEADS].rearrange("(k p) n -> p k n", p=P)).then_inc(gates_in, 16)
            act.dma_start(small[0:HEADS, 50:51], A["fgate_b"].rearrange("(h a) -> h a", a=1)).then_inc(gates_in, 16)

        def attend(kind, layer=0):
            offs, widths, keys, pt = attention_shape(kind)
            mem = kind == "mem"
            heads = MEM_HEADS if mem else HEADS
            wid = 2 * S if mem else WID

            def load_table(h):
                if mem or h >= heads:
                    return
                if kind == "fox":
                    src = bass.AP(negc_dram.tensor, h * S, [[0, P], [1, S]])
                else:
                    src = bass.AP(skew_dram.tensor, h * P * GCOLS + P - 1, [[GCOLS - 1, P], [1, S]])
                act.dma_start(t[:, h % 2, :], src).then_inc(table_in[h % 2], 16)

            def exps(h, i):
                act.wait_ge(maxed, b.at("maxed", TB * h + i + 1))
                n = 4 * (h % 2) + i
                row = prob[h % 2][:, offs[i]:offs[i] + widths[i]]
                if mem and i == 0 and h >= 2:
                    act.wait_ge(turned, b.at("turned", h - 1))
                act.activation(row, ps[:, i, 0:widths[i]] if mem else row, ACT.Exp, bias=small[:, 8 + n:9 + n],
                               accum_out=small[:, 16 + n:17 + n]).then_inc(expd, 1)

            def norm_last(h):
                i, n = TB - 1, 4 * (h % 2) + TB - 1
                row = prob[h % 2][:, offs[i]:offs[i] + widths[i]]
                act.wait_ge(summed, b.at("summed", TB * (h + 1)))
                act.activation(row, row, ACT.Copy, scale=small[:, 24 + n:25 + n]).then_inc(normed_last, 1)

            def turned_parts(h):
                act.wait_ge(turned, b.at("turned", h + 1))
                if h >= 2:
                    act.wait_ge(weighed, b.at("weighed", h - 1))
                act.activation(pt_hi[h % 2][:, 0:wid], flat(ps[:, 4:7, :], wid), ACT.Copy).then_inc(turned_hi, 1)

            def out_parts(h):
                act.wait_ge(weighed, b.at("weighed", h + 1))
                to, frm = out_of(kind, h, q_hi)
                act.activation(to, frm, ACT.Copy).then_inc(out_hi, 1)

            act.wait_ge(part_lo, b.at("part_lo"))
            if kind == "dil":
                act.wait_ge(skewed, 16)
            load_table(0)
            load_table(1)
            for h in range(heads + 2):
                if h < heads:
                    exps(h, 0)
                    exps(h, 1)
                if 1 <= h <= heads:
                    turned_parts(h - 1)
                if h < heads:
                    exps(h, 2)
                    exps(h, 3)
                    load_table(h + 2)
                if h >= 2:
                    out_parts(h - 2)
                if h < heads:
                    norm_last(h)

        def output():
            act.wait_ge(pe_side, b.at("pe_side", 2 * TB))
            act.activation(small[:, 4:8], ps[:, 2 * TB - 1, 0:TB], ACT.Sqrt, scale=1.0 / D,
                           bias=eps_col(RMS_EPS)).then_inc(act_side, 1)
            act.wait_ge(rstd_ready, b.at("rstd_ready", 1))
            for i in range(TB):
                act.wait_ge(pe_side, b.at("pe_side", TB + i + 1 if i < TB - 1 else 2 * TB + 1))
                act.activation(xnat[:, i, S:2 * S], ps[:, 2 * i + 1, :], ACT.Copy, scale=small[:, 4 + i:5 + i]).then_inc(gated, 1)

        schedule(b, dict(prologue=prologue, group=group, mem_rows=mem_rows, mem_turn=mem_turn, prep=prep,
                         prep_all=prep_all, skew=skew, diag_hi_first=diag_hi_first, ln_sum=ln_sum, keys_out=keys_out_dma, keys_back=keys_back_dma, conv_pe=conv_pe,
                         ln_centred=ln_centred, ln_scaled=ln_scaled, gates_split=gates_split, gates_sum=gates_sum,
                         gates_out=gates_out, gates_load=gates_load, final_norm=final_norm,
                         attend=attend, output=output))

    @block.vector
    def _(dve):
        b = Book(dve)
        rstd2 = rstd[:, :].unsqueeze(1).broadcast_to([P, 2, S])

        def lo_of(to, value, hi):
            return dve.tensor_tensor(to, value, hi.bitcast(F32), ALU.subtract)

        def lo_of_h(gain, pair):
            for c in (2 * pair, 2 * pair + 1):
                last = dve.scalar_tensor_tensor(out=h_lo[:, c, :], in0=x[:, c, :], scalar=column(gain + c),
                                                in1=h_hi[:, c, :].bitcast(F32), op0=ALU.mult, op1=ALU.subtract)
            return last

        def settle():
            dve.wait_ge(psum_read, b.at("psum_read"))
            dve.wait_ge(t_ready, b.at("t_ready"))
            dve.wait_ge(part_lo, b.at("part_lo"))
            dve.wait_ge(step, b.at("step"))

        def group(kind, src, g, rhs, dst, fresh, tiles, at=0, stats=False, rows=None, width=S, scale=None,
                  bias=None, columns=False, reprep=None, **_):
            base = 4 * b.parity
            before = 0
            if reprep is not None:
                before = tiles
                for m in range(tiles):
                    dve.wait_ge(part_hi, b.at("part_hi", m + 1))
                    lo_of_h(reprep, m).then_inc(part_lo, 1)
            if columns:
                dve.wait_ge(pe_side, b.at("pe_side", 1))
                dve.tensor_copy(small[:, 4:8], ps[:, 4 - base, :].rearrange("p (i s) -> p i s", i=TB)[:, :, 0]
                                ).then_inc(step, 1)
            if stats:
                dve.wait_ge(act_side, b.at("act_side", 1))
                dve.reciprocal(rstd[:, :], rstd[:, :]).then_inc(rstd_ready, 1)
            dve.wait_ge(rstd_ready, b.at("rstd_ready", 1 if stats else 0))
            settle()
            dve.wait_ge(tiles_used, b.at("tiles", tiles))
            for a in range(2):
                bank, here = ps[:, base + 2 * a:base + 2 * a + 2, :], t[:, 2 * a:2 * a + 2, :]
                if kind == "add":
                    cs = range(4 * at + 2 * a, 4 * at + 2 * a + 2)
                    if bias:
                        for c in cs:
                            last = dve.scalar_tensor_tensor(out=x[:, c, :], in0=ps[:, base + c - 4 * at, :],
                                                            scalar=column(VECTORS[bias] + c), in1=x[:, c, :],
                                                            op0=ALU.add, op1=ALU.add)
                    else:
                        last = dve.tensor_tensor(x[:, cs[0]:cs[1] + 1, :], bank, x[:, cs[0]:cs[1] + 1, :], ALU.add)
                elif dst in ("km", "vm"):
                    if dst == "km":
                        last = dve.tensor_copy(t[:, 2 * a:2 * a + 2, 0:width], ps[:, base + 2 * a:base + 2 * a + 2, 0:width])
                    else:
                        last = dve.tensor_copy(t[:, a, :], ps[:, base + a, :])
                elif rows:
                    dve.wait_ge(step, b.at("step"))
                    for i in (2 * a, 2 * a + 1):
                        last = dve.tensor_scalar(t[:, i, :], ps[:, base + i, :], small[:, 4 + i:5 + i], None, ALU.mult)
                elif scale:
                    last = dve.scalar_tensor_tensor(out=here, in0=bank, scalar=scale, in1=rstd2, op0=ALU.mult,
                                                    op1=ALU.mult)
                else:
                    last = dve.tensor_tensor(here, bank, rstd2, ALU.mult)
                last.then_inc(psum_read, 1)
            if kind in ("glu", "glu_split"):
                dve.wait_ge(psum_read, b.at("psum_read", 2))
                dve.wait_ge(gated, b.at("gated", 1))
                for a in range(2):
                    c = 2 * at + a
                    to = u_pad[:, c, PAD:PAD + S] if kind == "glu" else t[:, a, :]
                    last = dve.scalar_tensor_tensor(out=to, in0=t[:, 2 + a, :], in1=t[:, a, :],
                                                    scalar=column(VECTORS["conv_pw1_b"] + c), op0=ALU.add, op1=ALU.mult)
                last.then_inc(t_ready, 1)
            if kind == "glu_split":
                dve.wait_ge(part_hi, b.at("part_hi", 1))
                lo_of(u_lo[:, :, PAD:PAD + S], t[:, 0:2, :], u_hi[:, :, PAD:PAD + S]).then_inc(part_lo, 1)
            if kind == "gate":
                dve.wait_ge(psum_read, b.at("psum_read", 2))
                dve.wait_ge(gated, b.at("gated", 1))
                dve.tensor_tensor(t[:, 2:4, :], t[:, 0:2, :], t[:, 2:4, :], ALU.mult).then_inc(t_ready, 1)
                dve.wait_ge(part_hi, b.at("part_hi", 1))
                cs = slice(2 * at, 2 * at + 2)
                lo_of(mid_lo[:, cs, :], t[:, 2:4, :], mid_hi[:, cs, :]).then_inc(part_lo, 1)
            if kind in ("relu2", "bmul"):
                for a in range(2):
                    here, cs = t[:, 2 * a:2 * a + 2, :], slice(4 * at + 2 * a, 4 * at + 2 * a + 2)
                    dve.wait_ge(psum_read, b.at("psum_read", a + 1))
                    if kind == "relu2":
                        last = dve.scalar_tensor_tensor(out=here, in0=here, scalar=0.0, in1=here, op0=ALU.max,
                                                        op1=ALU.mult)
                    else:
                        last = dve.tensor_tensor(here, here, y2[:, cs, :], ALU.mult)
                    last.then_inc(t_ready, 1)
                for a in range(2):
                    here, cs = t[:, 2 * a:2 * a + 2, :], slice(4 * at + 2 * a, 4 * at + 2 * a + 2)
                    dve.wait_ge(part_hi, b.at("part_hi", a + 1))
                    lo_of(mid_lo[:, cs, :], here, mid_hi[:, cs, :]).then_inc(part_lo, 1)
            if kind == "proj":
                for a, ((to, frm), (hi, _f)) in enumerate(zip(proj_parts(dst, 1, at, width), proj_parts(dst, 0, at, width))):
                    dve.wait_ge(part_hi, b.at("part_hi", before + a + 1))
                    lo_of(to, frm, hi).then_inc(part_lo, 1)
            if kind == "cu":
                dve.wait_ge(psum_read, b.at("psum_read", 2))
                if at == 0:
                    dve.memset(z_pad[:, :, 0:2], 0.0)
                dve.tensor_tensor(z_pad[:, :, 2:2 + S], t[:, 0:2, :], t[:, 2:4, :], ALU.mult).then_inc(step, 1)
                for k in range(3):
                    dve.wait_ge(step, b.at("step", k + 1))
                    for a in range(2):
                        c = 2 * at + a
                        w = column(VECTORS["conv_kernel_2"] + DC * k + c)
                        if k == 0:
                            last = dve.tensor_scalar(y2[:, c, :], z_pad[:, a, 0:S], w, None, ALU.mult)
                        else:
                            last = dve.scalar_tensor_tensor(out=y2[:, c, :], in0=z_pad[:, a, k:k + S], scalar=w,
                                                            in1=y2[:, c, :], op0=ALU.mult, op1=ALU.add)
                    last.then_inc(step, 1)

        def prologue():
            dve.memset(small[:, 40:41], RMS_EPS)
            dve.memset(small[:, 41:42], LN_EPS)
            dve.wait_ge(pe_side, 1)
            dve.tensor_copy(vec[:, :], ps[:, 0, 0:n_rows]).then_inc(step, 1)
            dve.wait_ge(pe_side, 2)
            dve.wait_ge(rows_in, ROWS_IN)
            dve.tensor_tensor(g_tab[:, :], flat(ps[0:HEADS, 1:3, :], GCOLS), g_log[:, :], ALU.add).then_inc(step, 1)
            for p in range(4):
                dve.wait_ge(pe_side, 2 + 2 * p + 2)
                dve.tensor_copy(x[:, 2 * p:2 * p + 2, :], ps[:, 2 * p:2 * p + 2, :]).then_inc(psum_read, 1)
            dve.memset(u_hi[:, :, 0:PAD].bitcast(F32), 0.0)
            dve.memset(u_lo[:, :, 0:PAD].bitcast(F32), 0.0)
            dve.memset(u_pad[:, :, 0:PAD], 0.0).then_inc(step, 1)

        def mem_rows():
            dve.wait_ge(act_side, b.at("act_side", 3))
            dve.reciprocal(small[:, 2:4], small[:, 2:4]).then_inc(step, 1)
            dve.wait_ge(step, b.at("step", 1))
            for i in range(MB):
                dve.tensor_scalar(memn[:, i, :], memn[:, i, :], small[:, 2 + i:3 + i], None, ALU.mult).then_inc(step, 1)

        def mem_turn(layer):
            for m in range(4):
                dve.wait_ge(part_hi, b.at("part_hi", m + 1))
                for a in range(2):
                    c = 2 * m + a
                    last = dve.scalar_tensor_tensor(
                        out=hm_lo[:, c, :], in0=ps[:, 4 * b.parity + m, a * MEM:(a + 1) * MEM],
                        scalar=column(VECTORS["norm_memsrc_g"] + DC * layer + c), in1=hm_hi[:, c, :].bitcast(F32),
                        op0=ALU.mult, op1=ALU.subtract)
                last.then_inc(part_lo, 1)

        def take(p, a, done):
            if p == 0:
                dve.tensor_tensor(acc[:, :], t[:, a, :], t[:, a + 1, :], ALU.add).then_inc(step, 1)
                return done + 1
            dve.tensor_tensor(t[:, a, :], t[:, a, :], t[:, a + 1, :], ALU.add).then_inc(step, 1)
            dve.wait_ge(step, b.at("step", done + 1))
            dve.tensor_tensor(acc[:, :], acc[:, :], t[:, a, :], ALU.add).then_inc(step, 1)
            return done + 2

        def prep(gain, first, n, split, squares=True, whole=False, last=False):
            done = 0
            for m in range(n):
                p = first + m
                if not whole:
                    dve.wait_ge(psum_read, b.at("psum_read", m + 1 - n))
                if split:
                    dve.wait_ge(part_hi, b.at("part_hi", m + 1))
                    lo_of_h(gain, p).then_inc(part_lo, 1)
                if squares:
                    dve.wait_ge(squared, b.at("squared", m + 1))
                    done = take(p, 2 * (p % 2), done)

        def prep_all(gain, squares=True):
            dve.wait_ge(psum_read, b.at("psum_read"))
            dve.wait_ge(step, b.at("step"))
            prep(gain, 0, 4, True, squares, whole=True)

        def conv_taps(pair, first, n):
            cs = (2 * pair, 2 * pair + 1)
            w = VECTORS["conv_dw_w"]
            if first == 0:
                dve.wait_ge(t_ready, b.at("t_ready"))
                dve.wait_ge(pe_side, b.at("pe_side"))
                for c in cs:
                    dve.tensor_scalar(conv[:, c, :], u_pad[:, c, 0:S], column(w + c), column(VECTORS["conv_dw_b"] + c),
                                      ALU.mult, ALU.add).then_inc(step, 1)
                n -= 1
                first = 1
                now = b.at("step", 2)
            else:
                now = b.at("step")
            if n == 0:
                return
            with dve.Fori(first, first + n) as k:
                for a, c in enumerate(cs):
                    dve.wait_ge(step, k * 2 + (now + a - 1 - 2 * first))
                    dve.scalar_tensor_tensor(out=conv[:, c, :], in0=u_pad[:, c, bass.ds(k, S)],
                                             scalar=vec[:, bass.ds(k * DC + (w + c), 1)], in1=conv[:, c, :],
                                             op0=ALU.mult, op1=ALU.add).then_inc(step, 1)

        def conv_pe():
            dve.wait_ge(diag_used, 2 * len(ROUNDS))
            for a in range(2):
                c = 2 * DVE_PAIRS + a
                dve.tensor_scalar(conv[:, c, :], ps[:, 4 * b.parity + a, :], column(VECTORS["conv_dw_b"] + c), None,
                                  ALU.add).then_inc(psum_read, 1)

        def ln_centred():
            dve.wait_ge(psum_read, b.at("psum_read"))
            dve.wait_ge(part_lo, b.at("part_lo"))
            dve.wait_ge(step, b.at("step"))
            dve.wait_ge(pe_side, b.at("pe_side", 1))
            dve.tensor_scalar(t[:, 0, :], ps[:, 4 * b.parity + 3, :], 1.0 / D, None, ALU.mult).then_inc(step, 1)
            dve.wait_ge(step, b.at("step", 1))
            mean2 = t[:, 0, :].unsqueeze(1).broadcast_to([P, 2, S])
            for p in range(4):
                c = conv[:, 2 * p:2 * p + 2, :]
                dve.tensor_tensor(c, c, mean2, ALU.subtract).then_inc(step, 1)
            done = LN_CENTRE
            for p in range(4):
                dve.wait_ge(squared, b.at("squared", p + 1))
                done = take(p, 2, done)

        def ln_scaled():
            dve.wait_ge(act_side, b.at("act_side"))
            dve.reciprocal(rstd[:, :], rstd[:, :]).then_inc(rstd_ready, 1)
            dve.wait_ge(rstd_ready, b.at("rstd_ready", 1))
            for p in range(4):
                c = conv[:, 2 * p:2 * p + 2, :]
                dve.tensor_tensor(c, c, rstd2, ALU.mult).then_inc(step, 1)
            for p in range(4):
                cs = slice(2 * p, 2 * p + 2)
                dve.wait_ge(part_hi, b.at("part_hi", p + 1))
                lo_of(mid_lo[:, cs, :], conv[:, cs, :], mid_hi[:, cs, :]).then_inc(part_lo, 1)

        def gates_split():
            dve.wait_ge(psum_read, b.at("psum_read"))
            dve.memset(wf_hi[:, :, :].bitcast(F32), 0.0)
            dve.memset(wf_lo[:, :, :].bitcast(F32), 0.0).then_inc(step, 1)
            dve.wait_ge(act_side, b.at("act_side", 1))
            lo_of(wf_lo[:, :, 0:HEADS], wf[:, :, :], wf_hi[:, :, 0:HEADS]).then_inc(step, 1)

        def gates():
            dve.wait_ge(pe_side, b.at("pe_side", 1))
            for a in range(2):
                half = slice(a * S // 2, (a + 1) * S // 2)
                dve.tensor_tensor(f_t[:, 0, half], ps[0:HEADS, 4 * b.parity, half], rstd[0:HEADS, half],
                                  ALU.mult).then_inc(psum_read, 1)

        def gates_sum():
            dve.wait_ge(psum_read, b.at("psum_read"))
            dve.wait_ge(gates_in, 32)
            dve.tensor_scalar(f_t[:, 0, :], f_t[:, 0, :], small[0:HEADS, 50:51], None, ALU.add).then_inc(step, 1)
            dve.wait_ge(step, b.at("step", 1))
            dve.tensor_scalar(f_t[:, 2, :], f_t[:, 0, :], -1.0, 0.0, ALU.mult, ALU.max).then_inc(step, 1)
            dve.wait_ge(act_side, b.at("act_side", 3))
            dve.wait_ge(step, b.at("step", 2))
            dve.tensor_tensor_scan(f_t[:, 3, :], f_t[:, 1, :], f_t[:, 2, :], initial=0.0, op0=ALU.add,
                                   op1=ALU.add).then_inc(step, 1)

        def final_norm(gain):
            dve.wait_ge(act_side, b.at("act_side", 1))
            dve.reciprocal(rstd[:, :], rstd[:, :]).then_inc(rstd_ready, 1)
            dve.wait_ge(rstd_ready, b.at("rstd_ready", 1))
            dve.wait_ge(psum_read, b.at("psum_read"))
            for c in range(DC):
                last = dve.scalar_tensor_tensor(out=x[:, c, :], in0=x[:, c, :], scalar=column(gain + c),
                                                in1=rstd[:, :], op0=ALU.mult, op1=ALU.mult)
                if c % 2:
                    last.then_inc(step, 1)

        def attend(kind, layer=0):
            offs, widths, keys, pt = attention_shape(kind)
            mem = kind == "mem"
            heads = MEM_HEADS if mem else HEADS
            wid = 2 * S if mem else WID

            def shift(h, i):
                if mem:
                    return
                row, w = prob[h % 2][:, offs[i]:offs[i] + widths[i]], widths[i]
                if i == 0:
                    if h >= 2:
                        dve.wait_ge(turned, b.at("turned", h - 1))
                    dve.wait_ge(table_in[h % 2], 16 * (b.count.get("tables", 0) + h // 2 + 1))
                dve.wait_ge(scored, b.at("scored", TB * h + i + 1))
                table = t[:, h % 2, S - w:S] if kind == "dil" else t[:, h % 2, 0:w]
                dve.tensor_tensor(row, ps[:, i, 0:w], table, ALU.add).then_inc(shifted, 1)

            def peak(h, i):
                n = 4 * (h % 2) + i
                if mem:
                    dve.wait_ge(scored, b.at("scored", TB * h + i + 1))
                else:
                    dve.wait_ge(shifted, b.at("shifted", TB * h + i + 1))
                row = ps[:, i, 0:widths[i]] if mem else prob[h % 2][:, offs[i]:offs[i] + widths[i]]
                dve.reduce_max(small[:, 8 + n:9 + n], row, AX_X, negate=True).then_inc(maxed, 1)

            def over_sum(h, i):
                n = 4 * (h % 2) + i
                dve.wait_ge(expd, b.at("expd", TB * h + i + 1))
                dve.reciprocal(small[:, 24 + n:25 + n], small[:, 16 + n:17 + n]).then_inc(summed, 1)

            def turned_parts(h):
                dve.wait_ge(turned_hi, b.at("turned_hi", h + 1))
                lo_of(pt_lo[h % 2][:, 0:wid], flat(ps[:, 4:7, :], wid), pt_hi[h % 2][:, 0:wid]).then_inc(turned_lo, 1)

            def out_parts(h):
                dve.wait_ge(out_hi, b.at("out_hi", h + 1))
                to, frm = out_of(kind, h, q_lo)
                lo_of(to, frm, out_of(kind, h, q_hi)[0]).then_inc(out_lo, 1)

            for h in range(heads + 2):
                if h < heads:
                    shift(h, 0)
                    shift(h, 1)
                    peak(h, 0)
                    shift(h, 2)
                    peak(h, 1)
                    over_sum(h, 0)
                    shift(h, 3)
                    peak(h, 2)
                    over_sum(h, 1)
                    peak(h, 3)
                if 1 <= h <= heads:
                    turned_parts(h - 1)
                if h < heads:
                    over_sum(h, 2)
                    over_sum(h, 3)
                if h >= 2:
                    out_parts(h - 2)

        def output():
            dve.wait_ge(act_side, b.at("act_side", 1))
            dve.reciprocal(small[:, 4:8], small[:, 4:8]).then_inc(rstd_ready, 1)
            dve.wait_ge(rstd_ready, b.at("rstd_ready", 1))
            for i in range(TB):
                dve.wait_ge(pe_side, b.at("pe_side", i + 1))
                dve.tensor_scalar(xnat[:, i, 0:S], ps[:, 2 * i, :], small[:, 4 + i:5 + i], None, ALU.mult).then_inc(t_ready, 1)

        schedule(b, dict(prologue=prologue, group=group, mem_turn=mem_turn, prep=prep, prep_all=prep_all,
                         mem_rows=mem_rows, conv=conv_taps, conv_pe=conv_pe, ln_centred=ln_centred,
                         ln_scaled=ln_scaled, gates_split=gates_split, gates=gates, gates_sum=gates_sum,
                         final_norm=final_norm, attend=attend, output=output))


INPUTS = ["x", "mem", "norm_mix_g", "norm_mem_g", "norm_memsrc_g", "norm_ff_g", "mem_wq", "mem_wk", "mem_wv",
          "mem_wo", "ff_w1", "ff_w2", "conv_pw1_w", "conv_pw1_b", "conv_dw_w", "conv_dw_b", "conv_ln_g",
          "conv_ln_b", "conv_pw2_w", "conv_pw2_b", "kv_norm_g", "kvf_w", "fgate_b", "fox_wq", "fox_wo",
          "final_norm_g", "mix_norm_2", "ffn_norm_2", "final_norm_2", "conv_w_in_2", "conv_kernel_2",
          "conv_w_out_2", "attn_w_qkv_2", "attn_w_out_2", "rel_bias_2", "ffn_w_gate_2", "ffn_w_up_2",
          "ffn_w_down_2"]


def kernel(**inputs):
    import concourse.bacc as bacc
    from concourse.bass_utils import run_bass_kernel_spmd

    nc = bacc.Bacc("TRN2", target_bir_lowering=False, num_devices=1)
    arrays, aps = {}, {}
    for name in INPUTS:
        a = np.ascontiguousarray(inputs[name])
        arrays[f"in_{name}"] = a
        aps[name] = nc.dram_tensor(f"in_{name}", a.shape, mybir.dt.from_np(a.dtype), kind="ExternalInput").ap()
    out = nc.dram_tensor("out", (1, S, D), F32, kind="ExternalOutput").ap()
    build(nc, aps, out)
    r = run_bass_kernel_spmd(nc, [arrays], core_ids=[0])
    return r.results[0]["out"]
```

```python
from contextlib import ExitStack, contextmanager

import numpy as np

import concourse.bass as bass
from concourse import mybir

P = 128
F32 = mybir.dt.float32
F32R = mybir.dt.float32r
ALU = mybir.AluOpType
ACT = mybir.ActivationFunctionType
AX_X = mybir.AxisListType.X

D = 1024
S = 512
DC = D // P
TB = S // P
MEM = 256
MB = MEM // P
D_FF = 4 * D
D_FF2 = 2816
TAPS = 31
PAD = TAPS - 1
DVE_PAIRS = 3
ROUNDS = [(0, 5), (5, 5), (10, 5), (15, 4), (19, 4), (23, 4), (27, 4)]
HEADS, HEAD_DIM = 16, 64
MEM_HEADS, MEM_HEAD_DIM = 4, 256
BUCKETS, MAX_DISTANCE = 32, 2048
BRANCHES = ((128, 1), (512, 4), (2048, 16))
RMS_EPS, LN_EPS = 1e-6, 1e-5
MASKED = -2.0 ** 100

SLOTS = 4
COLS = 512
GCOLS = 640
SBUF_BASE = 16640

GROUP = {
    "relu2": dict(psum_read=2, t_ready=2, part_hi=2, part_lo=2),
    "gate": dict(psum_read=2, gated=1, t_ready=1, part_hi=1, part_lo=1),
    "glu": dict(psum_read=2, gated=1, t_ready=1),
    "glu_split": dict(psum_read=2, gated=1, t_ready=1, part_hi=1, part_lo=1),
    "cu": dict(psum_read=2, step=4),
    "bmul": dict(psum_read=2, t_ready=2, part_hi=2, part_lo=2),
    "proj": dict(psum_read=2, part_hi=2, part_lo=2),
    "add": dict(psum_read=2),
}
STATS = dict(pe_side=1, act_side=1, rstd_ready=1)
MEM_ROWS = dict(act_side=3, step=3)
MEM_TURN = dict(pe_side=4, part_hi=4, part_lo=4)
LN_CENTRE, LN_SQUARES = 1 + 4, 7
LN_CENTRED = dict(pe_side=1, step=LN_CENTRE + LN_SQUARES, squared=4)
LN_SUM = dict(pe_side=1, act_side=1)
LN_SCALED = dict(rstd_ready=1, step=4, gated=4, part_hi=4, part_lo=4)
GATES_SPLIT = dict(act_side=1, step=2)
GATES = dict(pe_side=1, psum_read=2)
GATES_SUM = dict(act_side=3, step=3)
COLUMNS = dict(pe_side=1, step=1)
TWO_NORMS = dict(pe_side=2, act_side=2, rstd_ready=5)
PROLOGUE = dict(pe_side=2 + DC, psum_read=4, step=3)


def prep_counts(first, n, split=True, squares=True, last=False, twice=False):
    c = {}
    if split:
        c.update(part_hi=n, part_lo=n)
    if last:
        c.update(part_hi=n)
    if squares:
        c.update(squared=n, step=sum(1 if p == 0 else 2 for p in range(first, first + n)))
    if twice:
        c.update(squared=2 * n, step=2 * c["step"], scaled=n)
    return c


VECTORS = {}


def vector_rows():
    rows, at = [], 0
    for name, n in (("norm_mix_g", 16), ("norm_mem_g", 16), ("norm_memsrc_g", 16), ("norm_ff_g", 16),
                    ("kv_norm_g", 8), ("final_norm_g", 8), ("mix_norm_2", 16), ("ffn_norm_2", 16),
                    ("final_norm_2", 8),
                    ("conv_pw1_b", 16), ("conv_dw_b", 8), ("conv_ln_g", 8), ("conv_ln_b", 8),
                    ("conv_pw2_b", 8), ("conv_kernel_2", 24), ("conv_dw_w", 8 * TAPS)):
        rows.append((name, at, n))
        VECTORS[name] = at
        at += n
    return rows, at


def distance_tables():
    d = (S - 1) - np.arange(GCOLS)
    exact = BUCKETS // 2
    df = np.maximum(d, 1).astype(np.float32)
    large = exact + (np.log(df / np.float32(exact)) / np.float32(np.log(MAX_DISTANCE / exact))
                     * np.float32(BUCKETS - exact)).astype(np.int32)
    bucket = np.where(d < exact, d, np.minimum(large, BUCKETS - 1))
    onehot = np.zeros((BUCKETS, GCOLS), np.float32)
    count = np.zeros(GCOLS)
    for window, dilation in BRANCHES:
        count += (d >= 0) & (d % dilation == 0) & (d // dilation <= window // dilation)
    for m in range(GCOLS):
        if d[m] >= 0:
            onehot[bucket[m], m] = 1.0
    logcount = np.where(count > 0, np.log(np.maximum(count, 1)), MASKED).astype(np.float32)
    return onehot, np.tile(logcount[None, :], (HEADS, 1))


class Book:

    def __init__(self, eng):
        self.eng, self.count, self.index, self.per, self.parity = eng, {}, None, {}, 0

    def at(self, name, more=0):
        v = max(self.count.get(name, 0) + more, 0)
        return v if self.index is None else v + self.index * self.per.get(name, 0)

    def add(self, **more):
        for k, v in more.items():
            self.count[k] = self.count.get(k, 0) + v

    def here(self):
        fixed = Book(None)
        fixed.count = dict(self.count)
        return fixed

    @contextmanager
    def loop(self, n, per):
        before = dict(self.count)
        if self.eng is None:
            yield 0
        else:
            with self.eng.Fori(0, n) as i:
                self.index, self.per = i, per
                yield i
        for k in set(self.count) | set(per):
            assert self.count.get(k, 0) - before.get(k, 0) == per.get(k, 0), (k, per)
            self.count[k] = before.get(k, 0) + n * per.get(k, 0)
        self.index, self.per = None, {}


def group_counts(kind, tiles, columns=False, reprep=None, **_):
    c = {**GROUP[kind], "tiles": tiles}
    if columns:
        c.update(COLUMNS)
    if reprep is not None:
        c.update({k: c[k] + 4 for k in ("part_hi", "part_lo")})
    return c


def attention_shape(kind):
    if kind == "mem":
        return [MEM * i for i in range(TB)], [MEM] * TB, (lambda i: range(MB)), [(0, 0), (S, 0)]
    return ([0, 128, 384, 768], [(i + 1) * P for i in range(TB)], (lambda i: range(i + 1)),
            [(0, 0), (512, 128), (1024, 256), (896, 384)])


def attention_counts(kind):
    n = MEM_HEADS if kind == "mem" else HEADS
    c = {k: TB * n for k in ("scored", "maxed", "expd", "summed")}
    c["normed"] = (TB - 1) * n
    c.update({k: n for k in ("normed_last", "turned", "turned_hi", "turned_lo", "weighed", "out_hi", "out_lo")})
    if kind != "mem":
        c.update(tables=n // 2, shifted=TB * n)
    return c


def schedule(b, e):

    def do(step, counts, *args, **kw):
        if step in e:
            e[step](*args, **kw)
        b.add(**counts)

    def groups(kind, src, rhs, dst=None, first=False, tiles=4, g=0, n=1, c0=None, **kw):
        for i in range(n):
            do("group", group_counts(kind, tiles, **kw), kind, src, g + i, rhs, dst, first and i == 0, tiles,
               at=(g if c0 is None else c0) + i, **kw)
            b.parity ^= 1

    def normed(kind, src, rhs, dst=None, n=1, **kw):
        do("group", {**group_counts(kind, 4), **STATS}, kind, src, 0, rhs, dst, True, 4, at=0, stats=True, **kw)
        b.parity ^= 1
        groups(kind, src, rhs, dst, n=n - 1, g=1, **kw)

    def add(src, rhs, gain=None, tiles=4, fresh=True, bias=None, row0=0, split=True,
            last=False, twice=None, after=None):
        for g in range(2):
            do("group", group_counts("add", tiles), "add", src, g, rhs, None, fresh and g == 0, tiles,
               at=g, bias=bias, row0=row0, after=after if g == 0 else None)
            b.parity ^= 1
            if gain is not None:
                do("prep", prep_counts(2 * g, 2, split, last=last, twice=twice is not None), gain, 2 * g, 2, split,
                   last=last, twice=twice)

    def mem_kv_groups(layer):
        return [lambda g=g: groups("proj", f"mem_wk{layer}", "hm", "km", g=g, width=MEM, settled=layer == 1)
                for g in range(2)] + \
               [lambda g=g, **kw: groups("proj", f"mem_wv{layer}", "hm", "vm", g=g, rows=MB, **kw)
                for g in range(2)]

    def mem_attention(layer, next_gain):
        normed("proj", f"mem_wq{layer}", "h", "q", scale=MEM_HEAD_DIM ** -0.5)
        groups("proj", f"mem_wq{layer}", "h", "q", g=1, scale=MEM_HEAD_DIM ** -0.5, early="mem", layer=layer)
        do("attend", attention_counts("mem"), "mem")
        add(f"mem_wo{layer}", "q", gain=next_gain, fresh=False, after="mem")

    def ff(layer, next_gain, twice=None):
        up, down = f"ff_w1{layer}", f"ff_w2{layer}"
        rounds = D_FF // D
        per_round = {}
        for part in (group_counts("relu2", 4), group_counts("relu2", 4),
                     group_counts("add", 4), group_counts("add", 4)):
            for k, v in part.items():
                per_round[k] = per_round.get(k, 0) + v
        normed("relu2", up, "h", "mid", n=2)
        add(down, "mid")
        with b.loop(rounds - 2, per_round) as i:
            groups("relu2", up, "h", "mid", g=2 * i + 2, n=2, c0=0)
            add(down, "mid", row0=(i + 1) * D)
        groups("relu2", up, "h", "mid", g=2 * (rounds - 1), n=2, c0=0)
        add(down, "mid", gain=next_gain, row0=(rounds - 1) * D, twice=twice)

    def swiglu(layer, next_gain, last=False):
        src, down = f"glu2{layer}", f"down2{layer}"
        normed("gate", src, "h", "mid", n=4)
        add(down, "mid")
        groups("gate", src, "h", "mid", g=4, n=4, c0=0)
        add(down, "mid", row0=D)
        rest = (D_FF2 - 2 * D) // 256
        groups("gate", src, "h", "mid", g=8, n=rest, c0=0)
        add(down, "mid", gain=next_gain, tiles=rest, row0=2 * D, split=not last, last=last)

    def gain(name, layer=0):
        return VECTORS[name] + DC * layer

    def mem_turn(layer):
        do("mem_turn", MEM_TURN, layer)
        b.parity ^= 1

    pair_taps = [(p, k) for p in range(DVE_PAIRS) for k in range(TAPS)]

    def taps(n):
        while n and pair_taps:
            p, k = pair_taps[0]
            m = min(n, TAPS - k)
            del pair_taps[:m]
            n -= m
            do("conv", dict(step=2 * m), p, k, m)

    do("prologue", PROLOGUE)
    do("prep", prep_counts(0, 4), gain("norm_mix_g"), 0, 4, True)
    do("mem_rows", MEM_ROWS)
    normed("glu", "pw1", "h")
    mem_turn(1)
    taps(10)
    groups("glu", "pw1", "h", g=1, after_turn=True)
    do("skew", {})
    for n, group in zip((4, 6, 6, 6), mem_kv_groups(1)):
        taps(n)
        group()
    mem_turn(0)
    taps(12)
    groups("glu", "pw1", "h", g=2, after_turn=True)
    do("keys_out", {})
    do("diag_hi_first", {})
    taps(13)
    groups("glu_split", "pw1", "h", g=3, settled=True)
    do("diag_lo_first", {})
    keys0, keys1, values0, values1 = mem_kv_groups(0)
    taps(4)
    keys0()
    taps(6)
    keys1()
    taps(DVE_PAIRS * TAPS)
    do("conv_pe", dict(psum_read=2))
    b.parity ^= 1
    do("ln_centred", LN_CENTRED)
    values0()
    do("ln_sum", LN_SUM)
    do("ln_scaled", LN_SCALED)
    values1(ahead=False)
    add("pw2", "mid", gain=gain("norm_mem_g"), bias="conv_pw2_b")
    mem_attention(0, gain("norm_ff_g"))
    ff(0, gain("kv_norm_g"))
    do("gates_load", {})
    normed("proj", "fox_k", "h", "k")
    do("gates_split", GATES_SPLIT)
    groups("proj", "fox_k", "h", "k", g=1, columns=True)
    do("gates", GATES)
    b.parity ^= 1
    do("gates_sum", GATES_SUM)
    groups("proj", "fox_v", "h", "v", rows=TB)
    groups("proj", "fox_v", "h", "v", g=1, rows=TB, reprep=gain("norm_mix_g", 1))
    do("gates_out", {})
    groups("proj", "fox_wq", "h", "q", n=2, first=True, since=2, scale=HEAD_DIM ** -0.5)
    do("attend", attention_counts("fox"), "fox")
    do("keys_back", {})
    add("fox_wo", "q", gain=gain("norm_mem_g", 1), fresh=False, after="fox")
    mem_attention(1, gain("norm_ff_g", 1))
    ff(1, gain("mix_norm_2"), twice=gain("final_norm_g"))
    do("group", {**group_counts("cu", 4), **TWO_NORMS}, "cu", "conv_cu", 0, "h", None, True, 4, at=0, two_norms=True)
    b.parity ^= 1
    do("scale_x", dict(step=4))
    groups("cu", "conv_cu", "h", n=3, g=1)
    groups("bmul", "conv_b", "h", "mid", n=2)
    add("conv_out", "mid", gain=gain("ffn_norm_2"))
    swiglu(0, gain("mix_norm_2", 1))
    normed("proj", "dil_q", "h", "q", n=2, scale=HEAD_DIM ** -0.5)
    groups("proj", "dil_k", "h", "k")
    groups("proj", "dil_k", "h", "k", g=1, columns=True)
    groups("proj", "dil_v", "h", "v", n=2, rows=TB)
    do("attend", attention_counts("dil"), "dil")
    add("dil_out", "q", gain=gain("ffn_norm_2", 1), fresh=False, after="dil")
    swiglu(1, gain("final_norm_2"), last=True)
    do("output", {})


def build(nc, A, out):
    with ExitStack() as ctx:
        build_in(nc, A, out, ctx)


def build_in(nc, A, out, ctx):
    def sem(name):
        return ctx.enter_context(nc.semaphore(name))

    KB = 1024
    place = [SBUF_BASE]

    def region(nbytes):
        place[0] += nbytes
        assert place[0] <= nc.sbuf_usable_end
        return place[0] - nbytes

    def at(name, shape, dt, offset):
        return nc.alloc_sbuf_tensor_at(name, shape, dt, offset=offset)

    rows, n_rows = vector_rows()
    R_X, R_H, R_MID = region(16 * KB), region(32 * KB), region(32 * KB)
    R_ST, R_W = region(16 * KB), region(32 * KB)
    R_A0, R_A1, R_T = region(32 * KB), region(32 * KB), region(8 * KB)

    x = at("x", [P, DC, S], F32, R_X)
    h_hi, h_lo = at("h_hi", [P, DC, S], F32R, R_H), at("h_lo", [P, DC, S], F32R, R_H + 16 * KB)
    mid_hi, mid_lo = at("mid_hi", [P, DC, S], F32R, R_MID), at("mid_lo", [P, DC, S], F32R, R_MID + 16 * KB)
    stage = at("stage", [P, SLOTS, 2, COLS], F32, R_ST)
    w_hi = at("w_hi", [P, SLOTS, 2, COLS], F32R, R_W)
    w_lo = at("w_lo", [P, SLOTS, 2, COLS], F32R, R_W + 16 * KB)
    q_hi, q_lo = at("q_hi", [P, DC, S], F32R, R_A0), at("q_lo", [P, DC, S], F32R, R_A0 + 16 * KB)
    k_hi, k_lo = at("k_hi", [P, DC, S], F32R, R_A1), at("k_lo", [P, DC, S], F32R, R_A1 + 16 * KB)
    t = at("t", [P, 4, S], F32, R_T)
    rstd, acc = at("rstd", [P, S], F32, region(2 * KB)), at("acc", [P, S], F32, region(2 * KB))
    ident, ones = at("ident", [P, P], F32, region(512)), at("ones", [P, P], F32, region(512))
    mask = at("mask", [P, P], F32, region(512))
    vec = at("vec", [P, n_rows], F32, region((n_rows * 4 + 31) // 32 * 32))
    small = at("small", [P, 64], F32, region(256))
    xnat = at("xnat", [P, TB, D], F32, R_MID)
    vrow = at("vrow", [P, 4, P], F32, R_A0)
    g_tab = at("g_tab", [HEADS, GCOLS], F32, R_A1)
    g_log = at("g_log", [HEADS, GCOLS], F32, R_A1 + 3 * KB)
    onehot_sb = at("onehot_sb", [BUCKETS, GCOLS], F32, R_A1 + 6 * KB)
    relb = at("relb", [BUCKETS, HEADS], F32, R_A1 + 9 * KB)
    memn = at("memn", [P, MB, D], F32, R_A0 + 8 * KB)
    junk = at("junk", [P, D], F32, R_MID + 28 * KB)
    hm_hi = at("hm_hi", [P, DC, MEM], F32R, R_A0 + 16 * KB)
    hm_lo = at("hm_lo", [P, DC, MEM], F32R, R_A0 + 24 * KB)
    km_hi, km_lo = at("km_hi", [P, DC, MEM], F32R, R_A1), at("km_lo", [P, DC, MEM], F32R, R_A1 + 8 * KB)
    vm_hi, vm_lo = at("vm_hi", [P, MB, D], F32R, R_A1 + 16 * KB), at("vm_lo", [P, MB, D], F32R, R_A1 + 24 * KB)
    u_pad = at("u_pad", [P, 2 * DVE_PAIRS, PAD + S], F32, R_MID)
    u_hi = at("u_hi", [P, 2, PAD + S], F32R, R_MID + 13056)
    u_lo = at("u_lo", [P, 2, PAD + S], F32R, R_MID + 17408)
    diag = at("diag", [P, 2, 2, 5, P], F32R, R_MID + 21760)
    tap_hi, tap_lo = at("tap_hi", [P, 2, TAPS], F32R, R_MID + 32000), at("tap_lo", [P, 2, TAPS], F32, R_MID + 32256)
    conv = at("conv", [P, DC, S], F32, R_A0)
    z_pad, y2 = at("z_pad", [P, 2, 2 + S], F32, R_A1), at("y2", [P, DC, S], F32, R_A0)
    v_hi, v_lo = at("v_hi", [P, TB, D], F32R, R_MID), at("v_lo", [P, TB, D], F32R, R_MID + 16 * KB)
    wf = at("wf", [P, DC, HEADS], F32, R_A0)
    wf_hi, wf_lo = at("wf_hi", [P, DC, P], F32R, R_A0 + 4 * KB), at("wf_lo", [P, DC, P], F32R, R_A0 + 8 * KB)
    f_t = at("f_t", [HEADS, 4, S], F32, R_A0 + 16 * KB)
    WID = 1280
    prob = [at(f"prob{i}", [P, WID], F32, R_H + i * 5 * KB) for i in range(2)]
    ident_r, mask_r = at("ident_r", [P, P], F32R, R_H + 30 * KB), at("mask_r", [P, P], F32R, R_H + 30 * KB + 512)
    pt_hi = [at(f"pt_hi{i}", [P, WID], F32R, R_H + (10 + 10 * i) * KB) for i in range(2)]
    pt_lo = [at(f"pt_lo{i}", [P, WID], F32R, R_H + (15 + 10 * i) * KB) for i in range(2)]

    kv_parts = [part[:, :, :].bitcast(F32).rearrange("p a n -> p (a n)") for part in (km_hi, km_lo, vm_hi, vm_lo)]
    prob_m = [at(f"prob_m{i}", [P, TB * MEM], F32, R_MID + 4 * KB * i) for i in range(2)]
    pt_hi_m = [at(f"pt_hi_m{i}", [P, MB * S], F32R, R_MID + (8 + 8 * i) * KB) for i in range(2)]
    pt_lo_m = [at(f"pt_lo_m{i}", [P, MB * S], F32R, R_MID + (12 + 8 * i) * KB) for i in range(2)]

    def buffers(kind):
        return (prob_m, pt_hi_m, pt_lo_m) if kind == "mem" else (prob, pt_hi, pt_lo)

    operand = {"h": (h_hi, h_lo), "mid": (mid_hi, mid_lo), "q": (q_hi, q_lo), "k": (k_hi, k_lo),
               "hm": (hm_hi, hm_lo), "km": (km_hi, km_lo), "vm": (vm_hi, vm_lo), "v": (v_hi, v_lo)}

    ps = ctx.enter_context(nc.psum_tensor("ps", [P, 8, S], F32))

    negc_dram = nc.dram_tensor("negc_dram", (HEADS, S), F32, kind="Internal").ap()
    g_dram = nc.dram_tensor("g_dram", (HEADS, GCOLS), F32, kind="Internal").ap()
    skew_dram = nc.dram_tensor("skew_dram", (HEADS, P * GCOLS), F32, kind="Internal").ap()
    keys_dram = nc.dram_tensor("keys_dram", (P, 8 * D), F32, kind="Internal").ap()
    onehot, logcount = distance_tables()
    onehot_c = nc.inline_tensor(onehot, "onehot_c").ap()
    logcount_c = nc.inline_tensor(logcount, "logcount_c").ap()

    tile_loaded = [sem(f"tile_loaded{i}") for i in range(SLOTS)]
    tile_hi, tile_lo = sem("tile_hi"), sem("tile_lo")
    tiles_used = sem("tiles_used")
    psum_read = sem("psum_read")
    t_ready = sem("t_ready")
    gated = sem("gated")
    part_hi, part_lo = sem("part_hi"), sem("part_lo")
    squared = sem("squared")
    step = sem("step")
    pe_side, act_side = sem("pe_side"), sem("act_side")
    rstd_ready = sem("rstd_ready")
    scaled = sem("scaled")
    consts = sem("consts")
    tap_parts, diag_hi, diag_lo = sem("tap_parts"), sem("diag_hi"), sem("diag_lo")
    diag_used = sem("diag_used")
    keys_out, keys_back = sem("keys_out"), sem("keys_back")
    rows_in, x_in, mem_in = sem("rows_in"), sem("x_in"), sem("mem_in")
    g_out, skewed, gates_in, negc_out, stored = (sem(n) for n in ("g_out", "skewed", "gates_in", "negc_out", "stored"))
    table_in = [sem("table_in0"), sem("table_in1")]
    scored, shifted, maxed, expd = (sem(n) for n in ("scored", "shifted", "maxed", "expd"))
    summed, turned = sem("summed"), sem("turned")
    normed_p, normed_last = sem("normed"), sem("normed_last")
    turned_hi, turned_lo, weighed = sem("turned_hi"), sem("turned_lo"), sem("weighed")
    out_hi, out_lo = sem("out_hi"), sem("out_lo")

    def column(j):
        return vec[:, j:j + 1]

    def head_rows(h):
        return h * HEAD_DIM // P, slice(h * HEAD_DIM % P, h * HEAD_DIM % P + HEAD_DIM)

    dry = Book(None)
    schedule(dry, {})
    TILES = dry.count["tiles"]

    def loaded_at(b, ahead):
        n = b.count.get("tiles", 0) + ahead
        v = 32 * (n // SLOTS + 1)
        if b.index is not None:
            v = v + b.index * (32 // SLOTS * b.per["tiles"])
        return n % SLOTS, v

    def flat(banks, n):
        return banks.rearrange("p b s -> p (b s)")[:, 0:n]

    def proj_parts(dst, lo, at, width):
        to = operand[dst][lo]
        c = slice(S * at, S * at + S)
        if dst == "vm":
            return [(to[:, a, c], t[:, a, :]) for a in range(2)]
        if dst == "v":
            return [(to[:, 2 * a:2 * a + 2, c], t[:, 2 * a:2 * a + 2, :]) for a in range(2)]
        return [(to[:, 4 * at + 2 * a:4 * at + 2 * a + 2, :], t[:, 2 * a:2 * a + 2, 0:width]) for a in range(2)]

    def out_of(kind, h, q, ob):
        if kind == "mem":
            return q[:, 2 * h:2 * h + 2, :], ps[:, ob + 2:ob + 4, :]
        c, r = head_rows(h)
        return q[r, c, :], ps[r, ob + 3, :]

    row_loads = []
    for name, first, n in rows:
        flat_ap = A[name].rearrange("(a b) -> a b", b=P) if len(A[name].shape) == 1 else \
            A[name].rearrange("a (b c) -> (a b) c", c=P) if len(A[name].shape) == 2 else \
            A[name][0].rearrange("a (b c) -> (a b) c", c=P)
        done = 0
        while done < n:
            r = first + done
            m = min(n - done, P - r % P)
            row_loads.append((vrow[r % P:r % P + m, r // P, :], (flat_ap[done:done + m, :], m)))
            done += m
    row_loads += [(relb[:, :], (A["rel_bias_2"], 0)), (onehot_sb[:, :], (onehot_c, 0)), (g_log[:, :], (logcount_c, 0))]
    ROWS_IN = 16 * len(row_loads)
    HALF = len(row_loads) // 2

    block = ctx.enter_context(nc.Block())

    @block.sync
    def _(sp):
        b = Book(sp)

        def plain(w):
            def src(g, j, row0):
                return [(stage_at[:, a, :], w[bass.ds(row0 + (2 * j + a) * P, P), bass.ds(g * COLS, COLS)])
                        for a in (0, 1)]
            return src

        def pair(wa, wb, off_a=0, off_b=0):
            def src(g, j, row0):
                return [(stage_at[:, :, 256 * n:256 * n + 256],
                         w[2 * j * P:2 * (j + 1) * P, off + g * 256:off + (g + 1) * 256]
                         .rearrange("(a p) n -> p a n", p=P))
                        for n, (w, off) in enumerate(((wa, off_a), (wb, off_b)))]
            return src

        src_of = {"pw1": pair(A["conv_pw1_w"][0], A["conv_pw1_w"][0], D, 0), "pw2": plain(A["conv_pw2_w"][0]),
                  "fox_k": plain(A["kvf_w"][:, 0:D]), "fox_v": plain(A["kvf_w"][:, D:2 * D]),
                  "fox_wq": plain(A["fox_wq"][0]), "fox_wo": plain(A["fox_wo"][0]),
                  "conv_cu": pair(A["conv_w_in_2"][0], A["conv_w_in_2"][0], D, 2 * D),
                  "conv_b": plain(A["conv_w_in_2"][0][:, 0:D]), "conv_out": plain(A["conv_w_out_2"][0]),
                  "dil_q": plain(A["attn_w_qkv_2"][0][:, 0:D]), "dil_k": plain(A["attn_w_qkv_2"][0][:, D:2 * D]),
                  "dil_v": plain(A["attn_w_qkv_2"][0][:, 2 * D:3 * D]), "dil_out": plain(A["attn_w_out_2"][0])}
        for layer in range(2):
            for n in ("mem_wq", "mem_wk", "mem_wv", "mem_wo", "ff_w1", "ff_w2"):
                src_of[f"{n}{layer}"] = plain(A[n][layer])
            src_of[f"glu2{layer}"] = pair(A["ffn_w_gate_2"][layer], A["ffn_w_up_2"][layer])
            src_of[f"down2{layer}"] = plain(A["ffn_w_down_2"][layer])

        def group(kind, src, g, rhs, dst, fresh, tiles, row0=0, **_):
            nonlocal stage_at
            for j in range(tiles):
                slot, _v = loaded_at(b, j)
                stage_at = stage[:, slot]
                sp.wait_ge(tile_lo, b.at("tiles", j - SLOTS + 1))
                for to, frm in src_of[src](g, j, row0):
                    sp.dma_start(to, frm).then_inc(tile_loaded[slot], 16)

        def prologue():
            for r, (frm, n) in row_loads[HALF:]:
                sp.dma_start(r, frm).then_inc(rows_in, 16)

        stage_at = None
        def output():
            for i in range(TB):
                sp.wait_ge(t_ready, b.at("t_ready", i + 1))
                sp.wait_ge(gated, b.at("gated", i + 1))
                sp.dma_start(out[0, i * P:(i + 1) * P, :], xnat[:, i, :]).then_inc(stored, 16)

        schedule(b, dict(prologue=prologue, group=group, output=output))
        sp.wait_ge(stored, 16 * TB)

    @block.gpsimd
    def _(pool):
        b = Book(pool)
        pool.memset(ones[:, :], 1.0)
        pool.memset(ident[:, :], 0.0)
        pool.memset(mask[:, :], 0.0).then_inc(consts, 1)
        pool.wait_ge(consts, 1)
        pool.affine_select(out=ident[:, :], in_=ident[:, :], compare_op=ALU.not_equal, fill=1.0,
                           base=0, pattern=[[-1, P]], channel_multiplier=1)
        pool.affine_select(out=mask[:, :], in_=mask[:, :], compare_op=ALU.is_ge, fill=MASKED,
                           base=0, pattern=[[-1, P]], channel_multiplier=1).then_inc(consts, 1)

        def group(kind, src, g, rhs, dst, fresh, tiles, after=None, **_):
            for j in range(2 if after else 0, tiles):
                tile(j)

        def tile(j):
            slot, _v = loaded_at(b, j)
            pool.wait_ge(tile_hi, b.at("tiles", j + 1))
            pool.tensor_tensor(w_lo[:, slot], stage[:, slot], w_hi[:, slot].bitcast(F32),
                               ALU.subtract).then_inc(tile_lo, 1)

        def diag_lo_first():
            pool.wait_ge(tap_parts, 1)
            taps = vec[:, VECTORS["conv_dw_w"]:VECTORS["conv_dw_w"] + TAPS * DC].rearrange("p (k c) -> p c k", c=DC)
            pool.tensor_tensor(tap_lo[:, :, :], taps[:, 2 * DVE_PAIRS:, :], tap_hi[:, :, :].bitcast(F32),
                               ALU.subtract).then_inc(tap_parts, 1)
            pool.wait_ge(tap_parts, 2)
            diagonal_rounds(0, 2)

        def conv_pe():
            diagonal_rounds(2, 2 * len(ROUNDS))

        def diagonal_rounds(first, last):
            for r in range(first, last):
                c, (k, n) = r // len(ROUNDS), ROUNDS[r % len(ROUNDS)]
                if r >= 2:
                    pool.wait_ge(diag_used, r - 1)
                pool.tensor_tensor(diag[:, r % 2, 1, 0:n, :], ident[:, :].unsqueeze(1).broadcast_to([P, n, P]),
                                   tap_lo[:, c, k:k + n].unsqueeze(2).broadcast_to([P, n, P]),
                                   ALU.mult).then_inc(diag_lo, 1)

        def attend(kind):
            offs, widths, _keys, _pt = attention_shape(kind)
            heads = MEM_HEADS if kind == "mem" else HEADS
            prob = buffers(kind)[0]
            if kind == "fox":
                pool.wait_ge(part_lo, b.at("part_lo"))
                pool.tensor_copy(ident_r[:, :], ident[:, :])
                pool.tensor_copy(mask_r[:, :], mask[:, :]).then_inc(consts, 1)
            for h in range(heads):
                for i in range(TB - 1):
                    pool.wait_ge(summed, b.at("summed", TB * h + i + 1))
                    row, n = prob[h % 2][:, offs[i]:offs[i] + widths[i]], 4 * (h % 2) + i
                    pool.tensor_scalar(row, row, small[:, 24 + n:25 + n], None, ALU.mult).then_inc(normed_p, 1)
                if heads - 3 <= h < heads - 1:
                    tile(h - (heads - 3))

        schedule(b, dict(group=group, diag_lo_first=diag_lo_first, conv_pe=conv_pe, attend=attend))

    @block.tensor
    def _(pe):
        b = Book(pe)

        attention = None

        def sums(bank, of=acc):
            pe.matmul(ps[:, bank, :], ones[:, :], of[:, :], start=True, stop=True).then_inc(pe_side, 1)

        def group(kind, src, g, rhs, dst, fresh, tiles, stats=False, rows=None, width=S, settled=False,
                  after_turn=False, columns=False, since=0, two_norms=False, early=None,
                  layer=0, after=None, **_):
            r_hi, r_lo = operand[rhs]
            base = 4 * b.parity
            nonlocal attention
            pe.wait_ge(psum_read, b.at("psum_read", 0 if after_turn else -2))
            if settled:
                pe.wait_ge(part_lo, b.at("part_lo"))
            for j in range(tiles):
                if early and j == 2:
                    pe.wait_ge(psum_read, b.at("psum_read"))
                    pe.wait_ge(part_lo, b.at("part_lo"))
                    if layer:
                        pe.wait_ge(keys_back, 64)
                    attention = attention_steps(early, 4 - base)
                    attention[0](0)
                if after:
                    _scores, turn, weigh, a, heads = attention
                    if j == 0:
                        if after == "mem":
                            pe.wait_ge(expd, a.at("expd", TB * heads))
                        else:
                            pe.wait_ge(shifted, a.at("shifted", TB * heads))
                    if j == 1:
                        turn(heads - 1)
                        weigh(heads - 2)
                    if j == 2:
                        weigh(heads - 1)
                    pe.wait_ge(out_lo, a.at("out_lo", (j + 1) * heads // tiles))
                if (stats or two_norms) and j == tiles - 1:
                    pe.wait_ge(step, b.at("step"))
                    pe.wait_ge(psum_read, b.at("psum_read"))
                    sums(4 - base)
                    if two_norms:
                        sums(5 - base, rstd)
                if columns and j == tiles - 1:
                    pe.wait_ge(rstd_ready, b.at("rstd_ready"))
                    pe.wait_ge(psum_read, b.at("psum_read"))
                    for i in range(TB):
                        last = pe.transpose(ps[:, 4 - base, i * P:(i + 1) * P], rstd[:, i * P:(i + 1) * P], ident[:, :])
                    last.then_inc(pe_side, 1)
                if fresh:
                    pe.wait_ge(part_lo, b.at("part_lo", j + 1 - tiles - since))
                slot, _v = loaded_at(b, j)
                pe.wait_ge(tile_lo, b.at("tiles", j + 1))
                for a in range(2):
                    k = 2 * j + a
                    for n in range(rows or 4):
                        c = slice(n * P, (n + 1) * P)
                        if rows:
                            passes = ((r_hi[:, k, c], w_hi[:, slot, a, :]), (r_hi[:, k, c], w_lo[:, slot, a, :]),
                                      (r_lo[:, k, c], w_hi[:, slot, a, :]))
                        else:
                            passes = ((w_hi[:, slot, a, c], r_hi[:, k, :]), (w_hi[:, slot, a, c], r_lo[:, k, :]),
                                      (w_lo[:, slot, a, c], r_hi[:, k, :]))
                        for m, (lhs, mov) in enumerate(passes):
                            last = pe.matmul(ps[:, base + n, 0:width], lhs, mov, start=k == 0 and m == 0,
                                             stop=k == 2 * tiles - 1 and m == 2)
                last.then_inc(tiles_used, 1)
            if stats:
                pe.wait_ge(act_side, b.at("act_side", 1))
            if two_norms:
                pe.wait_ge(act_side, b.at("act_side", 1))
                pe.wait_ge(rstd_ready, b.at("rstd_ready", 2))
            if columns:
                pe.wait_ge(step, b.at("step", 1))

        def prologue():
            pe.wait_ge(consts, 2)
            pe.wait_ge(rows_in, ROWS_IN)
            for r in range(4):
                n = min(P, n_rows - r * P)
                last = pe.transpose(ps[:, 0, r * P:r * P + n], vrow[0:n, r, :], ident[0:n, 0:n])
            last.then_inc(pe_side, 1)
            for c, n in ((0, S), (S, GCOLS - S)):
                last = pe.matmul(ps[0:HEADS, 1 + c // S, 0:n], relb[:, :], onehot_sb[:, c:c + n],
                                 start=True, stop=True)
            last.then_inc(pe_side, 1)
            pe.wait_ge(x_in, 16)
            for c in range(DC):
                if c < 2:
                    pe.wait_ge(step, c + 1)
                for i in range(TB):
                    last = pe.transpose(ps[:, c, i * P:(i + 1) * P], xnat[:, i, c * P:(c + 1) * P], ident[:, :])
                last.then_inc(pe_side, 1)

        def mem_turn(layer):
            pe.wait_ge(psum_read, b.at("psum_read", -2))
            pe.wait_ge(step, b.at("step"))
            for c in range(DC):
                for i in range(MB):
                    o = (c % 2) * MEM + i * P
                    last = pe.transpose(ps[:, 4 * b.parity + c // 2, o:o + P], memn[:, i, c * P:(c + 1) * P], ident[:, :])
                if c % 2:
                    last.then_inc(pe_side, 1)

        def conv_pe():
            pe.wait_ge(psum_read, b.at("psum_read", -2))
            pe.wait_ge(part_lo, b.at("part_lo", -2 * GROUP["proj"]["part_lo"]))
            for r in range(2 * len(ROUNDS)):
                c, (k0, n) = r // len(ROUNDS), ROUNDS[r % len(ROUNDS)]
                pe.wait_ge(diag_hi, r + 1)
                pe.wait_ge(diag_lo, r + 1)
                for m in range(n):
                    k = k0 + m
                    for p, (part, u) in enumerate(((0, u_hi), (0, u_lo), (1, u_hi))):
                        last = pe.matmul(ps[:, 4 * b.parity + c, :], diag[:, r % 2, part, m, :], u[:, c, k:k + S],
                                         start=k == 0 and p == 0, stop=k == TAPS - 1 and p == 2)
                last.then_inc(diag_used, 1)

        def ln_centred():
            pe.wait_ge(psum_read, b.at("psum_read", -2))
            pe.wait_ge(step, b.at("step"))
            for c in range(DC):
                if c == 2 * DVE_PAIRS:
                    pe.wait_ge(psum_read, b.at("psum_read"))
                last = pe.matmul(ps[:, 4 * b.parity + 3, :], ones[:, :], conv[:, c, :], start=c == 0, stop=c == DC - 1)
            last.then_inc(pe_side, 1)

        def ln_sum():
            pe.wait_ge(psum_read, b.at("psum_read", -2))
            pe.wait_ge(step, b.at("step"))
            sums(4 * b.parity + 3)

        def gates():
            bank = 4 * b.parity
            pe.wait_ge(psum_read, b.at("psum_read", -2))
            pe.wait_ge(step, b.at("step"))
            n = 0
            for k in range(DC):
                for lhs, mov in ((wf_hi, h_hi), (wf_hi, h_lo), (wf_lo, h_hi)):
                    last = pe.matmul(ps[:, bank, :], lhs[:, k, :], mov[:, k, :], start=n == 0, stop=n == 3 * DC - 1)
                    n += 1
            last.then_inc(pe_side, 1)

        def attention_steps(kind, sb):
            ob, a = 4 - sb, b.here()
            prob, pt_hi, pt_lo = buffers(kind)
            offs, widths, keys, pt = attention_shape(kind)
            mem = kind == "mem"
            heads, dch = (MEM_HEADS, MEM_HEAD_DIM // P) if mem else (HEADS, 1)
            (K_hi, K_lo), (V_hi, V_lo) = operand["km" if mem else "k"], operand["vm" if mem else "v"]
            def scores(h):
                for i in range(TB):
                    if h and mem:
                        pe.wait_ge(expd, a.at("expd", TB * (h - 1) + i + 1))
                    elif h:
                        pe.wait_ge(shifted, a.at("shifted", TB * (h - 1) + i + 1))
                    n = 0
                    for dc in range(dch):
                        c, r = (h * dch + dc, slice(0, P)) if mem else head_rows(h)
                        for lhs, mov in ((q_hi, K_hi), (q_hi, K_lo), (q_lo, K_hi)):
                            last = pe.matmul(ps[:, sb + i, 0:widths[i]], lhs[r, c, i * P:(i + 1) * P],
                                             mov[r, c, 0:widths[i]], start=n == 0, stop=n == 3 * dch - 1)
                            if kind == "fox" and n == 0:
                                pe.matmul(ps[:, sb + i, i * P:(i + 1) * P], ident_r[:, :], mask_r[:, :], start=False, stop=False)
                            n += 1
                    last.then_inc(scored, 1)

            def turn(h):
                if h:
                    pe.wait_ge(turned_lo, a.at("turned_lo", h))
                for i in range(TB):
                    if i < TB - 1:
                        pe.wait_ge(normed_p, a.at("normed", (TB - 1) * h + i + 1))
                    else:
                        pe.wait_ge(normed_last, a.at("normed_last", h + 1))
                    for j in keys(i):
                        c = pt[j][0] + i * P - pt[j][1]
                        last = pe.transpose(ps[:, ob + c // S, c % S:c % S + P],
                                            prob[h % 2][:, offs[i] + j * P:offs[i] + (j + 1) * P], ident[:, :])
                last.then_inc(turned, 1)

            def weigh(h):
                pe.wait_ge(turned_lo, a.at("turned_lo", h + 1))
                if h:
                    pe.wait_ge(out_lo, a.at("out_lo", h))
                for dc in range(dch):
                    bank, c = (ob + 2 + dc, h * dch + dc) if mem else (ob + 3, head_rows(h)[0])
                    n = 0
                    for j, (col, tok) in enumerate(pt):
                        for lhs, mov in ((V_hi, pt_hi), (V_hi, pt_lo), (V_lo, pt_hi)):
                            last = pe.matmul(ps[:, bank, tok:S], lhs[:, j, c * P:(c + 1) * P],
                                             mov[h % 2][:, col:col + S - tok], start=n == 0, stop=n == 3 * len(pt) - 1)
                            n += 1
                last.then_inc(weighed, 1)

            return scores, turn, weigh, a, heads

        def attend(kind):
            nonlocal attention
            if kind != "mem":
                attention = attention_steps(kind, 4 * b.parity)
            scores, turn, weigh, _a, heads = attention
            if kind == "mem":
                scores(1)
            pe.wait_ge(psum_read, b.at("psum_read"))
            pe.wait_ge(part_lo, b.at("part_lo"))
            if kind == "fox":
                pe.wait_ge(consts, 3)
            if kind != "mem":
                scores(0)
                scores(1)
            for h in range(1, heads):
                turn(h - 1)
                if h >= 2:
                    weigh(h - 2)
                if h + 1 < heads:
                    scores(h + 1)

        def output():
            def turn(i, half):
                for a in range(4):
                    last = pe.transpose(ps[:, 2 * i + half, a * P:(a + 1) * P],
                                        x[:, 4 * half + a, i * P:(i + 1) * P], ident[:, :])
                last.then_inc(pe_side, 1)

            pe.wait_ge(psum_read, b.at("psum_read"))
            pe.wait_ge(part_hi, b.at("part_hi", -2))
            for i in range(TB):
                turn(i, 0)
            pe.wait_ge(part_hi, b.at("part_hi"))
            for i in range(TB - 1):
                turn(i, 1)
            pe.wait_ge(step, b.at("step"))
            for i in range(TB):
                last = pe.matmul(ps[:, 2 * TB - 1, i:i + 1], acc[:, i * P:(i + 1) * P], ones[:, 0:1], start=True, stop=True)
            last.then_inc(pe_side, 1)
            pe.wait_ge(act_side, b.at("act_side", 1))
            turn(TB - 1, 1)

        schedule(b, dict(prologue=prologue, group=group, mem_turn=mem_turn, conv_pe=conv_pe,
                         ln_centred=ln_centred, ln_sum=ln_sum, gates=gates, attend=attend, output=output))

    @block.scalar
    def _(act):
        b = Book(act)

        def split_tiles(first, n):
            for m in range(first, first + n):
                if b.index is None and b.count.get("tiles", 0) + m >= TILES:
                    return
                slot, v = loaded_at(b, m)
                act.wait_ge(tile_loaded[slot], v)
                act.wait_ge(tiles_used, b.at("tiles", m - SLOTS + 1))
                act.activation(w_hi[:, slot], stage[:, slot], ACT.Copy).then_inc(tile_hi, 1)

        def root(bank, eps, to=rstd):
            act.activation(to[:, :], ps[:, bank, :], ACT.Sqrt, scale=1.0 / D, bias=eps_col(eps)).then_inc(act_side, 1)

        def eps_col(eps):
            return small[:, 40:41] if eps == RMS_EPS else small[:, 41:42]

        def group(kind, src, g, rhs, dst, fresh, tiles, at=0, stats=False, rows=None, width=S, ahead=True,
                  reprep=None, two_norms=False, early=None, **_):
            if ahead and reprep is None:
                split_tiles(SLOTS, tiles - 1)
            if reprep is not None:
                for m in range(tiles):
                    if m < tiles - 1:
                        split_tiles(SLOTS + m, 1)
                    act.wait_ge(tiles_used, b.at("tiles", m + 1))
                    for c in (2 * m, 2 * m + 1):
                        last = act.activation(h_hi[:, c, :], x[:, c, :], ACT.Copy, scale=column(reprep + c))
                    last.then_inc(part_hi, 1)
            if stats:
                act.wait_ge(pe_side, b.at("pe_side", 1))
                root(4 - 4 * b.parity, RMS_EPS)
            if two_norms:
                act.wait_ge(pe_side, b.at("pe_side", 2))
                root(4 - 4 * b.parity, RMS_EPS, acc)
                act.wait_ge(rstd_ready, b.at("rstd_ready", 3))
                act.activation(rstd[:, :], rstd[:, :], ACT.Sqrt, scale=1.0 / D, bias=eps_col(RMS_EPS)).then_inc(act_side, 1)
            if kind in ("glu", "glu_split"):
                act.wait_ge(psum_read, b.at("psum_read", 1))
                for a in range(2):
                    last = act.activation(t[:, a, :], t[:, a, :], ACT.Sigmoid,
                                          bias=column(VECTORS["conv_pw1_b"] + DC + 2 * at + a))
                last.then_inc(gated, 1)
            if kind == "glu_split":
                act.wait_ge(t_ready, b.at("t_ready", 1))
                act.activation(u_hi[:, :, PAD:PAD + S], t[:, 0:2, :], ACT.Copy).then_inc(part_hi, 1)
            if kind == "gate":
                act.wait_ge(psum_read, b.at("psum_read", 1))
                act.activation(t[:, 0:2, :], t[:, 0:2, :], ACT.Silu).then_inc(gated, 1)
                act.wait_ge(t_ready, b.at("t_ready", 1))
                act.activation(mid_hi[:, 2 * at:2 * at + 2, :], t[:, 2:4, :], ACT.Copy).then_inc(part_hi, 1)
            if kind in ("relu2", "bmul"):
                for a in range(2):
                    act.wait_ge(t_ready, b.at("t_ready", a + 1))
                    act.activation(mid_hi[:, 4 * at + 2 * a:4 * at + 2 * a + 2, :], t[:, 2 * a:2 * a + 2, :],
                                   ACT.Copy).then_inc(part_hi, 1)
            if early:
                _load, exps, norm_last, _turned, _out = attention_steps(early, 4 - 4 * b.parity)
                for i in range(TB):
                    exps(0, i)
                norm_last(0)
            if kind == "proj":
                if src == "mem_wk0":
                    act.wait_ge(keys_out, 64)
                for a, (to, frm) in enumerate(proj_parts(dst, 0, at, width)):
                    act.wait_ge(psum_read, b.at("psum_read", a + 1))
                    act.activation(to, frm, ACT.Copy).then_inc(part_hi, 1)
            if ahead:
                split_tiles(SLOTS + tiles - 1, 1)

        def prologue():
            act.dma_start(xnat[:, :, :], A["x"][0].rearrange("(i p) d -> p i d", p=P)).then_inc(x_in, 16)
            for r, (frm, n) in row_loads[:HALF]:
                act.dma_start(r, frm).then_inc(rows_in, 16)
            act.dma_start(memn[:, :, :], A["mem"][0].rearrange("(i p) d -> p i d", p=P)).then_inc(mem_in, 16)
            split_tiles(0, SLOTS)

        def skew():
            act.wait_ge(g_out, 16)
            act.dma_start(skew_dram.rearrange("h (p n) -> h p n", p=P),
                          bass.AP(g_dram.tensor, 0, [[GCOLS, HEADS], [0, P], [1, GCOLS]])).then_inc(skewed, 16)

        def mem_rows():
            act.wait_ge(step, b.at("step"))
            act.dma_start(g_dram, g_tab[:, :]).then_inc(g_out, 16)
            act.wait_ge(mem_in, 16)
            for i in range(MB):
                act.activation(junk[:, :], memn[:, i, :], ACT.Square, accum_out=small[:, i:i + 1]).then_inc(act_side, 1)
                act.wait_ge(act_side, b.at("act_side", i + 1))
            act.activation(small[:, 2:4], small[:, 0:2], ACT.Sqrt, scale=1.0 / D, bias=eps_col(RMS_EPS)).then_inc(act_side, 1)

        def mem_turn(layer):
            for m in range(4):
                act.wait_ge(pe_side, b.at("pe_side", m + 1))
                for a in range(2):
                    last = act.activation(hm_hi[:, 2 * m + a, :], ps[:, 4 * b.parity + m, a * MEM:(a + 1) * MEM],
                                          ACT.Copy, scale=column(VECTORS["norm_memsrc_g"] + DC * layer + 2 * m + a))
                last.then_inc(part_hi, 1)

        def keys_out_dma():
            act.wait_ge(part_lo, b.at("part_lo"))
            for n, part in enumerate(kv_parts):
                act.dma_start(keys_dram[:, 2 * D * n:2 * D * n + 2 * D], part).then_inc(keys_out, 16)

        def keys_back_dma():
            act.wait_ge(weighed, b.at("weighed"))
            act.wait_ge(keys_out, 64)
            for n, part in enumerate(kv_parts):
                act.dma_start(part, keys_dram[:, 2 * D * n:2 * D * n + 2 * D]).then_inc(keys_back, 16)

        def diag_hi_first():
            taps = vec[:, VECTORS["conv_dw_w"]:VECTORS["conv_dw_w"] + TAPS * DC].rearrange("p (k c) -> p c k", c=DC)
            act.activation(tap_hi[:, :, :], taps[:, 2 * DVE_PAIRS:, :], ACT.Copy).then_inc(tap_parts, 1)
            diagonal_rounds(0, 2)

        def conv_pe():
            diagonal_rounds(2, 2 * len(ROUNDS))

        def diagonal_rounds(first, end):
            w = VECTORS["conv_dw_w"] + 2 * DVE_PAIRS
            for r in range(first, end):
                c, (k, n) = r // len(ROUNDS), ROUNDS[r % len(ROUNDS)]
                if r >= 2:
                    act.wait_ge(diag_used, r - 1)
                for m in range(n):
                    last = act.activation(diag[:, r % 2, 0, m, :], ident[:, :], ACT.Copy,
                                          scale=column(w + DC * (k + m) + c))
                last.then_inc(diag_hi, 1)

        def prep(gain, first, n, split, squares=True, whole=False, last=False, twice=None):
            scale_x = last
            if twice is not None:
                return prep_twice(gain, twice, first, n)
            for m in range(n):
                p = first + m
                if not whole:
                    act.wait_ge(psum_read, b.at("psum_read", m + 1 - n))
                if split:
                    for c in (2 * p, 2 * p + 1):
                        last = act.activation(h_hi[:, c, :], x[:, c, :], ACT.Copy, scale=column(gain + c))
                    last.then_inc(part_hi, 1)
                if squares:
                    if m >= 2:
                        act.wait_ge(step, b.at("step", steps_after(first, m - 1)))
                    a = 2 * (p % 2)
                    act.activation(t[:, a:a + 2, :], x[:, 2 * p:2 * p + 2, :], ACT.Square).then_inc(squared, 1)
                if scale_x:
                    act.wait_ge(squared, b.at("squared", m + 1))
                    for c in (2 * p, 2 * p + 1):
                        last = act.activation(x[:, c, :], x[:, c, :], ACT.Copy, scale=column(gain + c))
                    last.then_inc(part_hi, 1)

        def prep_twice(gain, inner, first, n):
            for m in range(n):
                p = first + m
                pair = x[:, 2 * p:2 * p + 2, :]
                act.wait_ge(psum_read, b.at("psum_read", m + 1 - n))
                if m:
                    act.wait_ge(step, b.at("step", 1 if p == 1 else 2))
                act.activation(t[:, 0:2, :], pair, ACT.Square).then_inc(squared, 1)
                act.wait_ge(squared, b.at("squared", 2 * m + 1))
                for c in (2 * p, 2 * p + 1):
                    last = act.activation(x[:, c, :], x[:, c, :], ACT.Copy, scale=column(inner + c))
                last.then_inc(scaled, 1)
                act.wait_ge(scaled, b.at("scaled", m + 1))
                for c in (2 * p, 2 * p + 1):
                    last = act.activation(h_hi[:, c, :], x[:, c, :], ACT.Copy, scale=column(gain + c))
                last.then_inc(part_hi, 1)
                if m:
                    act.wait_ge(step, b.at("step", 2 if p == 1 else 4))
                act.activation(t[:, 2:4, :], pair, ACT.Square).then_inc(squared, 1)

        def steps_after(first, m):
            return sum(1 if p == 0 else 2 for p in range(first, first + m))

        def prep_all(gain, squares=True):
            act.wait_ge(psum_read, b.at("psum_read"))
            act.wait_ge(step, b.at("step"))
            act.wait_ge(pe_side, b.at("pe_side"))
            prep(gain, 0, 4, True, squares, whole=True)

        def ln_centred():
            for p in range(4):
                act.wait_ge(step, b.at("step", p + 2 if p == 0 else LN_CENTRE + 2 * p - 1))
                act.activation(t[:, 2:4, :], conv[:, 2 * p:2 * p + 2, :], ACT.Square).then_inc(squared, 1)

        def ln_sum():
            act.wait_ge(pe_side, b.at("pe_side", 1))
            root(4 * b.parity + 3, LN_EPS)

        def ln_scaled():
            for p in range(4):
                act.wait_ge(step, b.at("step", p + 1))
                for c in (2 * p, 2 * p + 1):
                    last = act.activation(conv[:, c, :], conv[:, c, :], ACT.Silu,
                                          scale=column(VECTORS["conv_ln_g"] + c), bias=column(VECTORS["conv_ln_b"] + c))
                last.then_inc(gated, 1)
                act.wait_ge(gated, b.at("gated", p + 1))
                act.activation(mid_hi[:, 2 * p:2 * p + 2, :], conv[:, 2 * p:2 * p + 2, :], ACT.Copy).then_inc(part_hi, 1)
                split_tiles(SLOTS + p, 1)

        def gates_split():
            act.wait_ge(gates_in, 32)
            act.wait_ge(step, b.at("step", 1))
            act.activation(wf_hi[:, :, 0:HEADS], wf[:, :, :], ACT.Copy).then_inc(act_side, 1)

        def gates_sum():
            act.wait_ge(step, b.at("step", 1))
            act.activation(f_t[:, 1, :], f_t[:, 0, :], ACT.Abs).then_inc(act_side, 1)
            act.wait_ge(act_side, b.at("act_side", 1))
            act.activation(f_t[:, 1, :], f_t[:, 1, :], ACT.Exp, scale=-1.0).then_inc(act_side, 1)
            act.wait_ge(act_side, b.at("act_side", 2))
            act.activation(f_t[:, 1, :], f_t[:, 1, :], ACT.Ln, bias=1.0).then_inc(act_side, 1)

        def gates_out():
            act.wait_ge(step, b.at("step"))
            act.dma_start(negc_dram, f_t[:, 3, :]).then_inc(negc_out, 16)
            act.wait_ge(negc_out, 16)

        def gates_load():
            act.wait_ge(psum_read, b.at("psum_read"))
            act.dma_start(wf[:, :, :], A["kvf_w"][:, 2 * D:2 * D + HEADS].rearrange("(k p) n -> p k n", p=P)).then_inc(gates_in, 16)
            act.dma_start(small[0:HEADS, 50:51], A["fgate_b"].rearrange("(h a) -> h a", a=1)).then_inc(gates_in, 16)

        def attention_steps(kind, sb):
            ob = 4 - sb
            prob, pt_hi, _pt_lo = buffers(kind)
            offs, widths, keys, pt = attention_shape(kind)
            mem = kind == "mem"
            heads = MEM_HEADS if mem else HEADS
            wid = 2 * S if mem else WID

            def load_table(h):
                if mem or h >= heads:
                    return
                if kind == "fox":
                    src = bass.AP(negc_dram.tensor, h * S, [[0, P], [1, S]])
                else:
                    src = bass.AP(skew_dram.tensor, h * P * GCOLS + P - 1, [[GCOLS - 1, P], [1, S]])
                act.dma_start(t[:, h % 2, :], src).then_inc(table_in[h % 2], 16)

            def exps(h, i):
                act.wait_ge(maxed, b.at("maxed", TB * h + i + 1))
                n = 4 * (h % 2) + i
                row = prob[h % 2][:, offs[i]:offs[i] + widths[i]]
                if mem and i == 0 and h >= 2:
                    act.wait_ge(turned, b.at("turned", h - 1))
                act.activation(row, ps[:, sb + i, 0:widths[i]] if mem else row, ACT.Exp, bias=small[:, 8 + n:9 + n],
                               accum_out=small[:, 16 + n:17 + n]).then_inc(expd, 1)

            def norm_last(h):
                i, n = TB - 1, 4 * (h % 2) + TB - 1
                row = prob[h % 2][:, offs[i]:offs[i] + widths[i]]
                act.wait_ge(summed, b.at("summed", TB * (h + 1)))
                act.activation(row, row, ACT.Copy, scale=small[:, 24 + n:25 + n]).then_inc(normed_last, 1)

            def turned_parts(h):
                act.wait_ge(turned, b.at("turned", h + 1))
                if h >= 2:
                    act.wait_ge(weighed, b.at("weighed", h - 1))
                act.activation(pt_hi[h % 2][:, 0:wid], flat(ps[:, ob:ob + 3, :], wid), ACT.Copy).then_inc(turned_hi, 1)

            def out_parts(h):
                act.wait_ge(weighed, b.at("weighed", h + 1))
                to, frm = out_of(kind, h, q_hi, ob)
                act.activation(to, frm, ACT.Copy).then_inc(out_hi, 1)

            return load_table, exps, norm_last, turned_parts, out_parts

        def attend(kind):
            load_table, exps, norm_last, turned_parts, out_parts = attention_steps(kind, 4 * b.parity)
            heads = MEM_HEADS if kind == "mem" else HEADS
            act.wait_ge(part_lo, b.at("part_lo"))
            if kind == "dil":
                act.wait_ge(skewed, 16)
            load_table(0)
            load_table(1)
            for h in range(heads + 2):
                now = h < heads and (h > 0 or kind != "mem")
                if now:
                    exps(h, 0)
                    exps(h, 1)
                if 1 <= h <= heads:
                    turned_parts(h - 1)
                if now:
                    exps(h, 2)
                    exps(h, 3)
                    load_table(h + 2)
                if h >= 2:
                    out_parts(h - 2)
                if now:
                    norm_last(h)

        def output():
            act.wait_ge(pe_side, b.at("pe_side", 2 * TB))
            act.activation(small[:, 4:8], ps[:, 2 * TB - 1, 0:TB], ACT.Sqrt, scale=1.0 / D,
                           bias=eps_col(RMS_EPS)).then_inc(act_side, 1)
            act.wait_ge(rstd_ready, b.at("rstd_ready", 1))
            for i in range(TB):
                act.wait_ge(pe_side, b.at("pe_side", TB + i + 1 if i < TB - 1 else 2 * TB + 1))
                act.activation(xnat[:, i, S:2 * S], ps[:, 2 * i + 1, :], ACT.Copy, scale=small[:, 4 + i:5 + i]).then_inc(gated, 1)

        schedule(b, dict(prologue=prologue, group=group, mem_rows=mem_rows, mem_turn=mem_turn, prep=prep,
                         prep_all=prep_all, skew=skew, diag_hi_first=diag_hi_first, ln_sum=ln_sum, keys_out=keys_out_dma, keys_back=keys_back_dma, conv_pe=conv_pe,
                         ln_centred=ln_centred, ln_scaled=ln_scaled, gates_split=gates_split, gates_sum=gates_sum,
                         gates_out=gates_out, gates_load=gates_load,
                         attend=attend, output=output))

    @block.vector
    def _(dve):
        b = Book(dve)
        rstd2 = rstd[:, :].unsqueeze(1).broadcast_to([P, 2, S])

        def lo_of(to, value, hi):
            return dve.tensor_tensor(to, value, hi.bitcast(F32), ALU.subtract)

        def lo_of_h(gain, pair):
            for c in (2 * pair, 2 * pair + 1):
                last = dve.scalar_tensor_tensor(out=h_lo[:, c, :], in0=x[:, c, :], scalar=column(gain + c),
                                                in1=h_hi[:, c, :].bitcast(F32), op0=ALU.mult, op1=ALU.subtract)
            return last

        def settle():
            dve.wait_ge(psum_read, b.at("psum_read"))
            dve.wait_ge(t_ready, b.at("t_ready"))
            dve.wait_ge(part_lo, b.at("part_lo"))
            dve.wait_ge(step, b.at("step"))

        def group(kind, src, g, rhs, dst, fresh, tiles, at=0, stats=False, rows=None, width=S, scale=None,
                  bias=None, columns=False, reprep=None, two_norms=False, early=None, **_):
            base = 4 * b.parity
            before = 0
            if reprep is not None:
                before = tiles
                for m in range(tiles):
                    dve.wait_ge(part_hi, b.at("part_hi", m + 1))
                    lo_of_h(reprep, m).then_inc(part_lo, 1)
            if early:
                _shift, peak, over_sum, _turned, _out = attention_steps(early, 4 - base)
                for i in range(TB):
                    peak(0, i)
                for i in range(TB):
                    over_sum(0, i)
            if columns:
                dve.wait_ge(pe_side, b.at("pe_side", 1))
                dve.tensor_copy(small[:, 4:8], ps[:, 4 - base, :].rearrange("p (i s) -> p i s", i=TB)[:, :, 0]
                                ).then_inc(step, 1)
            if stats:
                dve.wait_ge(act_side, b.at("act_side", 1))
                dve.reciprocal(rstd[:, :], rstd[:, :]).then_inc(rstd_ready, 1)
            if two_norms:
                dve.wait_ge(act_side, b.at("act_side", 1))
                dve.reciprocal(acc[:, :], acc[:, :]).then_inc(rstd_ready, 1)
                dve.wait_ge(rstd_ready, b.at("rstd_ready", 1))
                dve.tensor_tensor(rstd[:, :], ps[:, 5 - base, :], acc[:, :], ALU.mult).then_inc(rstd_ready, 1)
                dve.wait_ge(rstd_ready, b.at("rstd_ready", 2))
                dve.tensor_tensor(rstd[:, :], rstd[:, :], acc[:, :], ALU.mult).then_inc(rstd_ready, 1)
                dve.wait_ge(act_side, b.at("act_side", 2))
                dve.reciprocal(rstd[:, :], rstd[:, :]).then_inc(rstd_ready, 1)
                dve.wait_ge(rstd_ready, b.at("rstd_ready", 4))
                dve.tensor_tensor(rstd[:, :], rstd[:, :], acc[:, :], ALU.mult).then_inc(rstd_ready, 1)
            dve.wait_ge(rstd_ready, b.at("rstd_ready", 5 if two_norms else 1 if stats else 0))
            settle()
            dve.wait_ge(tiles_used, b.at("tiles", tiles))
            for a in range(2):
                bank, here = ps[:, base + 2 * a:base + 2 * a + 2, :], t[:, 2 * a:2 * a + 2, :]
                if kind == "add":
                    cs = range(4 * at + 2 * a, 4 * at + 2 * a + 2)
                    if bias:
                        for c in cs:
                            last = dve.scalar_tensor_tensor(out=x[:, c, :], in0=ps[:, base + c - 4 * at, :],
                                                            scalar=column(VECTORS[bias] + c), in1=x[:, c, :],
                                                            op0=ALU.add, op1=ALU.add)
                    else:
                        last = dve.tensor_tensor(x[:, cs[0]:cs[1] + 1, :], bank, x[:, cs[0]:cs[1] + 1, :], ALU.add)
                elif dst in ("km", "vm"):
                    if dst == "km":
                        last = dve.tensor_copy(t[:, 2 * a:2 * a + 2, 0:width], ps[:, base + 2 * a:base + 2 * a + 2, 0:width])
                    else:
                        last = dve.tensor_copy(t[:, a, :], ps[:, base + a, :])
                elif rows:
                    dve.wait_ge(step, b.at("step"))
                    for i in (2 * a, 2 * a + 1):
                        last = dve.tensor_scalar(t[:, i, :], ps[:, base + i, :], small[:, 4 + i:5 + i], None, ALU.mult)
                elif scale:
                    last = dve.scalar_tensor_tensor(out=here, in0=bank, scalar=scale, in1=rstd2, op0=ALU.mult,
                                                    op1=ALU.mult)
                else:
                    last = dve.tensor_tensor(here, bank, rstd2, ALU.mult)
                last.then_inc(psum_read, 1)
            if kind in ("glu", "glu_split"):
                dve.wait_ge(psum_read, b.at("psum_read", 2))
                dve.wait_ge(gated, b.at("gated", 1))
                for a in range(2):
                    c = 2 * at + a
                    to = u_pad[:, c, PAD:PAD + S] if kind == "glu" else t[:, a, :]
                    last = dve.scalar_tensor_tensor(out=to, in0=t[:, 2 + a, :], in1=t[:, a, :],
                                                    scalar=column(VECTORS["conv_pw1_b"] + c), op0=ALU.add, op1=ALU.mult)
                last.then_inc(t_ready, 1)
            if kind == "glu_split":
                dve.wait_ge(part_hi, b.at("part_hi", 1))
                lo_of(u_lo[:, :, PAD:PAD + S], t[:, 0:2, :], u_hi[:, :, PAD:PAD + S]).then_inc(part_lo, 1)
            if kind == "gate":
                dve.wait_ge(psum_read, b.at("psum_read", 2))
                dve.wait_ge(gated, b.at("gated", 1))
                dve.tensor_tensor(t[:, 2:4, :], t[:, 0:2, :], t[:, 2:4, :], ALU.mult).then_inc(t_ready, 1)
                dve.wait_ge(part_hi, b.at("part_hi", 1))
                cs = slice(2 * at, 2 * at + 2)
                lo_of(mid_lo[:, cs, :], t[:, 2:4, :], mid_hi[:, cs, :]).then_inc(part_lo, 1)
            if kind in ("relu2", "bmul"):
                for a in range(2):
                    here, cs = t[:, 2 * a:2 * a + 2, :], slice(4 * at + 2 * a, 4 * at + 2 * a + 2)
                    dve.wait_ge(psum_read, b.at("psum_read", a + 1))
                    if kind == "relu2":
                        last = dve.scalar_tensor_tensor(out=here, in0=here, scalar=0.0, in1=here, op0=ALU.max,
                                                        op1=ALU.mult)
                    else:
                        last = dve.tensor_tensor(here, here, y2[:, cs, :], ALU.mult)
                    last.then_inc(t_ready, 1)
                for a in range(2):
                    here, cs = t[:, 2 * a:2 * a + 2, :], slice(4 * at + 2 * a, 4 * at + 2 * a + 2)
                    dve.wait_ge(part_hi, b.at("part_hi", a + 1))
                    lo_of(mid_lo[:, cs, :], here, mid_hi[:, cs, :]).then_inc(part_lo, 1)
            if kind == "proj":
                for a, ((to, frm), (hi, _f)) in enumerate(zip(proj_parts(dst, 1, at, width), proj_parts(dst, 0, at, width))):
                    dve.wait_ge(part_hi, b.at("part_hi", before + a + 1))
                    lo_of(to, frm, hi).then_inc(part_lo, 1)
            if kind == "cu":
                dve.wait_ge(psum_read, b.at("psum_read", 2))
                if at == 0:
                    dve.memset(z_pad[:, :, 0:2], 0.0)
                dve.tensor_tensor(z_pad[:, :, 2:2 + S], t[:, 0:2, :], t[:, 2:4, :], ALU.mult).then_inc(step, 1)
                for k in range(3):
                    dve.wait_ge(step, b.at("step", k + 1))
                    for a in range(2):
                        c = 2 * at + a
                        w = column(VECTORS["conv_kernel_2"] + DC * k + c)
                        if k == 0:
                            last = dve.tensor_scalar(y2[:, c, :], z_pad[:, a, 0:S], w, None, ALU.mult)
                        else:
                            last = dve.scalar_tensor_tensor(out=y2[:, c, :], in0=z_pad[:, a, k:k + S], scalar=w,
                                                            in1=y2[:, c, :], op0=ALU.mult, op1=ALU.add)
                    last.then_inc(step, 1)

        def prologue():
            dve.memset(small[:, 40:41], RMS_EPS)
            dve.memset(small[:, 41:42], LN_EPS)
            dve.wait_ge(pe_side, 1)
            dve.tensor_copy(vec[:, :], ps[:, 0, 0:n_rows]).then_inc(step, 1)
            dve.wait_ge(pe_side, 2)
            dve.wait_ge(rows_in, ROWS_IN)
            dve.tensor_tensor(g_tab[:, :], flat(ps[0:HEADS, 1:3, :], GCOLS), g_log[:, :], ALU.add).then_inc(step, 1)
            for p in range(4):
                dve.wait_ge(pe_side, 2 + 2 * p + 2)
                dve.tensor_copy(x[:, 2 * p:2 * p + 2, :], ps[:, 2 * p:2 * p + 2, :]).then_inc(psum_read, 1)
            dve.memset(u_hi[:, :, 0:PAD].bitcast(F32), 0.0)
            dve.memset(u_lo[:, :, 0:PAD].bitcast(F32), 0.0)
            dve.memset(u_pad[:, :, 0:PAD], 0.0).then_inc(step, 1)

        def mem_rows():
            dve.wait_ge(act_side, b.at("act_side", 3))
            dve.reciprocal(small[:, 2:4], small[:, 2:4]).then_inc(step, 1)
            dve.wait_ge(step, b.at("step", 1))
            for i in range(MB):
                dve.tensor_scalar(memn[:, i, :], memn[:, i, :], small[:, 2 + i:3 + i], None, ALU.mult).then_inc(step, 1)

        def mem_turn(layer):
            for m in range(4):
                dve.wait_ge(part_hi, b.at("part_hi", m + 1))
                for a in range(2):
                    c = 2 * m + a
                    last = dve.scalar_tensor_tensor(
                        out=hm_lo[:, c, :], in0=ps[:, 4 * b.parity + m, a * MEM:(a + 1) * MEM],
                        scalar=column(VECTORS["norm_memsrc_g"] + DC * layer + c), in1=hm_hi[:, c, :].bitcast(F32),
                        op0=ALU.mult, op1=ALU.subtract)
                last.then_inc(part_lo, 1)

        def take(p, a, done, to=acc):
            if p == 0:
                dve.tensor_tensor(to[:, :], t[:, a, :], t[:, a + 1, :], ALU.add).then_inc(step, 1)
                return done + 1
            dve.tensor_tensor(t[:, a, :], t[:, a, :], t[:, a + 1, :], ALU.add).then_inc(step, 1)
            dve.wait_ge(step, b.at("step", done + 1))
            dve.tensor_tensor(to[:, :], to[:, :], t[:, a, :], ALU.add).then_inc(step, 1)
            return done + 2

        def prep(gain, first, n, split, squares=True, whole=False, last=False, twice=None):
            done = 0
            if twice is not None:
                for m in range(n):
                    p = first + m
                    dve.wait_ge(squared, b.at("squared", 2 * m + 1))
                    done = take(p, 0, done)
                    dve.wait_ge(part_hi, b.at("part_hi", m + 1))
                    lo_of_h(gain, p).then_inc(part_lo, 1)
                    dve.wait_ge(squared, b.at("squared", 2 * m + 2))
                    done = take(p, 2, done, rstd)
                return
            for m in range(n):
                p = first + m
                if not whole:
                    dve.wait_ge(psum_read, b.at("psum_read", m + 1 - n))
                if split:
                    dve.wait_ge(part_hi, b.at("part_hi", m + 1))
                    lo_of_h(gain, p).then_inc(part_lo, 1)
                if squares:
                    dve.wait_ge(squared, b.at("squared", m + 1))
                    done = take(p, 2 * (p % 2), done)

        def prep_all(gain, squares=True):
            dve.wait_ge(psum_read, b.at("psum_read"))
            dve.wait_ge(step, b.at("step"))
            prep(gain, 0, 4, True, squares, whole=True)

        def conv_taps(pair, first, n):
            cs = (2 * pair, 2 * pair + 1)
            w = VECTORS["conv_dw_w"]
            if first == 0:
                dve.wait_ge(t_ready, b.at("t_ready"))
                dve.wait_ge(pe_side, b.at("pe_side"))
                for c in cs:
                    dve.tensor_scalar(conv[:, c, :], u_pad[:, c, 0:S], column(w + c), column(VECTORS["conv_dw_b"] + c),
                                      ALU.mult, ALU.add).then_inc(step, 1)
                n -= 1
                first = 1
                now = b.at("step", 2)
            else:
                now = b.at("step")
            if n == 0:
                return
            with dve.Fori(first, first + n) as k:
                for a, c in enumerate(cs):
                    dve.wait_ge(step, k * 2 + (now + a - 1 - 2 * first))
                    dve.scalar_tensor_tensor(out=conv[:, c, :], in0=u_pad[:, c, bass.ds(k, S)],
                                             scalar=vec[:, bass.ds(k * DC + (w + c), 1)], in1=conv[:, c, :],
                                             op0=ALU.mult, op1=ALU.add).then_inc(step, 1)

        def conv_pe():
            dve.wait_ge(diag_used, 2 * len(ROUNDS))
            for a in range(2):
                c = 2 * DVE_PAIRS + a
                dve.tensor_scalar(conv[:, c, :], ps[:, 4 * b.parity + a, :], column(VECTORS["conv_dw_b"] + c), None,
                                  ALU.add).then_inc(psum_read, 1)

        def ln_centred():
            dve.wait_ge(psum_read, b.at("psum_read"))
            dve.wait_ge(part_lo, b.at("part_lo"))
            dve.wait_ge(step, b.at("step"))
            dve.wait_ge(pe_side, b.at("pe_side", 1))
            dve.tensor_scalar(t[:, 0, :], ps[:, 4 * b.parity + 3, :], 1.0 / D, None, ALU.mult).then_inc(step, 1)
            dve.wait_ge(step, b.at("step", 1))
            mean2 = t[:, 0, :].unsqueeze(1).broadcast_to([P, 2, S])
            for p in range(4):
                c = conv[:, 2 * p:2 * p + 2, :]
                dve.tensor_tensor(c, c, mean2, ALU.subtract).then_inc(step, 1)
            done = LN_CENTRE
            for p in range(4):
                dve.wait_ge(squared, b.at("squared", p + 1))
                done = take(p, 2, done)

        def ln_scaled():
            dve.wait_ge(act_side, b.at("act_side"))
            dve.reciprocal(rstd[:, :], rstd[:, :]).then_inc(rstd_ready, 1)
            dve.wait_ge(rstd_ready, b.at("rstd_ready", 1))
            for p in range(4):
                c = conv[:, 2 * p:2 * p + 2, :]
                dve.tensor_tensor(c, c, rstd2, ALU.mult).then_inc(step, 1)
            for p in range(4):
                cs = slice(2 * p, 2 * p + 2)
                dve.wait_ge(part_hi, b.at("part_hi", p + 1))
                lo_of(mid_lo[:, cs, :], conv[:, cs, :], mid_hi[:, cs, :]).then_inc(part_lo, 1)

        def gates_split():
            dve.wait_ge(psum_read, b.at("psum_read"))
            dve.memset(wf_hi[:, :, :].bitcast(F32), 0.0)
            dve.memset(wf_lo[:, :, :].bitcast(F32), 0.0).then_inc(step, 1)
            dve.wait_ge(act_side, b.at("act_side", 1))
            lo_of(wf_lo[:, :, 0:HEADS], wf[:, :, :], wf_hi[:, :, 0:HEADS]).then_inc(step, 1)

        def gates():
            dve.wait_ge(pe_side, b.at("pe_side", 1))
            for a in range(2):
                half = slice(a * S // 2, (a + 1) * S // 2)
                dve.tensor_tensor(f_t[:, 0, half], ps[0:HEADS, 4 * b.parity, half], rstd[0:HEADS, half],
                                  ALU.mult).then_inc(psum_read, 1)

        def gates_sum():
            dve.wait_ge(psum_read, b.at("psum_read"))
            dve.wait_ge(gates_in, 32)
            dve.tensor_scalar(f_t[:, 0, :], f_t[:, 0, :], small[0:HEADS, 50:51], None, ALU.add).then_inc(step, 1)
            dve.wait_ge(step, b.at("step", 1))
            dve.tensor_scalar(f_t[:, 2, :], f_t[:, 0, :], -1.0, 0.0, ALU.mult, ALU.max).then_inc(step, 1)
            dve.wait_ge(act_side, b.at("act_side", 3))
            dve.wait_ge(step, b.at("step", 2))
            dve.tensor_tensor_scan(f_t[:, 3, :], f_t[:, 1, :], f_t[:, 2, :], initial=0.0, op0=ALU.add,
                                   op1=ALU.add).then_inc(step, 1)

        def scale_x():
            dve.wait_ge(psum_read, b.at("psum_read"))
            for p in range(4):
                pair = x[:, 2 * p:2 * p + 2, :]
                dve.tensor_tensor(pair, pair, acc[:, :].unsqueeze(1).broadcast_to([P, 2, S]), ALU.mult).then_inc(step, 1)

        def attention_steps(kind, sb):
            ob = 4 - sb
            prob, pt_hi, pt_lo = buffers(kind)
            offs, widths, keys, pt = attention_shape(kind)
            mem = kind == "mem"
            heads = MEM_HEADS if mem else HEADS
            wid = 2 * S if mem else WID

            def shift(h, i):
                if mem:
                    return
                row, w = prob[h % 2][:, offs[i]:offs[i] + widths[i]], widths[i]
                if i == 0:
                    if h >= 2:
                        dve.wait_ge(turned, b.at("turned", h - 1))
                    dve.wait_ge(table_in[h % 2], 16 * (b.count.get("tables", 0) + h // 2 + 1))
                dve.wait_ge(scored, b.at("scored", TB * h + i + 1))
                table = t[:, h % 2, S - w:S] if kind == "dil" else t[:, h % 2, 0:w]
                dve.tensor_tensor(row, ps[:, sb + i, 0:w], table, ALU.add).then_inc(shifted, 1)

            def peak(h, i):
                n = 4 * (h % 2) + i
                if mem:
                    dve.wait_ge(scored, b.at("scored", TB * h + i + 1))
                else:
                    dve.wait_ge(shifted, b.at("shifted", TB * h + i + 1))
                row = ps[:, sb + i, 0:widths[i]] if mem else prob[h % 2][:, offs[i]:offs[i] + widths[i]]
                dve.reduce_max(small[:, 8 + n:9 + n], row, AX_X, negate=True).then_inc(maxed, 1)

            def over_sum(h, i):
                n = 4 * (h % 2) + i
                dve.wait_ge(expd, b.at("expd", TB * h + i + 1))
                dve.reciprocal(small[:, 24 + n:25 + n], small[:, 16 + n:17 + n]).then_inc(summed, 1)

            def turned_parts(h):
                dve.wait_ge(turned_hi, b.at("turned_hi", h + 1))
                lo_of(pt_lo[h % 2][:, 0:wid], flat(ps[:, ob:ob + 3, :], wid), pt_hi[h % 2][:, 0:wid]).then_inc(turned_lo, 1)

            def out_parts(h):
                dve.wait_ge(out_hi, b.at("out_hi", h + 1))
                to, frm = out_of(kind, h, q_lo, ob)
                lo_of(to, frm, out_of(kind, h, q_hi, ob)[0]).then_inc(out_lo, 1)

            return shift, peak, over_sum, turned_parts, out_parts

        def attend(kind):
            shift, peak, over_sum, turned_parts, out_parts = attention_steps(kind, 4 * b.parity)
            heads = MEM_HEADS if kind == "mem" else HEADS
            for h in range(heads + 2):
                now = h < heads and (h > 0 or kind != "mem")
                if now:
                    shift(h, 0)
                    shift(h, 1)
                    peak(h, 0)
                    shift(h, 2)
                    peak(h, 1)
                    over_sum(h, 0)
                    shift(h, 3)
                    peak(h, 2)
                    over_sum(h, 1)
                    peak(h, 3)
                if 1 <= h <= heads:
                    turned_parts(h - 1)
                if now:
                    over_sum(h, 2)
                    over_sum(h, 3)
                if h >= 2:
                    out_parts(h - 2)

        def output():
            dve.wait_ge(act_side, b.at("act_side", 1))
            dve.reciprocal(small[:, 4:8], small[:, 4:8]).then_inc(rstd_ready, 1)
            dve.wait_ge(rstd_ready, b.at("rstd_ready", 1))
            for i in range(TB):
                dve.wait_ge(pe_side, b.at("pe_side", i + 1))
                dve.tensor_scalar(xnat[:, i, 0:S], ps[:, 2 * i, :], small[:, 4 + i:5 + i], None, ALU.mult).then_inc(t_ready, 1)

        schedule(b, dict(prologue=prologue, group=group, mem_turn=mem_turn, prep=prep, prep_all=prep_all,
                         mem_rows=mem_rows, conv=conv_taps, conv_pe=conv_pe, ln_centred=ln_centred,
                         ln_scaled=ln_scaled, gates_split=gates_split, gates=gates, gates_sum=gates_sum,
                         scale_x=scale_x, attend=attend, output=output))


INPUTS = ["x", "mem", "norm_mix_g", "norm_mem_g", "norm_memsrc_g", "norm_ff_g", "mem_wq", "mem_wk", "mem_wv",
          "mem_wo", "ff_w1", "ff_w2", "conv_pw1_w", "conv_pw1_b", "conv_dw_w", "conv_dw_b", "conv_ln_g",
          "conv_ln_b", "conv_pw2_w", "conv_pw2_b", "kv_norm_g", "kvf_w", "fgate_b", "fox_wq", "fox_wo",
          "final_norm_g", "mix_norm_2", "ffn_norm_2", "final_norm_2", "conv_w_in_2", "conv_kernel_2",
          "conv_w_out_2", "attn_w_qkv_2", "attn_w_out_2", "rel_bias_2", "ffn_w_gate_2", "ffn_w_up_2",
          "ffn_w_down_2"]


def kernel(**inputs):
    import concourse.bacc as bacc
    from concourse.bass_utils import run_bass_kernel_spmd

    nc = bacc.Bacc("TRN2", target_bir_lowering=False, num_devices=1)
    arrays, aps = {}, {}
    for name in INPUTS:
        a = np.ascontiguousarray(inputs[name])
        arrays[f"in_{name}"] = a
        aps[name] = nc.dram_tensor(f"in_{name}", a.shape, mybir.dt.from_np(a.dtype), kind="ExternalInput").ap()
    out = nc.dram_tensor("out", (1, S, D), F32, kind="ExternalOutput").ap()
    build(nc, aps, out)
    r = run_bass_kernel_spmd(nc, [arrays], core_ids=[0])
    return r.results[0]["out"]
```
